# Optimizing a Trainium2 kernel written in Bass

```python
import math
import jax, jax.numpy as jnp
from jax import lax
import numpy as np
import jax
import jax.numpy as jnp

D_MODEL = 1024
BATCH = 1
SEQ = 256
DEPTH = 2

MLSTM_INNER = 2 * D_MODEL
MLSTM_HEADS = 4
MLSTM_HEAD_DIM = MLSTM_INNER // MLSTM_HEADS
MLSTM_CONV = 4
QKV_BLOCK = 4
MLSTM_CHUNK = 128
S5_GROUP = 16
S5_GROUPS = D_MODEL // S5_GROUP
S5_STATE = 64
S5_CHUNK = 128
DT_MIN = 0.001
DT_MAX = 0.1
D_FF = 2816
N_EXPERTS = 8
TOP_K = 2
N_EVEN = (DEPTH + 1) // 2
N_ODD = DEPTH // 2
DEEPNORM_ALPHA = (2 * DEPTH) ** 0.25
DEEPNORM_BETA = (8 * DEPTH) ** -0.25
LN_EPS = 1e-5


def layer_norm(x, g, b):
    xf = x.astype(jnp.float32)
    mu = jnp.mean(xf, -1, keepdims=True)
    var = jnp.mean(jnp.square(xf - mu), -1, keepdims=True)
    return ((xf - mu) * lax.rsqrt(var + LN_EPS) * g.astype(jnp.float32) + b.astype(jnp.float32)).astype(x.dtype)

def causal_depthwise_conv(x, w, b):
    K, C = w.shape
    y = lax.conv_general_dilated(x, w[:, None, :].astype(x.dtype), window_strides=(1,), padding=[(K - 1, 0)],
                                 dimension_numbers=('NWC', 'WIO', 'NWC'), feature_group_count=C)
    return y + b

def block_diag_proj(x, w):
    nb, blk, _ = w.shape
    xb = x.reshape(x.shape[:-1] + (nb, blk))
    return jnp.einsum('bsni,nio->bsno', xb, w).reshape(x.shape)

def swiglu(x, w13, w2):
    gate, up = jnp.split(x @ w13, 2, axis=-1)
    return (jax.nn.silu(gate) * up) @ w2

def mlstm_chunkwise(q, k, v, log_i, log_f):
    Bsz, NH, S, DH = q.shape
    L = MLSTM_CHUNK
    NC = S // L

    def chunks(t):
        return jnp.moveaxis(t.reshape((Bsz, NH, NC, L) + t.shape[3:]), 2, 0)

    causal = jnp.tril(jnp.ones((L, L), dtype=bool))

    def step(carry, inp):
        C, n, m = carry
        qc, kc, vc, ic, fc = inp
        b = jnp.cumsum(fc, axis=-1)
        d_log = jnp.where(causal, b[..., :, None] - b[..., None, :] + ic[..., None, :], -jnp.inf)
        inter = b + m[..., None]
        m_t = jnp.maximum(inter, jnp.max(d_log, axis=-1))
        scores = jnp.einsum('bhtd,bhsd->bhts', qc, kc) * jnp.exp(d_log - m_t[..., None])
        dec = jnp.exp(inter - m_t)
        num = jnp.einsum('bhts,bhse->bhte', scores, vc) + dec[..., None] * jnp.einsum('bhtd,bhde->bhte', qc, C)
        den = jnp.sum(scores, -1) + dec * jnp.einsum('bhtd,bhd->bht', qc, n)
        h = num / jnp.maximum(jnp.abs(den), jnp.exp(-m_t))[..., None]
        b_last = b[..., -1]
        g = b_last[..., None] - b + ic
        m_new = jnp.maximum(b_last + m, jnp.max(g, axis=-1))
        wk = jnp.exp(g - m_new[..., None])[..., None] * kc
        dC = jnp.exp(b_last + m - m_new)
        C_new = dC[..., None, None] * C + jnp.einsum('bhsd,bhse->bhde', wk, vc)
        n_new = dC[..., None] * n + jnp.sum(wk, axis=2)
        return (C_new, n_new, m_new), h

    init = (jnp.zeros((Bsz, NH, DH, DH), jnp.float32), jnp.zeros((Bsz, NH, DH), jnp.float32),
            jnp.zeros((Bsz, NH), jnp.float32))
    _, h = lax.scan(step, init, (chunks(q), chunks(k), chunks(v), chunks(log_i), chunks(log_f)))
    return jnp.moveaxis(h, 0, 2).reshape(Bsz, NH, S, DH)

def mlstm_mixer(u, w_in, conv_w, conv_b, wq, wk, wv, w_gates, b_gates, norm_w, skip, w_out):
    Bsz, S, _ = u.shape
    xm, z = jnp.split(u @ w_in, 2, axis=-1)
    xc = jax.nn.silu(causal_depthwise_conv(xm, conv_w, conv_b))
    q = block_diag_proj(xc, wq)
    k = block_diag_proj(xc, wk)
    v = block_diag_proj(xm, wv)
    wg_q, wg_k, wg_v = jnp.split(w_gates, 3, axis=0)
    gates = (q @ wg_q + k @ wg_k + v @ wg_v + b_gates).astype(jnp.float32)
    i_pre, f_pre = jnp.split(gates, 2, axis=-1)
    log_f = jax.nn.log_sigmoid(f_pre)

    def heads(t):
        return t.reshape(Bsz, S, MLSTM_HEADS, MLSTM_HEAD_DIM).transpose(0, 2, 1, 3).astype(jnp.float32)

    h = mlstm_chunkwise(heads(q) * (MLSTM_HEAD_DIM ** -0.5), heads(k), heads(v),
                        i_pre.transpose(0, 2, 1), log_f.transpose(0, 2, 1))
    mu = jnp.mean(h, -1, keepdims=True)
    var = jnp.mean(jnp.square(h - mu), -1, keepdims=True)
    h = ((h - mu) * lax.rsqrt(var + LN_EPS)).transpose(0, 2, 1, 3).reshape(Bsz, S, MLSTM_INNER).astype(u.dtype)
    h = (h * norm_w + skip * xc) * jax.nn.silu(z)
    return h @ w_out

def _complex_affine_combine(e1, e2):
    a1r, a1i, b1r, b1i = e1
    a2r, a2i, b2r, b2i = e2
    return (a2r * a1r - a2i * a1i, a2r * a1i + a2i * a1r,
            a2r * b1r - a2i * b1i + b2r, a2r * b1i + a2i * b1r + b2i)

def s5_mixer(u, lam_re, lam_im, b_re, b_im, c_re, c_im, d_skip, log_dt, w_glu, b_glu):
    Bsz, S, _ = u.shape
    G, P, H = b_re.shape
    L = S5_CHUNK
    NC = S // L
    f32 = lambda t: t.astype(jnp.float32)
    lr, li = f32(lam_re), f32(lam_im)
    dt = jnp.exp(f32(log_dt))[:, None]
    mag = jnp.exp(lr * dt)
    ar, ai = mag * jnp.cos(li * dt), mag * jnp.sin(li * dt)
    den = lr * lr + li * li
    kr = ((ar - 1.0) * lr + ai * li) / den
    ki = (ai * lr - (ar - 1.0) * li) / den
    br, bi = f32(b_re), f32(b_im)
    bbar_re = kr[..., None] * br - ki[..., None] * bi
    bbar_im = kr[..., None] * bi + ki[..., None] * br
    cr, ci = f32(c_re), f32(c_im)
    steps = jnp.arange(1, L + 1, dtype=jnp.float32)[:, None, None]
    pmag = jnp.exp(steps * lr * dt)
    pr = (pmag * jnp.cos(steps * li * dt))[:, None]
    pi_ = (pmag * jnp.sin(steps * li * dt))[:, None]
    uf = f32(u).reshape(Bsz, NC, L, G, H).transpose(1, 2, 0, 3, 4)

    def step(carry, uc):
        xr0, xi0 = carry
        bur = jnp.einsum('lbgh,gph->lbgp', uc, bbar_re)
        bui = jnp.einsum('lbgh,gph->lbgp', uc, bbar_im)
        a_r = jnp.broadcast_to(ar, bur.shape)
        a_i = jnp.broadcast_to(ai, bur.shape)
        _, _, sr, si = lax.associative_scan(_complex_affine_combine, (a_r, a_i, bur, bui), axis=0)
        xr = pr * xr0 - pi_ * xi0 + sr
        xi = pr * xi0 + pi_ * xr0 + si
        y = jnp.einsum('ghp,lbgp->lbgh', cr, xr) - jnp.einsum('ghp,lbgp->lbgh', ci, xi)
        return (xr[-1], xi[-1]), y

    init = (jnp.zeros((Bsz, G, P), jnp.float32), jnp.zeros((Bsz, G, P), jnp.float32))
    _, y = lax.scan(step, init, uf)
    y = y.transpose(2, 0, 1, 3, 4).reshape(Bsz, S, G * H) + f32(d_skip) * f32(u)
    g = jax.nn.gelu(y).astype(u.dtype)
    val, gate = jnp.split(g @ w_glu + b_glu, 2, axis=-1)
    return val * jax.nn.sigmoid(gate)

def moe_ffn(u, w_router, w13, w2):
    Bsz, S, D = u.shape
    t = u.reshape(-1, D)
    logits = (t @ w_router).astype(jnp.float32)
    top_val, top_idx = lax.top_k(logits, TOP_K)
    top_w = jax.nn.softmax(top_val, axis=-1)
    out = jnp.zeros_like(t)
    for e in range(N_EXPERTS):
        gate_e = jnp.sum(jnp.where(top_idx == e, top_w, 0.0), axis=-1).astype(t.dtype)
        out = out + gate_e[:, None] * swiglu(t, w13[e], w2[e])
    return out.reshape(Bsz, S, D)

def first_inputs(seed: int = 0) -> dict:
    key = jax.random.key(seed)
    ks = iter(jax.random.split(key, 40))
    f32 = jnp.float32

    def nrm(shape, std):
        return std * jax.random.normal(next(ks), shape, f32)

    D, Di, NH, G, P, H, F, E = D_MODEL, MLSTM_INNER, MLSTM_HEADS, S5_GROUPS, S5_STATE, S5_GROUP, D_FF, N_EXPERTS
    beta = DEEPNORM_BETA
    x = nrm((BATCH, SEQ, D), 1.0)
    c = nrm((BATCH, D), 1.0)
    ada_w = nrm((DEPTH, D, 6 * D), 0.2 * D ** -0.5)
    ada_b = nrm((DEPTH, 6 * D), 0.01)
    ln_mix_g = 1.0 + nrm((DEPTH, D), 0.01)
    ln_mix_b = nrm((DEPTH, D), 0.01)
    ln_ffn_g = 1.0 + nrm((DEPTH, D), 0.01)
    ln_ffn_b = nrm((DEPTH, D), 0.01)
    mlstm_w_in = nrm((N_EVEN, D, 2 * Di), D ** -0.5)
    mlstm_conv_w = nrm((N_EVEN, MLSTM_CONV, Di), MLSTM_CONV ** -0.5)
    mlstm_conv_b = nrm((N_EVEN, Di), 0.01)
    mlstm_wq = nrm((N_EVEN, Di // QKV_BLOCK, QKV_BLOCK, QKV_BLOCK), QKV_BLOCK ** -0.5)
    mlstm_wk = nrm((N_EVEN, Di // QKV_BLOCK, QKV_BLOCK, QKV_BLOCK), QKV_BLOCK ** -0.5)
    mlstm_wv = nrm((N_EVEN, Di // QKV_BLOCK, QKV_BLOCK, QKV_BLOCK), QKV_BLOCK ** -0.5)
    mlstm_w_gates = nrm((N_EVEN, 3 * Di, 2 * NH), (3 * Di) ** -0.5)
    mlstm_b_gates = jnp.concatenate([nrm((N_EVEN, NH), 0.1),
                                     jnp.linspace(3.0, 6.0, NH, dtype=f32)[None] + nrm((N_EVEN, NH), 0.01)], axis=-1)
    mlstm_norm_w = 1.0 + nrm((N_EVEN, Di), 0.01)
    mlstm_skip = 1.0 + nrm((N_EVEN, Di), 0.01)
    mlstm_w_out = nrm((N_EVEN, Di, D), beta * Di ** -0.5)
    ffn_w13 = nrm((N_EVEN, D, 2 * F), D ** -0.5)
    ffn_w2 = nrm((N_EVEN, F, D), beta * F ** -0.5)
    s5_lambda_re = -0.5 + nrm((N_ODD, G, P), 0.01)
    s5_lambda_im = jnp.tile((math.pi * jnp.arange(P, dtype=f32))[None, None, :], (N_ODD, G, 1))
    s5_b_re = nrm((N_ODD, G, P, H), (2 * H) ** -0.5)
    s5_b_im = nrm((N_ODD, G, P, H), (2 * H) ** -0.5)
    s5_c_re = nrm((N_ODD, G, H, P), (2 * P) ** -0.5)
    s5_c_im = nrm((N_ODD, G, H, P), (2 * P) ** -0.5)
    s5_d = nrm((N_ODD, D), 1.0)
    s5_log_dt = jax.random.uniform(next(ks), (N_ODD, G), f32, math.log(DT_MIN), math.log(DT_MAX))
    s5_w_glu = jnp.concatenate([nrm((N_ODD, D, D), beta * D ** -0.5), nrm((N_ODD, D, D), D ** -0.5)], axis=-1)
    s5_b_glu = nrm((N_ODD, 2 * D), 0.01)
    moe_router = nrm((N_ODD, D, E), D ** -0.5)
    moe_w13 = nrm((N_ODD, E, D, 2 * F), D ** -0.5)
    moe_w2 = nrm((N_ODD, E, F, D), beta * F ** -0.5)
    return {"x": x, "c": c, "ada_w": ada_w, "ada_b": ada_b, "ln_mix_g": ln_mix_g, "ln_mix_b": ln_mix_b,
            "ln_ffn_g": ln_ffn_g, "ln_ffn_b": ln_ffn_b,
            "mlstm_w_in": mlstm_w_in, "mlstm_conv_w": mlstm_conv_w, "mlstm_conv_b": mlstm_conv_b,
            "mlstm_wq": mlstm_wq, "mlstm_wk": mlstm_wk, "mlstm_wv": mlstm_wv, "mlstm_w_gates": mlstm_w_gates,
            "mlstm_b_gates": mlstm_b_gates, "mlstm_norm_w": mlstm_norm_w, "mlstm_skip": mlstm_skip,
            "mlstm_w_out": mlstm_w_out, "ffn_w13": ffn_w13, "ffn_w2": ffn_w2,
            "s5_lambda_re": s5_lambda_re, "s5_lambda_im": s5_lambda_im, "s5_b_re": s5_b_re, "s5_b_im": s5_b_im,
            "s5_c_re": s5_c_re, "s5_c_im": s5_c_im, "s5_d": s5_d, "s5_log_dt": s5_log_dt,
            "s5_w_glu": s5_w_glu, "s5_b_glu": s5_b_glu,
            "moe_router": moe_router, "moe_w13": moe_w13, "moe_w2": moe_w2}

def first_block(x, c, ada_w, ada_b, ln_mix_g, ln_mix_b, ln_ffn_g, ln_ffn_b,
              mlstm_w_in, mlstm_conv_w, mlstm_conv_b, mlstm_wq, mlstm_wk, mlstm_wv, mlstm_w_gates,
              mlstm_b_gates, mlstm_norm_w, mlstm_skip, mlstm_w_out, ffn_w13, ffn_w2,
              s5_lambda_re, s5_lambda_im, s5_b_re, s5_b_im, s5_c_re, s5_c_im, s5_d, s5_log_dt,
              s5_w_glu, s5_b_glu, moe_router, moe_w13, moe_w2):
    cond = jax.nn.silu(c)
    for i in range(DEPTH):
        j = i // 2
        mod = cond @ ada_w[i] + ada_b[i]
        sh_m, sc_m, g_m, sh_f, sc_f, g_f = [t[:, None, :] for t in jnp.split(mod, 6, axis=-1)]
        u = x * (1.0 + sc_m) + sh_m
        if i % 2 == 0:
            y = mlstm_mixer(u, mlstm_w_in[j], mlstm_conv_w[j], mlstm_conv_b[j], mlstm_wq[j], mlstm_wk[j],
                            mlstm_wv[j], mlstm_w_gates[j], mlstm_b_gates[j], mlstm_norm_w[j], mlstm_skip[j],
                            mlstm_w_out[j])
        else:
            y = s5_mixer(u, s5_lambda_re[j], s5_lambda_im[j], s5_b_re[j], s5_b_im[j], s5_c_re[j], s5_c_im[j],
                         s5_d[j], s5_log_dt[j], s5_w_glu[j], s5_b_glu[j])
        x = layer_norm(DEEPNORM_ALPHA * x + (1.0 + g_m) * y, ln_mix_g[i], ln_mix_b[i])
        u = x * (1.0 + sc_f) + sh_f
        if i % 2 == 0:
            y = swiglu(u, ffn_w13[j], ffn_w2[j])
        else:
            y = moe_ffn(u, moe_router[j], moe_w13[j], moe_w2[j])
        x = layer_norm(DEEPNORM_ALPHA * x + (1.0 + g_f) * y, ln_ffn_g[i], ln_ffn_b[i])
    return x


GRID_W = 64
CTX_LEN = 256
N_MIXERS = 3
EPS = 1e-6
ROPE_BASE = 10000.0
Q_BLOCK = 128
N_MOD = 6

MLA_HEADS = 8
MLA_NOPE = 128
MLA_ROPE = 64
MLA_V = 128
MLA_Q_RANK = 384
MLA_KV_RANK = 256

HG_HEADS = 8
HG_DK = D_MODEL // HG_HEADS
HG_DV = D_MODEL // HG_HEADS
HG_CHUNK = 64

DF_HEADS = 8
DF_DQK = D_MODEL // (2 * DF_HEADS)
DF_DV = 2 * DF_DQK

D_FF_2 = -(-(8 * D_MODEL) // (3 * 256)) * 256

N_MLA = (DEPTH + N_MIXERS - 1) // N_MIXERS
N_HG = (DEPTH + N_MIXERS - 2) // N_MIXERS
N_DF = DEPTH // N_MIXERS


def rms_norm(x, w):
    xf = x.astype(jnp.float32)
    y = xf * lax.rsqrt(jnp.mean(xf * xf, axis=-1, keepdims=True) + EPS)
    return (y * w.astype(jnp.float32)).astype(x.dtype)

def modulate(x, shift, scale):
    return x * (1 + scale) + shift

def swiglu_2(a, w1, w3, w2):
    return (jax.nn.silu(a @ w1) * (a @ w3)) @ w2

def split_heads(t, n_heads):
    b, n, _ = t.shape
    return t.reshape(b, n, n_heads, -1).transpose(0, 2, 1, 3)

def merge_heads(t):
    b, h, n, d = t.shape
    return t.transpose(0, 2, 1, 3).reshape(b, n, h * d)

def axial_rope_tables(rows, rot_dim):
    row = jnp.repeat(jnp.arange(rows, dtype=jnp.float32), GRID_W)
    col = jnp.tile(jnp.arange(GRID_W, dtype=jnp.float32), rows)
    axis_dim = rot_dim // 2
    inv_freq = jnp.power(ROPE_BASE, -jnp.arange(0, axis_dim, 2, dtype=jnp.float32) / axis_dim)
    ang_r = row[:, None] * inv_freq
    ang_c = col[:, None] * inv_freq
    ang = jnp.concatenate([ang_r, ang_r, ang_c, ang_c], axis=-1)
    return jnp.cos(ang), jnp.sin(ang)

def apply_axial_rope(t, cos, sin):
    t1, t2, t3, t4 = jnp.split(t, 4, axis=-1)
    rot = jnp.concatenate([-t2, t1, -t4, t3], axis=-1)
    return (t * cos + rot * sin).astype(t.dtype)

def softmax_attend(q, k, v, scale):
    s = jnp.einsum('bhqd,bhkd->bhqk', q, k, preferred_element_type=jnp.float32) * scale
    p = jax.nn.softmax(s, axis=-1)
    return jnp.einsum('bhqk,bhkd->bhqd', p.astype(v.dtype), v)

def sweep_query_blocks(fn, q):
    n, d = q.shape[-2], q.shape[-1]
    nb = n // Q_BLOCK
    qb = jnp.moveaxis(q.reshape(q.shape[:-2] + (nb, Q_BLOCK, d)), -3, 0)
    o = jnp.moveaxis(lax.map(fn, qb), 0, -3)
    return o.reshape(o.shape[:-3] + (n, o.shape[-1]))

def gla_chunk_scan(q, k, v, log_f, s0):
    b, h, n, _ = q.shape
    nc = n // HG_CHUNK

    def chunks(t):
        return jnp.moveaxis(t.reshape(b, h, nc, HG_CHUNK, t.shape[-1]), 2, 0)

    order = jnp.tril(jnp.ones((HG_CHUNK, HG_CHUNK), dtype=bool))[:, :, None]

    def step(state, inp):
        qc, kc, vc, lfc = inp
        cum = jnp.cumsum(lfc, axis=-2)
        rel = jnp.where(order, cum[..., :, None, :] - cum[..., None, :, :], -jnp.inf)
        att = jnp.einsum('bhtd,bhsd,bhtsd->bhts', qc, kc, jnp.exp(rel))
        o = (jnp.einsum('bhts,bhse->bhte', att, vc)
             + jnp.einsum('bhtd,bhde->bhte', qc * jnp.exp(cum), state))
        last = cum[..., -1:, :]
        state = (jnp.exp(last[..., 0, :])[..., None] * state
                 + jnp.einsum('bhsd,bhse->bhde', kc * jnp.exp(last - cum), vc))
        return state, o

    state, o = lax.scan(step, s0, (chunks(q), chunks(k), chunks(v), chunks(log_f)))
    o = jnp.moveaxis(o, 0, 2).reshape(b, h, n, v.shape[-1])
    return o, state

def mla_mixer(a_lat, a_ctx, rope, w_in, q_norm_w, kv_norm_w, w_uq, w_ukv, qn_w, qr_w, kn_w, kr_w, w_o, update_ctx):
    cos, sin = rope

    def project(a):
        b, n, _ = a.shape
        cq, ckv, kr = jnp.split(a @ w_in, [MLA_Q_RANK, MLA_Q_RANK + MLA_KV_RANK], axis=-1)
        q = split_heads(rms_norm(cq, q_norm_w) @ w_uq, MLA_HEADS)
        kv = split_heads(rms_norm(ckv, kv_norm_w) @ w_ukv, MLA_HEADS)
        q_nope = rms_norm(q[..., :MLA_NOPE], qn_w)
        q_rope = rms_norm(q[..., MLA_NOPE:], qr_w)
        k_nope = rms_norm(kv[..., :MLA_NOPE], kn_w)
        v = kv[..., MLA_NOPE:]
        k_rope = rms_norm(kr, kr_w)[:, None]
        return q_nope, q_rope, k_nope, k_rope, v

    def full_k(kn, kr):
        return jnp.concatenate([kn, jnp.broadcast_to(kr, kn.shape[:-1] + (MLA_ROPE,))], axis=-1)

    qn_l, qr_l, kn_l, kr_l, v_l = project(a_lat)
    qr_l = apply_axial_rope(qr_l, cos, sin)
    kr_l = apply_axial_rope(kr_l, cos, sin)
    qn_c, qr_c, kn_c, kr_c, v_c = project(a_ctx)
    k_c = full_k(kn_c, kr_c)
    k_all = jnp.concatenate([k_c, full_k(kn_l, kr_l)], axis=-2)
    v_all = jnp.concatenate([v_c, v_l], axis=-2)
    scale = 1.0 / math.sqrt(MLA_NOPE + MLA_ROPE)
    q_l = jnp.concatenate([qn_l, qr_l], axis=-1)
    o_l = sweep_query_blocks(lambda qb: softmax_attend(qb, k_all, v_all, scale), q_l)
    out_l = merge_heads(o_l) @ w_o
    out_c = None
    if update_ctx:
        q_c = jnp.concatenate([qn_c, qr_c], axis=-1)
        out_c = merge_heads(softmax_attend(q_c, k_c, v_c, scale)) @ w_o
    return out_l, out_c

def hgrn2_mixer(a_lat, a_ctx, layer_idx, w_in, lb_logits, o_norm_w, w_o, update_ctx):
    lb_cum = jnp.cumsum(jax.nn.softmax(lb_logits.astype(jnp.float32), axis=0), axis=0)
    lb = lb_cum[layer_idx] - lb_cum[0]

    def project(a):
        q, zf, zb, i, g = jnp.split(a @ w_in, 5, axis=-1)

        def heads(t):
            return split_heads(t, HG_HEADS).astype(jnp.float32)

        def log_forget(z, lbd):
            lbd = lbd.reshape(HG_HEADS, 1, HG_DK)
            return jnp.logaddexp(jnp.log(lbd), jnp.log1p(-lbd) + jax.nn.log_sigmoid(heads(z)))

        return heads(q), heads(i), log_forget(zf, lb[0]), log_forget(zb, lb[1]), g

    def scan_dir(q, i, log_f, s0):
        return gla_chunk_scan(q, -jnp.expm1(log_f), i, log_f, s0)

    def rev(t):
        return jnp.flip(t, axis=-2)

    def readout(o, g):
        o = rms_norm(o.astype(a_lat.dtype), o_norm_w)
        return (merge_heads(o) * jax.nn.silu(g)) @ w_o

    q_l, i_l, lf_l, lbk_l, g_l = project(a_lat)
    q_c, i_c, lf_c, lbk_c, g_c = project(a_ctx)
    s0 = jnp.zeros((a_ctx.shape[0], HG_HEADS, HG_DK, HG_DV), jnp.float32)
    o_cf, s_cf = scan_dir(q_c, i_c, lf_c, s0)
    o_cb, s_cb = scan_dir(rev(q_c), rev(i_c), rev(lbk_c), s0)
    o_lf, _ = scan_dir(q_l, i_l, lf_l, s_cf)
    o_lb, _ = scan_dir(rev(q_l), rev(i_l), rev(lbk_l), s_cb)
    out_l = readout(o_lf + rev(o_lb), g_l)
    out_c = readout(o_cf + rev(o_cb), g_c) if update_ctx else None
    return out_l, out_c

def diff_mixer(a_lat, a_ctx, rope, layer_idx, w_qkv, qn_w, kn_w, lam_vec, sub_norm_w, w_o, update_ctx):
    cos, sin = rope
    lam_init = 0.8 - 0.6 * math.exp(-0.3 * layer_idx)
    lv = lam_vec.astype(jnp.float32)
    lam = jnp.exp(jnp.sum(lv[0] * lv[1])) - jnp.exp(jnp.sum(lv[2] * lv[3])) + lam_init

    def project(a):
        b, n, _ = a.shape
        q, k, v = jnp.split(a @ w_qkv, 3, axis=-1)
        q = rms_norm(q.reshape(b, n, DF_HEADS, 2, DF_DQK).transpose(0, 2, 3, 1, 4), qn_w)
        k = rms_norm(k.reshape(b, n, DF_HEADS, 2, DF_DQK).transpose(0, 2, 3, 1, 4), kn_w)
        return q, k, split_heads(v, DF_HEADS)

    scale = 1.0 / math.sqrt(DF_DQK)

    def diff_attend(q, k, v):
        s = jnp.einsum('bhmqd,bhmkd->bhmqk', q, k, preferred_element_type=jnp.float32) * scale
        p = jax.nn.softmax(s, axis=-1)
        a = p[:, :, 0] - lam * p[:, :, 1]
        return jnp.einsum('bhqk,bhkd->bhqd', a.astype(v.dtype), v)

    def readout(o):
        return merge_heads(rms_norm(o, sub_norm_w) * (1.0 - lam_init)) @ w_o

    q_l, k_l, v_l = project(a_lat)
    q_l = apply_axial_rope(q_l, cos, sin)
    k_l = apply_axial_rope(k_l, cos, sin)
    q_c, k_c, v_c = project(a_ctx)
    k_all = jnp.concatenate([k_c, k_l], axis=-2)
    v_all = jnp.concatenate([v_c, v_l], axis=-2)
    out_l = readout(sweep_query_blocks(lambda qb: diff_attend(qb, k_all, v_all), q_l))
    out_c = readout(diff_attend(q_c, k_c, v_c)) if update_ctx else None
    return out_l, out_c

def second_inputs(seed: int = 0) -> dict:
    key = jax.random.key(seed)
    ks = iter(jax.random.split(key, 40))
    D = D_MODEL

    def nrm(shape, scale):
        return scale * jax.random.normal(next(ks), shape, jnp.float32)

    def gain(shape):
        return 1.0 + nrm(shape, 0.02)

    return {
        'x': nrm((BATCH, SEQ, D), 1.0),
        'c': nrm((BATCH, D), 1.0),
        'ctx': nrm((BATCH, CTX_LEN, D), 1.0),
        'c_ctx': nrm((D,), 1.0),
        'ada_w': nrm((DEPTH, D, N_MOD * D), 0.5 * D ** -0.5),
        'ada_b': nrm((DEPTH, N_MOD * D), 0.02),
        'norm1_w': gain((DEPTH, D)),
        'norm2_w': gain((DEPTH, D)),
        'ffn_w1': nrm((DEPTH, D, D_FF_2), D ** -0.5),
        'ffn_w3': nrm((DEPTH, D, D_FF_2), D ** -0.5),
        'ffn_w2': nrm((DEPTH, D_FF_2, D), D_FF_2 ** -0.5),
        'mla_w_in': nrm((N_MLA, D, MLA_Q_RANK + MLA_KV_RANK + MLA_ROPE), D ** -0.5),
        'mla_q_norm_w': gain((N_MLA, MLA_Q_RANK)),
        'mla_kv_norm_w': gain((N_MLA, MLA_KV_RANK)),
        'mla_w_uq': nrm((N_MLA, MLA_Q_RANK, MLA_HEADS * (MLA_NOPE + MLA_ROPE)), MLA_Q_RANK ** -0.5),
        'mla_w_ukv': nrm((N_MLA, MLA_KV_RANK, MLA_HEADS * (MLA_NOPE + MLA_V)), MLA_KV_RANK ** -0.5),
        'mla_qn_w': gain((N_MLA, MLA_NOPE)),
        'mla_qr_w': gain((N_MLA, MLA_ROPE)),
        'mla_kn_w': gain((N_MLA, MLA_NOPE)),
        'mla_kr_w': gain((N_MLA, MLA_ROPE)),
        'mla_w_o': nrm((N_MLA, MLA_HEADS * MLA_V, D), (MLA_HEADS * MLA_V) ** -0.5),
        'hg_w_in': nrm((N_HG, D, 5 * D), D ** -0.5),
        'hg_lb_logits': nrm((DEPTH, 2, D), 1.0),
        'hg_o_norm_w': gain((N_HG, HG_DV)),
        'hg_w_o': nrm((N_HG, D, D), D ** -0.5),
        'df_w_qkv': nrm((N_DF, D, 3 * D), D ** -0.5),
        'df_qn_w': gain((N_DF, DF_DQK)),
        'df_kn_w': gain((N_DF, DF_DQK)),
        'df_lambda': nrm((N_DF, 4, DF_DQK), 0.1),
        'df_sub_norm_w': gain((N_DF, DF_DV)),
        'df_w_o': nrm((N_DF, D, D), D ** -0.5),
    }

def second_block(x, c, ctx, c_ctx, ada_w, ada_b, norm1_w, norm2_w, ffn_w1, ffn_w3, ffn_w2,
              mla_w_in, mla_q_norm_w, mla_kv_norm_w, mla_w_uq, mla_w_ukv, mla_qn_w, mla_qr_w, mla_kn_w,
              mla_kr_w, mla_w_o, hg_w_in, hg_lb_logits, hg_o_norm_w, hg_w_o,
              df_w_qkv, df_qn_w, df_kn_w, df_lambda, df_sub_norm_w, df_w_o):
    rows = x.shape[1] // GRID_W
    rope_mla = axial_rope_tables(rows, MLA_ROPE)
    rope_df = axial_rope_tables(rows, DF_DQK)
    h_ctx = ctx
    for i in range(DEPTH):
        kind, j = i % N_MIXERS, i // N_MIXERS
        update_ctx = i < DEPTH - 1
        mod_l = jnp.split((jax.nn.silu(c) @ ada_w[i] + ada_b[i])[:, None, :], N_MOD, axis=-1)
        mod_c = jnp.split((jax.nn.silu(c_ctx) @ ada_w[i] + ada_b[i])[None, None, :], N_MOD, axis=-1)
        a_l = modulate(rms_norm(x, norm1_w[i]), mod_l[0], mod_l[1])
        a_c = modulate(rms_norm(h_ctx, norm1_w[i]), mod_c[0], mod_c[1])
        if kind == 0:
            o_l, o_c = mla_mixer(a_l, a_c, rope_mla, mla_w_in[j], mla_q_norm_w[j], mla_kv_norm_w[j],
                                 mla_w_uq[j], mla_w_ukv[j], mla_qn_w[j], mla_qr_w[j], mla_kn_w[j],
                                 mla_kr_w[j], mla_w_o[j], update_ctx)
        elif kind == 1:
            o_l, o_c = hgrn2_mixer(a_l, a_c, i, hg_w_in[j], hg_lb_logits, hg_o_norm_w[j], hg_w_o[j], update_ctx)
        else:
            o_l, o_c = diff_mixer(a_l, a_c, rope_df, i, df_w_qkv[j], df_qn_w[j], df_kn_w[j], df_lambda[j],
                                  df_sub_norm_w[j], df_w_o[j], update_ctx)
        x = x + mod_l[2] * o_l
        x = x + mod_l[5] * swiglu_2(modulate(rms_norm(x, norm2_w[i]), mod_l[3], mod_l[4]),
                                  ffn_w1[i], ffn_w3[i], ffn_w2[i])
        if update_ctx:
            h_ctx = h_ctx + mod_c[2] * o_c
            h_ctx = h_ctx + mod_c[5] * swiglu_2(modulate(rms_norm(h_ctx, norm2_w[i]), mod_c[3], mod_c[4]),
                                              ffn_w1[i], ffn_w3[i], ffn_w2[i])
    return x


def setup_inputs(seed=0):
    out = dict(first_inputs(seed))
    for name, value in second_inputs(seed + 1).items():
        if name != "x":
            out[name + "_2"] = value
    return out


def reference(
    x, c, ada_w, ada_b, ln_mix_g, ln_mix_b, ln_ffn_g, ln_ffn_b, mlstm_w_in, mlstm_conv_w,
    mlstm_conv_b, mlstm_wq, mlstm_wk, mlstm_wv, mlstm_w_gates, mlstm_b_gates, mlstm_norm_w,
    mlstm_skip, mlstm_w_out, ffn_w13, ffn_w2, s5_lambda_re, s5_lambda_im, s5_b_re, s5_b_im,
    s5_c_re, s5_c_im, s5_d, s5_log_dt, s5_w_glu, s5_b_glu, moe_router, moe_w13, moe_w2, c_2,
    ctx_2, c_ctx_2, ada_w_2, ada_b_2, norm1_w_2, norm2_w_2, ffn_w1_2, ffn_w3_2, ffn_w2_2,
    mla_w_in_2, mla_q_norm_w_2, mla_kv_norm_w_2, mla_w_uq_2, mla_w_ukv_2, mla_qn_w_2,
    mla_qr_w_2, mla_kn_w_2, mla_kr_w_2, mla_w_o_2, hg_w_in_2, hg_lb_logits_2, hg_o_norm_w_2,
    hg_w_o_2, df_w_qkv_2, df_qn_w_2, df_kn_w_2, df_lambda_2, df_sub_norm_w_2, df_w_o_2,
):
    x = first_block(
        x, c, ada_w, ada_b, ln_mix_g, ln_mix_b, ln_ffn_g, ln_ffn_b, mlstm_w_in, mlstm_conv_w,
        mlstm_conv_b, mlstm_wq, mlstm_wk, mlstm_wv, mlstm_w_gates, mlstm_b_gates, mlstm_norm_w,
        mlstm_skip, mlstm_w_out, ffn_w13, ffn_w2, s5_lambda_re, s5_lambda_im, s5_b_re, s5_b_im,
        s5_c_re, s5_c_im, s5_d, s5_log_dt, s5_w_glu, s5_b_glu, moe_router, moe_w13, moe_w2,
    )
    return second_block(
        x, c_2, ctx_2, c_ctx_2, ada_w_2, ada_b_2, norm1_w_2, norm2_w_2, ffn_w1_2, ffn_w3_2,
        ffn_w2_2, mla_w_in_2, mla_q_norm_w_2, mla_kv_norm_w_2, mla_w_uq_2, mla_w_ukv_2,
        mla_qn_w_2, mla_qr_w_2, mla_kn_w_2, mla_kr_w_2, mla_w_o_2, hg_w_in_2, hg_lb_logits_2,
        hg_o_norm_w_2, hg_w_o_2, df_w_qkv_2, df_qn_w_2, df_kn_w_2, df_lambda_2, df_sub_norm_w_2,
        df_w_o_2,
    )


_drawn_inputs = setup_inputs


def setup_inputs(seed=0):
    import zlib

    import numpy as np

    out = dict(_drawn_inputs(seed))
    spreads = {}
    factors = {'ada_b': 3.279,
     'ln_mix_g': 2.729,
     'ln_mix_b': 2.83,
     'ln_ffn_g': 2.924,
     'ln_ffn_b': 2.824,
     'mlstm_conv_b': 6.962,
     'mlstm_norm_w': 8.0,
     'mlstm_skip': 8.0,
     's5_lambda_re': 64.0,
     's5_lambda_im': 40.512,
     's5_b_re': 64.0,
     's5_b_im': 64.0,
     's5_c_re': 46.016,
     's5_c_im': 64.0,
     's5_log_dt': 55.424,
     's5_b_glu': 6.132,
     'norm1_w_2': 7.053,
     'norm2_w_2': 6.452,
     'mla_q_norm_w_2': 8.0,
     'mla_kv_norm_w_2': 8.0,
     'mla_qn_w_2': 8.0,
     'mla_qr_w_2': 8.0,
     'mla_kn_w_2': 8.0,
     'mla_kr_w_2': 8.0,
     'hg_o_norm_w_2': 27.082}
    for name, (base, spread) in spreads.items():
        noise = np.random.default_rng([zlib.crc32(name.encode()), seed]).standard_normal(out[name].shape)
        drawn = base * np.exp(spread * noise) if base else spread * noise
        out[name] = jnp.asarray(drawn.astype(out[name].dtype))
    for name, factor in factors.items():
        out[name] = (out[name] * factor).astype(out[name].dtype)
    return out
```

```python
from contextlib import ExitStack

import numpy as np

import concourse.bass as bass
from concourse import mybir

P = 128
F32 = mybir.dt.float32
ALU = mybir.AluOpType
ACT = mybir.ActivationFunctionType
AX = mybir.AxisListType

D = 1024
T = 256
DC = D // P
LN_EPS = 1e-5
RMS_EPS = 1e-6
ALPHA = 4 ** 0.25

DI = 2 * D
IC = DI // P
NH = 4
DH = DI // NH
HC = DH // P
CONV = 4

FF = 2816
FC = FF // P
FSTEPS = FC // 2
NE = 8

SG, SP_, SH = 64, 64, 16
SL = 128
NPAIR = SG // 2

AH = 8
NOPE, ROPE = 128, 64
QR, KVR = 384, 256
ATT_SCALE = (NOPE + ROPE) ** -0.5

RING = 6
SLOT = 2048
NB = 4
BANK = 512

LEVELS = [64, 32, 16, 8, 4, 2, 1]



def shape_constants():
    p = np.arange(P)
    parts = {}

    def put(name, a):
        full = np.zeros((P, a.shape[1]), np.float32)
        full[: a.shape[0]] = a
        parts[name] = full

    put("ident", np.eye(P))
    put("ones", np.ones((P, P)))
    put("block4", (p[:, None] // 4 == np.arange(32)[None]).astype(np.float32))
    s = p[:, None, None] + P * np.arange(2)[None, :, None]
    put("causal", np.where(s <= np.arange(T)[None, None], 0.0, -1e30).reshape(P, 2 * T))
    put("half", (p[:, None] // 64 == np.arange(2)[None]).astype(np.float32))
    put("parity", ((p[None] // SH) % 2 == p[:, None] // 64).astype(np.float32))
    put("before", np.tile((np.arange(NE)[None] < np.arange(NE)[:, None]).reshape(1, -1), (P, 1)))
    rows = T // 64
    row = np.repeat(np.arange(rows, dtype=np.float32), 64)
    col = np.tile(np.arange(64, dtype=np.float32), rows)
    inv = np.power(np.float32(10000.0), -np.arange(0, 32, 2, dtype=np.float32) / np.float32(32)).astype(np.float32)
    ar, ac = row[:, None] * inv, col[:, None] * inv
    ang = np.concatenate([ar, ar, ac, ac], axis=-1).astype(np.float32)
    put("rope_cos", np.cos(ang).T)
    put("rope_sin", np.sin(ang).T)
    rot = np.zeros((ROPE, ROPE), np.float32)
    for i in range(16):
        rot[i, 16 + i] = -1
        rot[16 + i, i] = 1
        rot[32 + i, 48 + i] = -1
        rot[48 + i, 32 + i] = 1
    put("rotT", rot.T)
    masks = []
    for b in LEVELS:
        same = p[:, None] // (2 * b) == p[None] // (2 * b)
        masks.append(same & (p[:, None] // b != p[None] // b))
    masks.append(np.eye(P, dtype=bool))
    put("levels", np.concatenate(masks, 1).astype(np.float32))
    where, at = {}, 0
    for name, a in parts.items():
        where[name] = (at, at + a.shape[1])
        at += a.shape[1]
    return np.concatenate(list(parts.values()), 1).astype(np.float32), where


def reserve(counts):
    first, n = {}, 0
    for name, k in counts:
        first[name] = n
        n += k
    first["end"] = n
    return first


MLA_ITEMS = [("cq", 0, 3), ("ckv", 0, 2), ("kr", 0, 1)]
for _h in range(AH):
    MLA_ITEMS += [("qn", _h, 1), ("qr", _h, 1)]
MLA_ITEMS += [("kn", _h, 1) for _h in range(AH)]


def mla_sequence():
    seq, waiting = [], []
    for m, (kind, h, n) in enumerate(MLA_ITEMS):
        seq += [("P", m, c) for c in range(n)]
        if waiting:
            seq.append(("S", waiting.pop(), 0))
        waiting.append(m)
        if kind == "kr":
            seq.append(("S", waiting.pop(), 0))
        if kind == "kn" and h % 4 == 3:
            seq += [("V", h // 4, a) for a in range(4)]
    seq.append(("S", waiting.pop(), 0))
    return seq


MLA_SEQ = mla_sequence()


def attention_sequence():
    seq = [("S", 0, k) for k in range(3)]
    for h in range(AH + 1):
        if h + 1 < AH:
            seq += [("S", h + 1, k) for k in range(3)]
        if h < AH:
            seq += [("T", h, k) for k in range(3)]
        if h >= 1:
            seq.append(("O", h - 1, 0))
    return seq


ATTN_SEQ = attention_sequence()

TILES = [("ada0", 24), ("m_in", 16), ("m_out", 8), ("ffn0", 3 * FSTEPS), ("ada1", 24), ("glu", 8),
         ("moe", 3 * FSTEPS * NE), ("ada2", 24), ("mla_in", 3), ("mla_uq", 3), ("mla_ukv", 2), ("mla_o", 4),
         ("ffn2", 34), ("ada3", 24), ("hg_q", 4), ("hg_z", 8), ("hg_i", 4), ("hg_g", 4), ("hg_o", 4),
         ("ffn3", 3 * FSTEPS)]
JOBS = [("params", 5), ("xT", 4), ("ada0", 1), ("m_in", 16), ("m_qk", 16), ("m_vT", 8), ("m_gates", 1),
        ("m_fsel", 1), ("m_cT", 1), ("m_rows", NH), ("m_v", 8), ("m_head", 4 * NH), ("m_norm", 2 * NH),
        ("m_out", 4), ("ln0", 2), ("ffn0", 2 * FSTEPS), ("ln1", 2), ("ada1", 1), ("s_bT", 4), ("s_cT", 4),
        ("s_pair", NPAIR), ("glu", 8), ("ln2", 2), ("router", 1), ("gateT", 1), ("gates", 4),
        ("moe", 2 * FSTEPS * NE), ("ln3", 2), ("ctxT", 4), ("ada2", 1), ("rms0", 1),
        ("mla_seq", len(MLA_SEQ)), ("rope", AH + 1), ("attn", len(ATTN_SEQ)), ("mla_o", 8), ("rms1", 1),
        ("ffn2", 4 * FSTEPS), ("ada3", 1), ("rms2", 1), ("hg_q", 4), ("hg_z", 16), ("hg_i", 8), ("hg_g", 4),
        ("hg_wk", 8), ("hg_state", 4), ("hg_level", 4 * (len(LEVELS) + 2)), ("hg_norm", 4), ("hg_o", 4), ("rms3", 1),
        ("ffn3", 2 * FSTEPS), ("outT", 4)]


def build_program(nc, w, const, out):
    _, cols = shape_constants()
    tile_of, job_of = reserve(TILES), reserve(JOBS)

    with ExitStack() as ctx:
        signals = {}

        def S(name):
            if name not in signals:
                signals[name] = ctx.enter_context(nc.semaphore(name))
            return signals[name]

        def sb(name, shape, scope=ctx):
            return scope.enter_context(nc.sbuf_tensor(name, shape, F32))

        loaded = [S(f"slot_loaded{i}") for i in range(RING)]
        tile_begun = S("tile_begun")
        bank_full = [S(f"bank_full{i}") for i in range(NB)]
        bank_out = [S(f"bank_out{i}") for i in range(NB)]

        psum = ctx.enter_context(nc.psum_tensor("psum", [P, 8, BANK], F32))
        ring = sb("ring", [P, RING, SLOT])
        cst = sb("cst", [P, const.shape[1]])
        prow = sb("prow", [P, 5, P])
        par = sb("par", [P, 5 * P])
        xT = sb("xT", [P, DC, T])
        mod = sb("mod", [P, 4, 48, 2])
        mod1 = sb("mod1", [P, 4, 48, 2])
        csil = sb("csil", [P, DC, 3])
        small = sb("small", [P, 64])
        stat = sb("stat", [P, 2, T])
        zeros = sb("zeros", [P, P])
        router_w = sb("router_w", [P, DC, NE])
        one = sb("one", [P, 1])

        def c_(name):
            a, b = cols[name]
            return cst[:, a:b]

        ident, ones = c_("ident"), c_("ones")

        def c_one(n):
            return ones[:, 0:1].broadcast_to([P, n])

        def val(base, it, inc):
            return base if it is None else it * inc + base

        def wait_tile(pe, t, it=None, per=0):
            pe.wait_ge(loaded[t % RING], val(16 * (t // RING + 1), it, 16 * (per // RING)))

        def wait_free(pe, j, it=None, per=0):
            if it is not None or j // NB > 0:
                pe.wait_ge(bank_out[j % NB], val(j // NB, it, per // NB))

        def wait_full(eng, j, it=None, per=0):
            eng.wait_ge(bank_full[j % NB], val(j // NB + 1, it, per // NB))

        def full(ins, j):
            ins.then_inc(bank_full[j % NB], 1)

        def out_of(ins, j):
            ins.then_inc(bank_out[j % NB], 1)

        def wait_out(eng, j, it=None, per=0):
            eng.wait_ge(bank_out[j % NB], val(j // NB + 1, it, per // NB))

        def bank(j):
            return psum[:, j % NB, :]

        def repeat(eng, n, g, body):
            whole = n // g
            if whole >= 2:
                with eng.Fori(0, whole) as it:
                    for j in range(g):
                        body(it, j)
                rest = whole * g
            else:
                rest = 0
            for j in range(rest, n):
                body(None, j)

        def after_two(eng, n, g, body):
            whole = (n - 2) // g
            with eng.Fori(0, whole) as it:
                for j in range(g):
                    body(it, 2 + j)
            for j in range(2 + whole * g, n):
                body(None, j)

        def step_of(it, j, g):
            return j if it is None else it * g + j

        prow_at, prow_dmas, n_rows = {}, [], 0

        def rows_of(name, ap, width=P):
            nonlocal n_rows
            k = ap.shape[0]
            prow_at[name] = n_rows
            done = 0
            while done < k:
                r = n_rows % P
                m = min(k - done, P - r)
                prow_dmas.append((prow[r:r + m, n_rows // P, 0:width], ap[done:done + m, :]))
                done += m
                n_rows += m

        def r128(ap):
            return ap.rearrange("(a b) -> a b", b=P)

        rows_of("c", w["c"].rearrange("o (a b) -> (o a) b", b=P))
        rows_of("c_2", w["c_2"].rearrange("o (a b) -> (o a) b", b=P))
        rows_of("c_ctx_2", r128(w["c_ctx_2"]))
        for l in range(2):
            rows_of(f"ada_b{l}", r128(w["ada_b"][l]))
            rows_of(f"ada_b{l + 2}", r128(w["ada_b_2"][l]))
            for name in ("ln_mix_g", "ln_mix_b", "ln_ffn_g", "ln_ffn_b", "norm1_w_2", "norm2_w_2"):
                rows_of(f"{name}{l}", r128(w[name][l]))
        rows_of("conv_w", w["mlstm_conv_w"].rearrange("o k (a b) -> (o k a) b", b=P))
        for name in ("mlstm_conv_b", "mlstm_norm_w", "mlstm_skip", "s5_d", "s5_b_glu",
                     "mla_q_norm_w_2", "mla_kv_norm_w_2", "mla_qn_w_2", "mla_kn_w_2", "hg_o_norm_w_2"):
            rows_of(name, r128(w[name][0]))
        rows_of("lam_re", w["s5_lambda_re"].rearrange("o (a b) p -> (o a) (b p)", b=2))
        rows_of("lam_im", w["s5_lambda_im"].rearrange("o (a b) p -> (o a) (b p)", b=2))
        rows_of("lb", w["hg_lb_logits_2"].rearrange("l d (a b) -> (l d a) b", b=P))
        rows_of("mla_qr_w_2", w["mla_qr_w_2"], ROPE)
        rows_of("mla_kr_w_2", w["mla_kr_w_2"], ROPE)
        rows_of("b_gates", w["mlstm_b_gates"], 8)
        assert n_rows <= 5 * P, n_rows

        def col(name, k=0, n=1):
            a = prow_at[name] + k
            return par[:, a:a + n]

        act_in = sb("act_in", [P, DC, T])
        first = ctx.enter_context(ExitStack())
        xm = sb("xm", [P, IC, T + 4], first)
        zs = sb("zs", [P, IC, T], first)
        work = ExitStack()
        xc = sb("xc", [P, IC, T], work)
        qk = sb("qk", [P, IC, 2, T], work)
        vbuf = sb("vbuf", [P, 2, DI], work)
        bd = sb("bd", [P, 3, IC, P], work)
        qkv_small = sb("qkv_small", [P, 3, IC, 4], work)
        wgates = sb("wgates", [P, 3 * IC, 2 * NH], work)
        work.close()
        vT = vbuf.rearrange("p a b -> p (a b)").rearrange("p (c t) -> p c t", t=T)
        xtok = zs.rearrange("p c t -> p (c t)")[:, 0:2 * D].rearrange("p (a d) -> p a d", a=2)
        hT = qk[:, :, 0, :]
        gate_rows = act_in
        nm = bd[:, 0].rearrange("p c o -> p (c o)").rearrange("p (h k t) -> p h k t", h=NH, k=2)
        decay = bd[:, 1, 0:4].rearrange("p c o -> p (c o)").rearrange("p (s t) -> p s t", s=2)
        scor = bd[:, 1, 4:12].rearrange("p c o -> p (c o)").rearrange("p (k s t) -> p k s t", k=2, s=2)
        recip_ = bd[:, 1, 12:16].rearrange("p c o -> p (c o)").rearrange("p (k t) -> p k t", k=2)
        cT = small[:, 0:8].rearrange("p (s h) -> p s h", s=2)
        res = xm.rearrange("p c t -> p (c t)")[:, 0:DC * T].rearrange("p (c t) -> p c t", t=T)
        sqr = xm.rearrange("p c t -> p (c t)")[:, DC * T:2 * DC * T].rearrange("p (c t) -> p c t", t=T)

        hid = zs[:, 0:4].rearrange("p (b a) t -> p b a t", a=2)
        sil = zs[:, 4:8].rearrange("p (b a) t -> p b a t", a=2)
        ffn_bufs = {"ffn0": (hid, sil), "moe": (hid, sil)}

        work = ExitStack()
        bmat = sb("bmat", [P, 2, NPAIR, SH], work)
        bbar = sb("bbar", [P, 2, NPAIR, SH], work)
        bpad = sb("bpad", [P, 2, DC, P], work)
        bT = sb("bT", [P, 2, DC, P], work)
        ctok = sb("ctok", [P, 2, DC, 2, SP_], work)
        cmT = sb("cmT", [P, 2, DC, P], work)
        rot = sb("rot", [P, 2, NPAIR, SL], work)
        sv = sb("sv", [P, 20, NPAIR], work)
        pairbuf = sb("pairbuf", [P, 12, T], work)
        work.close()
        dbl = pairbuf[:, 0:8].rearrange("p a t -> p (a t)").rearrange("p (j n) -> p j n", n=SL // 2)
        btmp = pairbuf[:, 8:10].rearrange("p a t -> p (a t)").rearrange("p (j n) -> p j n", n=SH)
        zri, xri, ztmp = pairbuf[:, 0:2], pairbuf[:, 2:6].rearrange("p (k a) t -> p k a t", k=2), pairbuf[:, 6:8]
        gT = zs[:, 8:16]

        work = ExitStack()
        gate_bc = sb("gate_bc", [P, NE, T], work)
        gate8 = sb("gate8", [P, T], work)
        lg = sb("lg", [P, 8, 2, NE], work)
        cmp_ = sb("cmp_", [P, 2, 2, NE, NE], work)
        work.close()

        first.close()
        second = ctx.enter_context(ExitStack())
        T2 = 2 * T
        ctxT = sb("ctxT", [P, DC, T], second)
        a2 = sb("a2", [P, DC, T2], second)
        norm_gain = sb("norm_gain", [P, DC, 2], second)
        rstd2 = sb("rstd2", [P, T2], second)
        halves = (xT, ctxT)

        work = ExitStack()
        qn = sb("qn", [P, AH, T2], work)
        qr = sb("qr", [P, AH, T2], work)
        kn = sb("kn", [P, AH, T2], work)
        vtok = sb("vtok", [P, 4, D], work)
        cq = sb("cq", [P, 3, T2], work)
        ckv = sb("ckv", [P, 2, T2], work)
        kr = sb("kr", [P, 1, T2], work)
        nstat = sb("nstat", [P, 2, T2], work)
        prob = sb("prob", [P, 2, 3, T2], work)
        smax = sb("smax", [P, 2, 16], work)
        work.close()
        nsq = prob[:, 0]
        rms_sq = qn
        probTs = [x.rearrange("p a t -> p (a t)")[:, 0:6 * T].rearrange("p (s t) -> p s t", t=T) for x in (cq, act_in)]
        oT = a2
        ctx_tok = qn.rearrange("p h t -> p (h t)")[:, 0:2 * D].rearrange("p (a d) -> p a d", a=2)
        rope_tmp = prob[:, 1]
        mla_buf = {"cq": cq, "ckv": ckv, "kr": kr, "qn": qn, "qr": qr, "kn": kn}
        mla_job = {key: job_of["mla_seq"] + n for n, key in enumerate(MLA_SEQ)}
        attn_job = {key: job_of["attn"] + n for n, key in enumerate(ATTN_SEQ)}

        def item_of(m):
            kind, h, n = MLA_ITEMS[m]
            rows = ROPE if kind in ("qr", "kr") else P
            weight = {"cq": "mla_q_norm_w_2", "ckv": "mla_kv_norm_w_2", "kr": "mla_kr_w_2", "qn": "mla_qn_w_2",
                      "qr": "mla_qr_w_2", "kn": "mla_kn_w_2"}[kind]
            slots = {"cq": (0, 1, 2), "ckv": (0, 1), "kr": (2,)}.get(kind, (m % 3,))
            return kind, h, n, rows, mla_buf[kind], weight, slots

        work = ExitStack()
        hid2 = sb("hid2", [P, FC, T2], work)
        sil2 = sb("sil2", [P, 2, T2], work)
        work.close()
        rms_sq2 = hid2[:, 0:DC]

        work = ExitStack()
        lf = sb("lf", [P, 2, AH, T2], work)
        kf = sb("kf", [P, 2, AH, T2], work)
        itok = sb("itok", [P, 4, D], work)
        ework2 = sb("ework2", [P, 2, AH, T], work)
        lbs = sb("lbs", [P, 3, 16], work)
        work.close()
        ework = a2.rearrange("p c t -> p (c t)").rearrange("p (k h t) -> p k h t", k=2, h=AH)
        eworks = (ework, ework2)
        wkT = ework2.rearrange("p k h t -> p (k h t)").rearrange("p (i s) -> p i s", s=P)
        qh = act_in
        gsil = ctxT
        atts = lf[:, 0, :, T:T + P].rearrange("p (b i) t -> p b i t", b=2)
        hstat = itok[:, 0:2].rearrange("p a d -> p (a d)").rearrange("p (h t) -> p h t", h=AH)
        state = kf
        rms_sq3 = kf[:, 0].rearrange("p h t -> p (h t)")[:, 0:DC * T].rearrange("p (c t) -> p c t", t=T)
        hid3 = gsil[:, 0:4].rearrange("p (b a) t -> p b a t", a=2)
        sil3 = gsil[:, 4:8].rearrange("p (b a) t -> p b a t", a=2)
        ffn_bufs["ffn3"] = (hid3, sil3)
        out_tok = ework2.rearrange("p k h t -> p (k h t)")[:, 0:2 * D].rearrange("p (a d) -> p a d", a=2)

        block = ctx.enter_context(nc.Block())

        @block.sync
        def _(sp):
            def load(t, width, shape, src, it=None, per=0):
                if it is not None or t >= RING:
                    sp.wait_ge(tile_begun, val(t - RING + 2, it, per))
                dst = ring[:, t % RING, 0:width]
                for pattern, dims in shape:
                    dst = dst.rearrange(pattern, **dims)
                sp.dma_start(dst, src).then_inc(loaded[t % RING], 16)

            def load_cols(t, mat, n0, n, k0=0, kc=DC, it=None, per=0):
                src = mat[k0 * P:(k0 + kc) * P].rearrange("(c p) n -> p c n", p=P)[:, :, bass.ds(n0, n)]
                load(t, kc * n, [("p (c n) -> p c n", dict(c=kc))], src, it, per)

            def load_rows(t, mat, k0, it=None, per=0):
                src = mat[bass.ds(k0, 2 * P)].rearrange("(c p) n -> p c n", p=P)
                load(t, 2 * D, [("p (c n) -> p c n", dict(c=2))], src, it, per)

            def ada(l, mat):
                def tile(it, j):
                    load_cols(tile_of[f"ada{l}"] + j, mat, step_of(it, j, 6) * 256, 256, it=it, per=6)
                for j in range(6):
                    tile(None, j)
                with sp.Fori(1, 4) as it:
                    for j in range(6):
                        tile(it, j)

            def ffn(t0, gate, up, down, steps=FSTEPS):
                def pair(t, s, it):
                    e = s // FSTEPS if steps > FSTEPS else 0
                    for i, mat in enumerate((gate, up)):
                        rows = mat[bass.ds(e * D, D)] if steps > FSTEPS else mat
                        load_cols(t + i, rows, (s % FSTEPS) * 256, 256, it=it, per=6)

                pair(t0, 0, None)

                def body(it, j):
                    s = step_of(it, j, 2)
                    t = t0 + 2 + 3 * j
                    pair(t, s + 1, it)
                    load_rows(t + 2, down, s * 256, it=it, per=6)
                repeat(sp, steps - 1, 2, body)
                load_rows(t0 + 3 * steps - 1, down, (steps - 1) * 256)

            def stage_prep():
                sp.dma_start(cst[:], const).then_inc(S("params_in"), 16)
                sp.wait_ge(S("prow_zero"), 1)
                for dst, src in prow_dmas:
                    sp.dma_start(dst, src).then_inc(S("params_in"), 16)
                sp.dma_start(xtok[:], w["x"][0].rearrange("(a p) d -> p a d", p=P)).then_inc(S("x_in"), 16)
                for i, name in enumerate(("mlstm_wq", "mlstm_wk", "mlstm_wv")):
                    src = w[name][0].rearrange("(c n) i o -> (n i) c o", n=32)
                    sp.dma_start(qkv_small[:, i], src).then_inc(S("mlstm_small_in"), 16)
                sp.dma_start(wgates[:], w["mlstm_w_gates"][0].rearrange("(c p) g -> p c g", p=P)
                             ).then_inc(S("mlstm_small_in"), 16)

            def stage_ada0():
                ada(0, w["ada_w"][0])

            def stage_mlstm():
                t0 = tile_of["m_in"]
                for j in range(16):
                    load_cols(t0 + j, w["mlstm_w_in"][0], 256 * j, 256)
                t0 = tile_of["m_out"]
                for j in range(8):
                    load_cols(t0 + j, w["mlstm_w_out"][0], 256 * (j // 2), 256, k0=8 * (j % 2))

            def stage_ffn0():
                w13 = w["ffn_w13"][0]
                ffn(tile_of["ffn0"], w13[:, 0:FF], w13[:, FF:2 * FF], w["ffn_w2"][0])

            def stage_s5():
                sp.wait_ge(S("ffn0_in_ready"), 1)
                sp.dma_start(router_w[:], w["moe_router"][0].rearrange("(c p) e -> p c e", p=P)).then_inc(S("s5_in"), 16)
                for i, name in enumerate(("s5_b_re", "s5_b_im")):
                    sp.dma_start(bmat[:, i], w[name][0].rearrange("(j g) p h -> (g p) j h", g=2)).then_inc(S("s5_in"), 16)
                for i, name in enumerate(("s5_c_re", "s5_c_im")):
                    for d in range(2):
                        sp.dma_start(ctok[:, i, :, d], w[name][0].rearrange("(c g) h p -> (g h) c p", g=8)
                                     ).then_inc(S("s5_in"), 16)
                log_dt = w["s5_log_dt"].rearrange("o (j g) -> g (o j)", g=2)
                for g in range(2):
                    sp.dma_start(sv[g * SP_:(g + 1) * SP_, 0], log_dt[g:g + 1].broadcast_to([SP_, NPAIR]),
                                 allow_slow_non_contiguous=True
                                 ).then_inc(S("s5_in"), 16)
                ada(1, w["ada_w"][1])
                t0, glu = tile_of["glu"], w["s5_w_glu"][0]
                for j in range(4):
                    load_cols(t0 + 2 * j, glu, 256 * j, 256)
                    load_cols(t0 + 2 * j + 1, glu, D + 256 * j, 256)

            def stage_moe():
                w13 = w["moe_w13"][0].rearrange("e k n -> (e k) n")
                ffn(tile_of["moe"], w13[:, 0:FF], w13[:, FF:2 * FF], w["moe_w2"][0].rearrange("e k n -> (e k) n"),
                    FSTEPS * NE)

            def stage_mla():
                sp.wait_ge(S("moe_done"), 1)
                sp.dma_start(ctx_tok, w["ctx_2"][0].rearrange("(a p) d -> p a d", p=P)).then_inc(S("ctx_in"), 16)
                ada(2, w["ada_w_2"][0])
                mat, t = w["mla_w_in_2"][0], tile_of["mla_in"]
                load_cols(t, mat, 0, 256)
                load_cols(t + 1, mat, 256, 256)
                load_cols(t + 2, mat, 512, 192)
                mat, t = w["mla_w_uq_2"][0], tile_of["mla_uq"]
                for i in range(3):
                    load_cols(t + i, mat, 576 * i, 576 if i < 2 else 384, kc=QR // P)
                mat, t = w["mla_w_ukv_2"][0], tile_of["mla_ukv"]
                for i in range(2):
                    load_cols(t + i, mat, 1024 * i, 1024, kc=KVR // P)
                for i in range(4):
                    load_cols(tile_of["mla_o"] + i, w["mla_w_o_2"][0], 256 * i, 256)

            def stage_ffn2():
                t0 = tile_of["ffn2"]

                def body(it, j):
                    s = step_of(it, j, 3)
                    load_cols(t0 + 2 * j, w["ffn_w1_2"][0], s * 256, 256, it=it, per=6)
                    load_cols(t0 + 2 * j + 1, w["ffn_w3_2"][0], s * 256, 256, it=it, per=6)
                repeat(sp, FSTEPS, 3, body)
                for i in range(12):
                    k0 = 4 * (i % 6)
                    load_cols(t0 + 22 + i, w["ffn_w2_2"][0], 512 * (i // 6), 512, k0=k0, kc=min(4, FC - k0))

            def stage_hg():
                ada(3, w["ada_w_2"][1])
                mat = w["hg_w_in_2"][0]
                for i in range(4):
                    load_cols(tile_of["hg_q"] + i, mat, 256 * i, 256)
                for i in range(8):
                    load_cols(tile_of["hg_z"] + i, mat, D + 256 * i, 256)
                for i in range(4):
                    load_cols(tile_of["hg_i"] + i, mat, 3 * D + 256 * i, 256)
                for i in range(4):
                    load_cols(tile_of["hg_g"] + i, mat, 4 * D + 256 * i, 256)
                for i in range(4):
                    load_cols(tile_of["hg_o"] + i, w["hg_w_o_2"][0], 256 * i, 256)

            def stage_ffn3():
                ffn(tile_of["ffn3"], w["ffn_w1_2"][1], w["ffn_w3_2"][1], w["ffn_w2_2"][1])

            def stage_out():
                sp.wait_ge(S("out_tok_ready"), 1)
                sp.dma_start(out[0].rearrange("(a p) d -> p a d", p=P), out_tok).then_inc(S("out_written"), 16)
                sp.wait_ge(S("out_written"), 16)

            stage_prep()
            stage_ada0()
            stage_mlstm()
            stage_ffn0()
            stage_s5()
            stage_moe()
            stage_mla()
            stage_ffn2()
            stage_hg()
            stage_ffn3()
            stage_out()

        @block.tensor
        def _(pe):
            def mm_pair(t, j, src, kc=DC, start=True, stop_=True, it=None, per_t=0, per_j=0, width=256):
                wait_tile(pe, t, it, per_t)
                wait_free(pe, j, it, per_j)
                tile = ring[:, t % RING, :]
                for n in range(2):
                    for k in range(kc):
                        last = pe.matmul(bank(j)[:, n * T:(n + 1) * T],
                                         tile[:, k * width + n * P:k * width + (n + 1) * P], src(k),
                                         start=start and k == 0, stop=stop_ and k == kc - 1)
                        if n == 0 and k == 0:
                            last.then_inc(tile_begun, 1)
                full(last, j)

            def stats(j, src, n, width=T, rows=P):
                wait_free(pe, j)
                for k in range(n):
                    last = pe.matmul(bank(j)[0:rows, 0:width], ones[0:rows, 0:rows], src(k), start=k == 0, stop=k == n - 1)
                full(last, j)

            def turn(j, srcs, rows=P):
                wait_free(pe, j)
                for i, src in enumerate(srcs):
                    n = src.shape[0]
                    m = src.free_size()
                    last = pe.transpose(bank(j)[0:m, i * P:i * P + n], src, ident[0:n, 0:n])
                full(last, j)

            def ada(l, who, n):
                j = job_of[f"ada{l}"]
                pe.wait_ge(S("csil_ready"), 1)
                wait_free(pe, j)

                def body(it, i):
                    t = tile_of[f"ada{l}"] + i
                    wait_tile(pe, t, it, 6)
                    for m in range(2):
                        at = step_of(it, i, 6) * 2 * n + m * n
                        for k in range(DC):
                            last = pe.matmul(bank(j)[:, bass.ds(at, n)],
                                             ring[:, t % RING, k * 256 + m * P:k * 256 + (m + 1) * P],
                                             csil[:, k, who:who + n], start=k == 0, stop=k == DC - 1)
                            if m == 0 and k == 0:
                                last.then_inc(tile_begun, 1)
                repeat(pe, 24, 6, body)
                pe.matmul(bank(j)[0:1, 511:512], ident[:, 0:1], ident[:, 0:1], start=True, stop=True
                          ).then_inc(bank_full[j % NB], 1)

            def layer_norm(i):
                pe.wait_ge(S("ln_sum_ready"), i + 1)
                stats(job_of[f"ln{i}"], lambda k: res[:, k], DC)
                pe.wait_ge(S("ln_sq_ready"), i + 1)
                stats(job_of[f"ln{i}"] + 1, lambda k: sqr[:, k], DC)

            def ffn(name, steps, ready):
                hid = ffn_bufs[name][0]
                t0, j0 = tile_of[name], job_of[name]
                ready()
                for b in range(4):
                    pe.matmul(psum[:, NB + b, :], zeros[:], cst[:, 0:BANK],
                              start=True, stop=False, skip_group_check=True)
                mm_pair(t0, j0, lambda k: act_in[:, k])
                mm_pair(t0 + 1, j0 + 1, lambda k: act_in[:, k])

                def down(t, i, it, last_step=False):
                    wait_tile(pe, t, it, 6)
                    wait_out(pe, j0 + 2 * i + 1, it, 4)
                    for n in range(DC):
                        for k in range(2):
                            last = pe.matmul(psum[:, NB + n // 2, (n % 2) * T:(n % 2 + 1) * T],
                                             ring[:, t % RING, k * D + n * P:k * D + (n + 1) * P],
                                             hid[:, i % 2, k], start=False, stop=last_step and k == 1,
                                             skip_group_check=True)
                            if n == 0 and k == 0:
                                last.then_inc(tile_begun, 1)
                    last.then_inc(S(f"{name}_down"), 1)

                def body(it, i):
                    t, j = t0 + 2 + 3 * i, j0 + 2 + 2 * i
                    mm_pair(t, j, lambda k: act_in[:, k], it=it, per_t=6, per_j=4)
                    mm_pair(t + 1, j + 1, lambda k: act_in[:, k], it=it, per_t=6, per_j=4)
                    down(t + 2, i, it)
                repeat(pe, steps - 1, 2, body)
                down(t0 + 3 * steps - 1, steps - 1, None, True)

            def stage_prep():
                pe.wait_ge(S("params_in"), 16 * (1 + len(prow_dmas)))
                for g in range(5):
                    turn(job_of["params"] + g, [prow[:, g, :]])
                pe.wait_ge(S("x_in"), 16)
                for g in range(4):
                    turn(job_of["xT"] + g, [xtok[:, a, (2 * g + d) * P:(2 * g + d + 1) * P]
                                            for d in range(2) for a in range(2)])

            def stage_ada0():
                ada(0, 0, 1)

            def stage_mlstm():
                pe.wait_ge(S("mlstm_in_ready"), 1)
                for j in range(16):
                    mm_pair(tile_of["m_in"] + j, job_of["m_in"] + j, lambda k: act_in[:, k])
                pe.wait_ge(S("block_diag_ready"), 3)
                for c in range(IC):
                    j = job_of["m_qk"] + c
                    pe.wait_ge(S("conv_ready"), c + 1)
                    wait_free(pe, j)
                    for i in range(2):
                        last = pe.matmul(bank(j)[:, i * T:(i + 1) * T], bd[:, i, c], xc[:, c], start=True, stop=True)
                    full(last, j)
                for g in range(8):
                    j = job_of["m_vT"] + g
                    wait_free(pe, j)
                    for i in range(2):
                        last = pe.matmul(bank(j)[:, i * T:(i + 1) * T], bd[:, 2, 2 * g + i], xm[:, 2 * g + i, 4:4 + T],
                                         start=True, stop=True)
                    full(last, j)
                j = job_of["m_gates"]
                wait_free(pe, j)
                wait_out(pe, job_of["m_qk"] + IC - 1)
                wait_out(pe, job_of["m_vT"] + 7)
                for i in range(3):
                    for c in range(IC):
                        src = vT[:, c] if i == 2 else qk[:, c, i]
                        last = pe.matmul(bank(j)[0:8, 0:T], wgates[:, i * IC + c], src,
                                         start=i == 0 and c == 0, stop=i == 2 and c == IC - 1)
                full(last, j)
                j = job_of["m_fsel"]
                wait_free(pe, j)
                wait_out(pe, job_of["m_gates"])
                full(pe.matmul(bank(j)[0:NH, 0:T], ident[0:8, NH:2 * NH], gate_rows[0:8, 0], start=True, stop=True), j)
                j = job_of["m_cT"]
                wait_free(pe, j)
                pe.wait_ge(S("gate_rows_ready"), 1)
                for a in range(2):
                    last = pe.matmul(bank(j)[:, a * NH:(a + 1) * NH], gate_rows[0:NH, 4, a * P:(a + 1) * P],
                                     ident[0:NH, 0:NH], start=True, stop=True)
                full(last, j)
                for h in range(NH):
                    j = job_of["m_rows"] + h
                    wait_free(pe, j)
                    full(pe.matmul(bank(j), ident[0:NH, h:h + 1].broadcast_to([NH, P]),
                                   gate_rows[0:NH, 5:7].rearrange("p a t -> p (a t)"), start=True, stop=True), j)
                for g in range(8):
                    a, c0 = g // 4, 4 * (g % 4)
                    j = job_of["m_v"] + g
                    wait_free(pe, j)
                    for c in range(4):
                        last = pe.matmul(bank(j)[:, c * P:(c + 1) * P], xm[:, c0 + c, 4 + a * P:4 + (a + 1) * P],
                                         bd[:, 2, c0 + c], start=True, stop=True)
                    full(last, j)
                for h in range(NH):
                    j = job_of["m_head"] + 4 * h
                    wait_free(pe, j)
                    for s in range(2):
                        for c in range(HC):
                            last = pe.matmul(bank(j)[:, s * T:(s + 1) * T], qk[:, h * HC + c, 1, s * P:(s + 1) * P],
                                             qk[:, h * HC + c, 0], start=c == 0, stop=c == HC - 1)
                    full(last, j)
                    wait_out(pe, j)
                    stats(j + 1, lambda s: scor[:, h % 2, s], 2)
                    wait_out(pe, job_of["m_v"] + 7)
                    for g in range(2):
                        wait_free(pe, j + 2 + g)
                        for e in range(2):
                            for s in range(2):
                                at = h * DH + (2 * g + e) * P
                                last = pe.matmul(bank(j + 2 + g)[:, e * T:(e + 1) * T], vbuf[:, s, at:at + P],
                                                 scor[:, h % 2, s], start=s == 0, stop=s == 1)
                        full(last, j + 2 + g)
                for h in range(NH):
                    j = job_of["m_norm"] + 2 * h
                    wait_out(pe, job_of["m_head"] + 4 * h + 3)
                    stats(j, lambda k: hT[:, h * HC + k], HC)
                    pe.wait_ge(S("h_sq_ready"), h + 1)
                    stats(j + 1, lambda k: vT[:, (h % 2) * HC + k], HC)
                pe.wait_ge(S("h_out_ready"), 1)
                for g in range(4):
                    t, j = tile_of["m_out"] + 2 * g, job_of["m_out"] + g
                    wait_tile(pe, t)
                    wait_tile(pe, t + 1)
                    wait_free(pe, j)
                    for n in range(2):
                        for k in range(IC):
                            last = pe.matmul(bank(j)[:, n * T:(n + 1) * T],
                                             ring[:, (t + k // 8) % RING, (k % 8) * 256 + n * P:(k % 8) * 256 + (n + 1) * P],
                                             hT[:, k], start=k == 0, stop=k == IC - 1)
                            if (n, k) in ((0, 0), (1, 8)):
                                last.then_inc(tile_begun, 1)
                    full(last, j)
                layer_norm(0)

            def stage_ffn0():
                ffn("ffn0", FSTEPS, lambda: pe.wait_ge(S("ffn0_in_ready"), 1))
                layer_norm(1)

            def stage_s5():
                ada(1, 0, 1)
                pe.wait_ge(S("bpad_ready"), 1)
                for g in range(4):
                    turn(job_of["s_bT"] + g, [bpad[:, g // 2, 4 * (g % 2) + i] for i in range(4)])
                pe.wait_ge(S("s5_in"), 7 * 16)
                for g in range(4):
                    turn(job_of["s_cT"] + g, [ctok[:, g // 2, 4 * (g % 2) + i].rearrange("p d s -> p (d s)")
                                              for i in range(4)])
                pe.wait_ge(S("s5_u_ready"), 1)
                wait_out(pe, job_of["s_cT"] + 3)

                def drive(p):
                    c, r = p // 4, 32 * (p % 4)
                    j = job_of["s_pair"] + p
                    wait_free(pe, j)
                    for i in range(2):
                        last = pe.matmul(bank(j)[:, i * T:(i + 1) * T], bT[r:r + 32, i, c], act_in[r:r + 32, c],
                                         start=True, stop=True)
                    full(last, j)

                drive(0)
                drive(1)
                for p in range(NPAIR):
                    if p + 2 < NPAIR:
                        drive(p + 2)
                    c, r = p // 4, 32 * (p % 4)
                    pe.wait_ge(S("s5_x_ready"), p + 1)
                    if p % 4 == 0 and c >= 2:
                        pe.wait_ge(S("s5_y_out"), c - 1)
                    for i in range(2):
                        last = pe.matmul(psum[r:r + 32, NB + c % 2, 0:T], cmT[:, i, c, r:r + 32], xri[:, p % 2, i],
                                         start=i == 0, stop=i == 1)
                    last.then_inc(S("s5_x_used"), 1)
                pe.wait_ge(S("gelu_ready"), DC)
                for j in range(8):
                    mm_pair(tile_of["glu"] + j, job_of["glu"] + j, lambda k: gT[:, k])
                layer_norm(2)

            def stage_moe():
                pe.wait_ge(S("moe_in_ready"), 1)
                j = job_of["router"]
                wait_free(pe, j)
                for a in range(2):
                    for k in range(DC):
                        last = pe.matmul(bank(j)[:, a * NE:(a + 1) * NE], act_in[:, k, a * P:(a + 1) * P], router_w[:, k],
                                         start=k == 0, stop=k == DC - 1)
                full(last, j)
                pe.wait_ge(S("top2_ready"), 1)
                turn(job_of["gateT"], [lg[:, 6, 0], lg[:, 6, 1]])
                wait_out(pe, job_of["gateT"])
                for g in range(4):
                    j = job_of["gates"] + g
                    wait_free(pe, j)
                    for i in range(2):
                        last = pe.matmul(bank(j)[:, i * T:(i + 1) * T],
                                         ident[0:NE, 2 * g + i:2 * g + i + 1].broadcast_to([NE, P]), gate8[0:NE],
                                         start=True, stop=True)
                    full(last, j)
                ffn("moe", FSTEPS * NE, lambda: None)
                layer_norm(3)

            def mm_wide(j, t, col0, rows, src, kc, width, first):
                wait_free(pe, j)
                for k in range(kc):
                    at = k * width + col0
                    last = pe.matmul(bank(j)[0:rows], ring[:, t % RING, at:at + rows], src(k), start=k == 0, stop=k == kc - 1)
                    if first and k == 0:
                        last.then_inc(tile_begun, 1)
                full(last, j)

            def rms2(i, srcs):
                pe.wait_ge(S("rms_sq_ready"), i + 1)
                j = job_of[f"rms{i}"]
                wait_free(pe, j)
                for n, src in enumerate(srcs):
                    for k in range(DC):
                        last = pe.matmul(bank(j)[:, n * T:(n + 1) * T], ones, src(k), start=k == 0, stop=k == DC - 1)
                full(last, j)

            def stage_mla():
                pe.wait_ge(S("ctx_in"), 16)
                for g in range(4):
                    turn(job_of["ctxT"] + g, [ctx_tok[:, a, (2 * g + d) * P:(2 * g + d + 1) * P]
                                              for d in range(2) for a in range(2)])
                ada(2, 1, 2)
                rms2(0, [lambda k: rms_sq[:, k, 0:T], lambda k: rms_sq[:, k, T:T2]])
                pe.wait_ge(S("a2_ready"), 1)
                for key in MLA_SEQ:
                    kind, m, c = key
                    j = mla_job[key]
                    if kind == "V":
                        t = tile_of["mla_ukv"] + m
                        wait_free(pe, j)
                        for k in range(2):
                            cols4 = ring[:, t % RING, k * 1024:(k + 1) * 1024].rearrange("p (h n) -> p h n", n=256)[:, :, P:]
                            last = pe.matmul(bank(j).rearrange("p (h n) -> p h n", n=P), ckv[:, k, c * P:(c + 1) * P],
                                             cols4, start=k == 0, stop=k == 1)
                        full(last, j)
                        continue
                    name, h, n, rows, dst, weight, slots = item_of(m)
                    if kind == "S":
                        pe.wait_ge(S("nsq_ready"), m + 1)
                        stats(j, lambda k: nsq[0:rows, slots[k]], n, T2, rows)
                        continue
                    if name in ("cq", "ckv", "kr"):
                        n0 = c + {"cq": 0, "ckv": 3, "kr": 5}[name]
                        t = tile_of["mla_in"] + n0 // 2
                        if n0 % 2 == 0:
                            wait_tile(pe, t)
                        mm_wide(j, t, P * (n0 % 2), rows, lambda k: a2[:, k], DC, 192 if n0 >= 4 else 256, n0 % 2 == 0)
                    elif name in ("qn", "qr"):
                        if h == 0:
                            pe.wait_ge(S("item_normed"), 1)
                        t, first_ = tile_of["mla_uq"] + h // 3, name == "qn" and h % 3 == 0
                        if first_:
                            wait_tile(pe, t)
                        mm_wide(j, t, 192 * (h % 3) + (P if name == "qr" else 0), rows, lambda k: cq[:, k], 3,
                                384 if h >= 6 else 576, first_)
                    else:
                        if h == 0:
                            pe.wait_ge(S("item_normed"), 2)
                        t = tile_of["mla_ukv"] + h // 4
                        if h % 4 == 0:
                            wait_tile(pe, t)
                        mm_wide(j, t, 256 * (h % 4), rows, lambda k: ckv[:, k], 2, 1024, h % 4 == 0)
                pe.wait_ge(S("item_normed"), len(MLA_ITEMS))
                for i in range(AH + 1):
                    j = job_of["rope"] + i
                    wait_free(pe, j)
                    src = kr[0:ROPE, 0, 0:T] if i == 0 else qr[0:ROPE, i - 1, 0:T]
                    full(pe.matmul(bank(j)[0:ROPE, 0:T], c_("rotT")[0:ROPE], src, start=True, stop=True), j)
                pe.wait_ge(S("rope_ready"), AH + 1)
                for kind, h, k in ATTN_SEQ:
                    j = attn_job[kind, h, k]
                    if kind == "S":
                        wait_free(pe, j)
                        spans = [(k * P, 0, T2, 0)] if k < 2 else [(T + a * P, T, T, a * T) for a in range(2)]
                        for q0, k0, n, at in spans:
                            pe.matmul(bank(j)[:, at:at + n], qn[:, h, q0:q0 + P], kn[:, h, k0:k0 + n], start=True, stop=False)
                            last = pe.matmul(bank(j)[:, at:at + n], qr[0:ROPE, h, q0:q0 + P], kr[0:ROPE, 0, k0:k0 + n],
                                             start=False, stop=True)
                        full(last, j)
                    elif kind == "T":
                        pe.wait_ge(S("prob_ready"), 3 * h + k + 1)
                        turn(j, [prob[:, h % 2, k, s * P:(s + 1) * P] for s in range(4)])
                    else:
                        wait_out(pe, attn_job["T", h, 2])
                        wait_free(pe, j)
                        for s in range(4):
                            pe.matmul(bank(j)[:, 0:T], vtok[:, s, h * P:(h + 1) * P], probTs[h % 2][:, s],
                                      start=s == 0, stop=s == 3)
                        for s in range(2):
                            last = pe.matmul(bank(j)[:, T:T2], vtok[:, 2 + s, h * P:(h + 1) * P], probTs[h % 2][:, 4 + s],
                                             start=s == 0, stop=s == 1)
                        full(last, j)
                wait_out(pe, attn_job["O", AH - 1, 0])
                for i in range(8):
                    t = tile_of["mla_o"] + i // 2
                    if i % 2 == 0:
                        wait_tile(pe, t)
                    mm_wide(job_of["mla_o"] + i, t, P * (i % 2), P, lambda k: oT[:, k], DC, 256, i % 2 == 0)

            def stage_ffn2():
                rms2(1, [lambda k: rms_sq2[:, k, 0:T], lambda k: rms_sq2[:, k, T:T2]])
                pe.wait_ge(S("a2_ready"), 2)
                t0, j0 = tile_of["ffn2"], job_of["ffn2"]

                def body(it, i):
                    for half in range(2):
                        t = t0 + 2 * i + half
                        wait_tile(pe, t, it, 6)
                        for n in range(2):
                            j = j0 + 4 * i + 2 * half + n
                            wait_free(pe, j, it, 12)
                            for k in range(DC):
                                last = pe.matmul(bank(j), ring[:, t % RING, k * 256 + n * P:k * 256 + (n + 1) * P],
                                                 a2[:, k], start=k == 0, stop=k == DC - 1)
                                if n == 0 and k == 0:
                                    last.then_inc(tile_begun, 1)
                            full(last, j)
                repeat(pe, FSTEPS, 3, body)
                for i in range(12):
                    t, k0 = t0 + 22 + i, 4 * (i % 6)
                    wait_tile(pe, t)
                    if i == 0:
                        wait_out(pe, j0 + 4 * FSTEPS - 1)
                    if i == 6:
                        pe.wait_ge(S("ffn2_out"), 1)
                    kc = min(4, FC - k0)
                    for k in range(kc):
                        for n in range(4):
                            last = pe.matmul(psum[:, NB + n], ring[:, t % RING, k * 512 + n * P:k * 512 + (n + 1) * P],
                                             hid2[:, k0 + k], start=k0 + k == 0, stop=k0 + k == FC - 1)
                            if n == 0 and k == 0:
                                last.then_inc(tile_begun, 1)
                    if i % 6 == 5:
                        last.then_inc(S("ffn2_sum"), 1)

            def stage_hg():
                ada(3, 1, 2)
                rms2(2, [lambda k: rms_sq[:, k, 0:T], lambda k: rms_sq[:, k, T:T2]])
                pe.wait_ge(S("a2_ready"), 3)
                for i in range(4):
                    mm_pair(tile_of["hg_q"] + i, job_of["hg_q"] + i, lambda k: a2[:, k, 0:T])
                for i in range(16):
                    t = tile_of["hg_z"] + i // 2
                    if i % 2 == 0:
                        wait_tile(pe, t)
                    mm_wide(job_of["hg_z"] + i, t, P * (i % 2), P, lambda k: a2[:, k], DC, 256, i % 2 == 0)
                for i in range(8):
                    t, j = tile_of["hg_i"] + i // 2, job_of["hg_i"] + i
                    if i % 2 == 0:
                        wait_tile(pe, t)
                    wait_free(pe, j)
                    for a in range(2):
                        tok = (2 * (i % 2) + a) * P
                        for k in range(DC):
                            last = pe.matmul(bank(j)[:, a * T:(a + 1) * T], a2[:, k, tok:tok + P],
                                             ring[:, t % RING, k * 256:(k + 1) * 256], start=k == 0, stop=k == DC - 1)
                            if i % 2 == 0 and a == 0 and k == 0:
                                last.then_inc(tile_begun, 1)
                    full(last, j)
                for i in range(4):
                    mm_pair(tile_of["hg_g"] + i, job_of["hg_g"] + i, lambda k: a2[:, k, 0:T])
                for i in range(8):
                    if i % 4 == 0:
                        pe.wait_ge(S("ctx_keys_ready"), i // 4 + 1)
                    turn(job_of["hg_wk"] + i, [kf[:, i // 4, 2 * (i % 4) + h, T + a * P:T + (a + 1) * P]
                                               for h in range(2) for a in range(2)])
                wait_out(pe, job_of["hg_wk"] + 7)
                for i in range(4):
                    j = job_of["hg_state"] + i
                    wait_free(pe, j)
                    for n in range(4):
                        m = 4 * i + n
                        for a in range(2):
                            last = pe.matmul(bank(j)[:, n * P:(n + 1) * P], wkT[:, 2 * m + a],
                                             itok[:, 2 + a, (m % AH) * P:(m % AH + 1) * P], start=a == 0, stop=a == 1)
                    full(last, j)
                for b in range(4):
                    pe.matmul(psum[:, NB + b, :], zeros[:], cst[:, 0:BANK], start=True, stop=False, skip_group_check=True)
                pe.wait_ge(S("q_decayed"), 1)
                wait_out(pe, job_of["hg_state"] + 3)

                def o_at(h, a=0, n=T):
                    return psum[:, NB + h // 2, (h % 2) * T + a:(h % 2) * T + a + n]

                for h in range(AH):
                    for d in range(2):
                        last = pe.matmul(o_at(h), state[:, d, h, T:T + P], ework[:, d, h], start=False, stop=False,
                                         skip_group_check=True)
                last.then_inc(S("q_decayed_used"), 1)

                def read_out(n):
                    lev, g = n // 4, n % 4
                    j = job_of["hg_level"] + n
                    wait_out(pe, j)
                    for i in range(4):
                        h, a = 2 * g + i // 2, i % 2
                        s = 1 - a if lev == 0 else a
                        last = pe.matmul(o_at(h, a * P, P), itok[:, s, h * P:(h + 1) * P], atts[:, n % 2, i],
                                         start=False, stop=n == 4 * n_lev - 1, skip_group_check=True)
                    last.then_inc(S("att_used"), 1)

                n_lev = len(LEVELS) + 2
                for lev in range(n_lev):
                    pe.wait_ge(S("level_ready"), lev + 1)
                    for g in range(4):
                        n = 4 * lev + g
                        j = job_of["hg_level"] + n
                        wait_free(pe, j)
                        for i in range(4):
                            h, a = 2 * g + i // 2, i % 2
                            s = 1 - a if lev == 0 else a
                            eq = qh if lev == n_lev - 1 else eworks[lev % 2][:, 0]
                            ek = eworks[lev % 2][:, 1]
                            last = pe.matmul(bank(j)[:, i * P:(i + 1) * P], ek[:, h, s * P:(s + 1) * P],
                                             eq[:, h, a * P:(a + 1) * P], start=True, stop=True)
                        full(last, j)
                        if n >= 1:
                            read_out(n - 1)
                read_out(4 * n_lev - 1)
                for i in range(4):
                    j = job_of["hg_norm"] + i
                    pe.wait_ge(S("o_sq_ready"), i + 1)
                    wait_free(pe, j)
                    for h in range(2):
                        last = pe.matmul(bank(j)[:, h * T:(h + 1) * T], ones, ework[:, 0, 2 * i + h], start=True, stop=True)
                    full(last, j)
                pe.wait_ge(S("hg_o_ready"), 1)
                for i in range(4):
                    mm_pair(tile_of["hg_o"] + i, job_of["hg_o"] + i, lambda k: ework[:, 1, k])

            def stage_ffn3():
                rms2(3, [lambda k: rms_sq3[:, k]])
                ffn("ffn3", FSTEPS, lambda: pe.wait_ge(S("ffn3_in_ready"), 1))

            def stage_out():
                pe.wait_ge(S("x_final"), 1)
                for g in range(4):
                    a = g // 2
                    turn(job_of["outT"] + g, [xT[:, 4 * (g % 2) + c, a * P:(a + 1) * P] for c in range(4)])

            stage_prep()
            stage_ada0()
            stage_mlstm()
            stage_ffn0()
            stage_s5()
            stage_moe()
            stage_mla()
            stage_ffn2()
            stage_hg()
            stage_ffn3()
            stage_out()

        @block.scalar
        def _(act):
            def layer_norm(i):
                wait_out(act, job_of[f"ln{i}"])
                act.activation(sqr[:], res[:], ACT.Square).then_inc(S("ln_sq_ready"), 1)
                wait_out(act, job_of[f"ln{i}"] + 1)
                act.activation(stat[:, 0], stat[:, 0], ACT.Sqrt).then_inc(S("ln_std_ready"), 1)

            def silu_steps(name, steps):
                sil = ffn_bufs[name][1]

                def body(it, i):
                    j = job_of[name] + 2 * i
                    wait_full(act, j, it, 4)
                    if it is not None or i >= 2:
                        wait_out(act, j - 3, it, 4)
                    out_of(act.activation(sil[:, i % 2].rearrange("p a t -> p (a t)"), bank(j), ACT.Silu), j)
                body(None, 0)
                body(None, 1)
                after_two(act, steps, 2, body)

            def stage_prep():
                wait_out(act, job_of["params"] + 4)
                for i, name in enumerate(("c", "c_2", "c_ctx_2")):
                    last = act.activation(csil[:, :, i], col(name, 0, DC), ACT.Silu)
                last.then_inc(S("csil_ready"), 1)

            def stage_mlstm():
                for i in range(16):
                    j = job_of["m_in"] + i
                    wait_full(act, j)
                    src = bank(j).rearrange("p (a t) -> p a t", a=2)
                    if i < 8:
                        out_of(act.activation(xm[:, 2 * i:2 * i + 2, 4:4 + T], src, ACT.Copy), j)
                    else:
                        out_of(act.activation(zs[:, 2 * i - 16:2 * i - 14], src, ACT.Silu), j)
                for c in range(IC):
                    act.wait_ge(S("conv_sum_ready"), c + 1)
                    act.activation(xc[:, c], xc[:, c], ACT.Silu, bias=col("mlstm_conv_b", c)).then_inc(S("conv_ready"), 1)
                    if c >= 2:
                        j = job_of["m_qk"] + c - 2
                        wait_full(act, j)
                        out_of(act.activation(qk[:, c - 2], bank(j).rearrange("p (a t) -> p a t", a=2), ACT.Copy), j)
                for c in range(IC - 2, IC):
                    j = job_of["m_qk"] + c
                    wait_full(act, j)
                    out_of(act.activation(qk[:, c], bank(j).rearrange("p (a t) -> p a t", a=2), ACT.Copy), j)
                for g in range(8):
                    j = job_of["m_vT"] + g
                    wait_full(act, j)
                    out_of(act.activation(vT[:, 2 * g:2 * g + 2], bank(j).rearrange("p (a t) -> p a t", a=2), ACT.Copy), j)
                wait_out(act, job_of["m_fsel"])
                act.activation(gate_rows[0:NH, 2], gate_rows[0:NH, 2], ACT.Exp)
                act.drain()
                act.activation(gate_rows[0:NH, 2], gate_rows[0:NH, 2], ACT.Ln, bias=one[0:NH, :]).then_inc(S("ln_f_ready"), 1)
                act.wait_ge(S("m_sum_ready"), 1)
                act.activation(gate_rows[0:NH, 6], gate_rows[0:NH, 6], ACT.Exp, scale=-1.0).then_inc(S("gate_rows_ready"), 1)
                for h in range(NH):
                    for s in range(2):
                        act.wait_ge(S("decay_sum_ready"), 2 * h + s + 1)
                        act.activation(decay[:, s], decay[:, s], ACT.Exp, bias=cT[:, s, h:h + 1]).then_inc(S("decay_ready"), 1)
                for h in range(NH):
                    wait_out(act, job_of["m_norm"] + 2 * h)
                    act.activation(vT[:, (h % 2) * HC:(h % 2 + 1) * HC], hT[:, h * HC:(h + 1) * HC], ACT.Square
                                   ).then_inc(S("h_sq_ready"), 1)
                    wait_out(act, job_of["m_norm"] + 2 * h + 1)
                    act.activation(stat[:, h % 2], stat[:, h % 2], ACT.Sqrt).then_inc(S("h_std_ready"), 1)
                layer_norm(0)

            def stage_ffn0():
                silu_steps("ffn0", FSTEPS)
                layer_norm(1)

            def stage_s5():
                act.wait_ge(S("s5_in"), 7 * 16 + 16 * 2)
                act.activation(sv[:, 0], sv[:, 0], ACT.Exp).then_inc(S("dt_ready"), 1)
                act.wait_ge(S("theta_ready"), 1)
                act.activation(sv[:, 3], sv[:, 3], ACT.Exp)
                for i in (5, 6):
                    last = act.activation(sv[:, i], sv[:, i], ACT.Sin)
                last.then_inc(S("sin_ready"), 1)
                for c in range(DC):
                    act.wait_ge(S("s5_y_out"), c + 1)
                    act.activation(gT[:, c], gT[:, c], ACT.Gelu_apprx_tanh).then_inc(S("gelu_ready"), 1)
                for i in range(4):
                    j = job_of["glu"] + 2 * i + 1
                    wait_full(act, j)
                    if i >= 2:
                        wait_out(act, job_of["glu"] + 2 * (i - 2))
                    for n in range(2):
                        last = act.activation(sil[:, i % 2, n], bank(j)[:, n * T:(n + 1) * T], ACT.Sigmoid,
                                              bias=col("s5_b_glu", DC + 2 * i + n))
                    out_of(last, j)
                layer_norm(2)

            def stage_moe():
                act.wait_ge(S("logits_ready"), 1)
                act.activation(lg[:, 1], lg[:, 1], ACT.Exp).then_inc(S("exp_logits_ready"), 1)
                silu_steps("moe", FSTEPS * NE)
                layer_norm(3)

            def rms2(i, dst):
                act.wait_ge(S("x2_ready"), i + 1)
                for n in range(len(dst)):
                    last = act.activation(dst[n], halves[n][:], ACT.Square)
                last.then_inc(S("rms_sq_ready"), 1)
                wait_out(act, job_of[f"rms{i}"])
                n = T * len(dst)
                act.activation(rstd2[:, 0:n], rstd2[:, 0:n], ACT.Sqrt).then_inc(S("rms_std_ready"), 1)

            def stage_mla():
                rms2(0, [rms_sq[:, :, 0:T], rms_sq[:, :, T:T2]])

                def root(m):
                    rows = item_of(m)[3]
                    wait_out(act, mla_job["S", m, 0])
                    act.activation(nstat[0:rows, m % 2], nstat[0:rows, m % 2], ACT.Sqrt).then_inc(S("nstd_ready"), 1)

                rooted, last_use = 0, {}
                for kind, m, c in MLA_SEQ:
                    j = mla_job[kind, m, c]
                    if kind == "V":
                        wait_full(act, j)
                        out_of(act.activation(vtok[:, c, 512 * m:512 * m + 512], bank(j), ACT.Copy), j)
                    elif kind == "P":
                        name, h, n, rows, dst, weight, slots = item_of(m)
                        wait_full(act, j)
                        if slots[c] in last_use:
                            wait_full(act, mla_job["S", last_use[slots[c]], 0])
                        last_use[slots[c]] = m
                        at = c if n > 1 else h
                        act.activation(dst[0:rows, at], bank(j)[0:rows], ACT.Copy)
                        out_of(act.activation(nsq[0:rows, slots[c]], bank(j)[0:rows], ACT.Square), j)
                        if c == n - 1:
                            act.drain().then_inc(S("nsq_ready"), 1)
                    else:
                        root(m)
                for kind, h, k in ATTN_SEQ:
                    j = attn_job[kind, h, k]
                    wait_full(act, j)
                    if kind == "S":
                        act.wait_ge(S("max_ready"), 3 * h + k + 1)
                        for a in range(1 if k < 2 else 2):
                            n = T2 if k < 2 else T
                            last = act.activation(prob[:, h % 2, k, a * n:(a + 1) * n], bank(j)[:, a * n:(a + 1) * n],
                                                  ACT.Exp, bias=smax[:, h % 2, 2 * k + a:2 * k + a + 1], scale=ATT_SCALE)
                        out_of(last, j)
                    elif kind == "T":
                        src = bank(j).rearrange("p (s t) -> p s t", t=P)
                        if k < 2:
                            out_of(act.activation(probTs[h % 2][:, 0:4, k * P:(k + 1) * P], src, ACT.Copy), j)
                        else:
                            out_of(act.activation(probTs[h % 2][:, 4:6].rearrange("p s (a t) -> p a s t", a=2),
                                                  bank(j).rearrange("p (a s t) -> p a s t", a=2, s=2), ACT.Copy), j)
                    else:
                        out_of(act.activation(oT[:, h], bank(j), ACT.Copy), j)

            def stage_ffn2():
                rms2(1, [rms_sq2[:, :, 0:T], rms_sq2[:, :, T:T2]])
                j0 = job_of["ffn2"]

                def body(it, i):
                    for n in range(2):
                        j = j0 + 4 * i + n
                        wait_full(act, j, it, 12)
                        if it is not None or i >= 1:
                            wait_out(act, j - 2, it, 12)
                        out_of(act.activation(sil2[:, n], bank(j), ACT.Silu), j)
                for i in range(3):
                    body(None, i)
                whole = (FSTEPS - 3) // 3
                with act.Fori(0, whole) as it:
                    for i in range(3):
                        body(it, 3 + i)
                for i in range(3 + 3 * whole, FSTEPS):
                    body(None, i)

            def stage_hg():
                rms2(2, [rms_sq[:, :, 0:T], rms_sq[:, :, T:T2]])
                act.wait_ge(S("lb_logits_ready"), 1)
                act.activation(lbs[:, 0], lbs[:, 0], ACT.Sigmoid).then_inc(S("lb_ready"), 1)
                for i in range(4):
                    j = job_of["hg_q"] + i
                    wait_full(act, j)
                    out_of(act.activation(qh[:, 2 * i:2 * i + 2], bank(j).rearrange("p (a t) -> p a t", a=2), ACT.Copy), j)
                for i in range(16):
                    j = job_of["hg_z"] + i
                    d, h = i // AH, i % AH
                    wait_full(act, j)
                    act.activation(lf[:, d, h], bank(j), ACT.Sigmoid)
                    out_of(act.activation(kf[:, d, h], bank(j), ACT.Sigmoid, scale=-1.0), j)
                for i in range(8):
                    j = job_of["hg_i"] + i
                    wait_full(act, j)
                    a = 2 * (i % 2)
                    out_of(act.activation(itok[:, a:a + 2, 256 * (i // 2):256 * (i // 2 + 1)],
                                          bank(j).rearrange("p (a t) -> p a t", a=2), ACT.Copy), j)
                for i in range(4):
                    j = job_of["hg_g"] + i
                    wait_full(act, j)
                    out_of(act.activation(gsil[:, 2 * i:2 * i + 2], bank(j).rearrange("p (a t) -> p a t", a=2), ACT.Silu), j)
                for d in range(2):
                    act.wait_ge(S("forget_ready"), d + 1)
                    act.activation(lf[:, d], lf[:, d], ACT.Ln).then_inc(S("log_forget_ready"), 1)
                for d in range(2):
                    act.wait_ge(S("ctx_decay_ready"), d + 1)
                    act.activation(lf[:, d, :, T:T2], lf[:, d, :, T:T2], ACT.Exp).then_inc(S("ctx_decay_exp"), 1)
                act.wait_ge(S("lat_sums_ready"), 1)
                act.activation(ework[:], lf[:, :, :, 0:T], ACT.Exp).then_inc(S("q_decay_exp"), 1)
                for lev in range(len(LEVELS) + 1):
                    act.wait_ge(S("level_exponents"), lev + 1)
                    e = eworks[lev % 2]
                    act.activation(e[:], e[:], ACT.Exp).then_inc(S("level_exp"), 1)
                for i in range(4):
                    act.wait_ge(S("att_used"), 4 * (len(LEVELS) + 2))
                    act.activation(ework[:, 0, 2 * i:2 * i + 2], psum[:, NB + i].rearrange("p (h t) -> p h t", h=2), ACT.Square
                                   ).then_inc(S("o_sq_ready"), 1)
                for i in range(4):
                    wait_out(act, job_of["hg_norm"] + i)
                    act.activation(hstat[:, 2 * i:2 * i + 2], hstat[:, 2 * i:2 * i + 2], ACT.Sqrt).then_inc(S("o_std_ready"), 1)

            def stage_ffn3():
                rms2(3, [rms_sq3])
                silu_steps("ffn3", FSTEPS)

            stage_prep()
            stage_mlstm()
            stage_ffn0()
            stage_s5()
            stage_moe()
            stage_mla()
            stage_ffn2()
            stage_hg()
            stage_ffn3()

        @block.vector
        def _(dve):
            def modulate(m, shift, signal):
                for c in range(DC):
                    last = dve.tensor_scalar(act_in[:, c], xT[:, c], mod1[:, m, shift + DC + c, 0:1],
                                             mod[:, m, shift + c, 0:1], ALU.mult, ALU.add)
                last.then_inc(S(signal), 1)

            def ada(l, n):
                j = job_of[f"ada{l}"]
                wait_full(dve, j)
                bias = col(f"ada_b{l}", 0, 48)[:, :, None].broadcast_to([P, 48, n])
                src = bank(j)[:, 0:48 * n].rearrange("p (c n) -> p c n", n=n)
                out_of(dve.tensor_tensor(mod[:, l, :, 0:n], src, bias, ALU.add), j)
                dve.drain()
                dve.tensor_scalar(mod1[:, l, :, 0:n], mod[:, l, :, 0:n], 1.0, None, ALU.add)
                dve.drain()

            def layer_norm(i, l, which):
                j = job_of[f"ln{i}"]
                wait_full(dve, j)
                mean = bank(j)[:, None, 0:T].broadcast_to([P, DC, T])
                out_of(dve.scalar_tensor_tensor(res[:], mean, -1.0 / D, res[:], ALU.mult, ALU.add), j)
                wait_full(dve, j + 1)
                out_of(dve.tensor_scalar(stat[:, 0], bank(j + 1)[:, 0:T], 1.0 / D, LN_EPS, ALU.mult, ALU.add), j + 1)
                dve.wait_ge(S("ln_std_ready"), i + 1)
                dve.reciprocal(stat[:, 0], stat[:, 0])
                dve.drain()
                dve.tensor_tensor(res[:], res[:], stat[:, 0:1].broadcast_to([P, DC, T]), ALU.mult)
                dve.drain()
                for c in range(DC):
                    dve.tensor_scalar(xT[:, c], res[:, c], col(f"ln_{which}_g{l}", c), col(f"ln_{which}_b{l}", c),
                                      ALU.mult, ALU.add)
                dve.drain()

            def residual(c, src, gate):
                dve.tensor_scalar(res[:, c], src, gate, None, ALU.mult)

            def hidden_steps(name, steps, gates=None):
                hid, sil = ffn_bufs[name]

                def body(it, i):
                    j = job_of[name] + 2 * i + 1
                    wait_out(dve, j - 1, it, 4)
                    if gates is not None:
                        dve.tensor_tensor(sil[:, i % 2], sil[:, i % 2], gates(it, i), ALU.mult)
                        dve.drain()
                    wait_full(dve, j, it, 4)
                    if it is not None or i >= 2:
                        dve.wait_ge(S(f"{name}_down"), val(i - 1, it, 2))
                    up = bank(j).rearrange("p (a t) -> p a t", a=2)
                    out_of(dve.tensor_tensor(hid[:, i % 2], sil[:, i % 2], up, ALU.mult), j)
                body(None, 0)
                body(None, 1)
                after_two(dve, steps, 2, body)
                dve.wait_ge(S(f"{name}_down"), steps)

            def ffn_residual(m):
                for c in range(DC):
                    dve.tensor_scalar(res[:, c], psum[:, NB + c // 2, (c % 2) * T:(c % 2 + 1) * T],
                                      mod1[:, m, 40 + c, 0:1], None, ALU.mult)
                dve.drain()
                dve.scalar_tensor_tensor(res[:], xT[:], ALPHA, res[:], ALU.mult, ALU.add).then_inc(S("ln_sum_ready"), 1)

            def stage_prep():
                dve.memset(prow[:], 0.0).then_inc(S("prow_zero"), 1)
                dve.memset(xm[:, :, 0:4], 0.0)
                dve.memset(zeros[:], 0.0)
                dve.memset(one[:], 1.0)
                for g in range(5):
                    j = job_of["params"] + g
                    wait_full(dve, j)
                    out_of(dve.tensor_copy(par[:, g * P:(g + 1) * P], bank(j)[:, 0:P]), j)
                for g in range(4):
                    j = job_of["xT"] + g
                    wait_full(dve, j)
                    out_of(dve.tensor_copy(xT[:, 2 * g:2 * g + 2], bank(j).rearrange("p (a t) -> p a t", a=2)), j)
                dve.wait_ge(S("mlstm_small_in"), 64)
                mask = c_("block4")[:, :, None].broadcast_to([P, 32, 4])
                for i in range(3):
                    for c in range(IC):
                        last = dve.tensor_tensor(bd[:, i, c].rearrange("p (n o) -> p n o", o=4),
                                                 qkv_small[:, i, c:c + 1].broadcast_to([P, 32, 4]), mask, ALU.mult)
                    last.then_inc(S("block_diag_ready"), 1)

            def stage_ada0():
                ada(0, 1)

            def stage_mlstm():
                modulate(0, 0, "mlstm_in_ready")
                for c in range(IC):
                    wait_out(dve, job_of["m_in"] + c // 2)
                    dve.tensor_scalar(xc[:, c], xm[:, c, 1:1 + T], col("conv_w", c), None, ALU.mult)
                    for k in range(1, CONV):
                        dve.drain()
                        last = dve.scalar_tensor_tensor(xc[:, c], xm[:, c, 1 + k:1 + k + T], col("conv_w", k * IC + c),
                                                        xc[:, c], ALU.mult, ALU.add)
                    last.then_inc(S("conv_sum_ready"), 1)
                j = job_of["m_gates"]
                wait_full(dve, j)
                g = gate_rows
                out_of(dve.tensor_scalar(g[0:8, 0], bank(j)[0:8, 0:T], col("b_gates")[0:8], None, ALU.add), j)
                j = job_of["m_fsel"]
                wait_full(dve, j)
                f = bank(j)[0:NH, 0:T]
                dve.tensor_scalar(g[0:NH, 1], f, 0.0, None, ALU.min)
                dve.drain()
                out_of(dve.scalar_tensor_tensor(g[0:NH, 2], g[0:NH, 1], 2.0, f, ALU.mult, ALU.subtract), j)
                dve.memset(g[0:NH, 7], 1.0)
                dve.wait_ge(S("ln_f_ready"), 1)
                dve.tensor_tensor(g[0:NH, 1], g[0:NH, 1], g[0:NH, 2], ALU.subtract)
                dve.drain()
                dve.tensor_tensor_scan(g[0:NH, 3], g[0:NH, 7], g[0:NH, 1], 0.0, ALU.mult, ALU.add)
                dve.drain()
                dve.tensor_tensor(g[0:NH, 4], g[0:NH, 0], g[0:NH, 3], ALU.subtract)
                dve.drain()
                dve.tensor_tensor_scan(g[0:NH, 5], g[0:NH, 4], g[0:NH, 4], 0.0, ALU.max, ALU.max)
                dve.drain()
                dve.tensor_tensor(g[0:NH, 6], g[0:NH, 3], g[0:NH, 5], ALU.add)
                dve.tensor_scalar(g[0:NH, 5], g[0:NH, 5], -1.0, None, ALU.mult).then_inc(S("m_sum_ready"), 1)
                j = job_of["m_cT"]
                wait_full(dve, j)
                out_of(dve.tensor_copy(cT, bank(j)[:, 0:2 * NH].rearrange("p (s h) -> p s h", s=2)), j)
                wait_out(dve, job_of["m_qk"] + IC - 1)
                for h in range(NH):
                    j = job_of["m_rows"] + h
                    wait_full(dve, j)
                    out_of(dve.tensor_copy(nm[:, h], bank(j).rearrange("p (k t) -> p k t", k=2)), j)
                for g in range(8):
                    a, c0 = g // 4, 4 * (g % 4)
                    j = job_of["m_v"] + g
                    wait_full(dve, j)
                    out_of(dve.tensor_copy(vbuf[:, a, c0 * P:(c0 + 4) * P], bank(j)), j)
                causal = c_("causal").rearrange("p (s t) -> p s t", s=2)
                for h in range(NH):
                    for s in range(2):
                        dve.tensor_tensor(decay[:, s], nm[:, h, 0], causal[:, s], ALU.add).then_inc(S("decay_sum_ready"), 1)
                    j = job_of["m_head"] + 4 * h
                    dve.wait_ge(S("decay_ready"), 2 * h + 2)
                    wait_full(dve, j)
                    out_of(dve.scalar_tensor_tensor(scor[:, h % 2], bank(j).rearrange("p (s t) -> p s t", s=2), DH ** -0.5,
                                                  decay[:], ALU.mult, ALU.mult), j)
                    wait_full(dve, j + 1)
                    dve.tensor_tensor(recip_[:, 0], bank(j + 1)[:, 0:T], nm[:, h, 1], ALU.max)
                    dve.drain()
                    out_of(dve.scalar_tensor_tensor(recip_[:, 0], bank(j + 1)[:, 0:T], -1.0, recip_[:, 0],
                                                    ALU.mult, ALU.max), j + 1)
                    dve.drain()
                    dve.reciprocal(recip_[:, 1], recip_[:, 0])
                    dve.drain()
                    for g in range(2):
                        wait_full(dve, j + 2 + g)
                        out_of(dve.tensor_tensor(hT[:, h * HC + 2 * g:h * HC + 2 * g + 2],
                                               bank(j + 2 + g).rearrange("p (a t) -> p a t", a=2),
                                               recip_[:, 1:2].broadcast_to([P, 2, T]), ALU.mult), j + 2 + g)
                for h in range(NH):
                    j = job_of["m_norm"] + 2 * h
                    wait_full(dve, j)
                    hh = hT[:, h * HC:(h + 1) * HC]
                    out_of(dve.scalar_tensor_tensor(hh, bank(j)[:, None, 0:T].broadcast_to([P, HC, T]), -1.0 / DH, hh,
                                                  ALU.mult, ALU.add), j)
                    wait_full(dve, j + 1)
                    out_of(dve.tensor_scalar(stat[:, h % 2], bank(j + 1)[:, 0:T], 1.0 / DH, LN_EPS, ALU.mult, ALU.add), j + 1)
                    dve.wait_ge(S("h_std_ready"), h + 1)
                    dve.reciprocal(stat[:, h % 2], stat[:, h % 2])
                    dve.drain()
                    dve.tensor_tensor(hh, hh, stat[:, h % 2:h % 2 + 1].broadcast_to([P, HC, T]), ALU.mult)
                    dve.drain()
                    for c in range(h * HC, (h + 1) * HC):
                        dve.tensor_scalar(xc[:, c], xc[:, c], col("mlstm_skip", c), None, ALU.mult)
                    dve.drain()
                    for c in range(h * HC, (h + 1) * HC):
                        dve.scalar_tensor_tensor(hT[:, c], hT[:, c], col("mlstm_norm_w", c), xc[:, c], ALU.mult, ALU.add)
                    dve.drain()
                    last = dve.tensor_tensor(hh, hh, zs[:, h * HC:(h + 1) * HC], ALU.mult)
                last.then_inc(S("h_out_ready"), 1)
                for g in range(4):
                    j = job_of["m_out"] + g
                    wait_full(dve, j)
                    for n in range(2):
                        last = dve.tensor_scalar(res[:, 2 * g + n], bank(j)[:, n * T:(n + 1) * T],
                                                 mod1[:, 0, 16 + 2 * g + n, 0:1], None, ALU.mult)
                    out_of(last, j)
                dve.drain()
                dve.scalar_tensor_tensor(res[:], xT[:], ALPHA, res[:], ALU.mult, ALU.add).then_inc(S("ln_sum_ready"), 1)
                layer_norm(0, 0, "mix")

            def stage_ffn0():
                modulate(0, 24, "ffn0_in_ready")
                hidden_steps("ffn0", FSTEPS)
                ffn_residual(0)
                layer_norm(1, 0, "ffn")

            def bc(v, n):
                return v[:, :, None].broadcast_to([P, v.shape[1], n])

            def stage_s5():
                ada(1, 1)
                modulate(1, 0, "s5_u_ready")
                dt, th, lam, mag, kk, sn, hs, den, ar, ai, kr, ki, cs, t1 = (sv[:, i] for i in range(14))
                lr, li = col("lam_re", 0, NPAIR), col("lam_im", 0, NPAIR)

                def step(*a):
                    dve.tensor_tensor(*a)
                    dve.drain()

                def step_s(*a):
                    dve.tensor_scalar(*a)
                    dve.drain()

                dve.wait_ge(S("dt_ready"), 1)
                step(mag, lr, dt, ALU.mult)
                step(th, li, dt, ALU.mult)
                magic = 1.5 * 2 ** 23
                step_s(kk, th, 1 / (2 * np.pi), magic, ALU.mult, ALU.add)
                step_s(kk, kk, magic, None, ALU.subtract)
                c1 = 6.28125
                c2 = float(np.float32(round((2 * np.pi - c1) * 2 ** 21) / 2 ** 21))
                c3 = 2 * np.pi - c1 - c2
                for c in (c1, c2, c3):
                    dve.scalar_tensor_tensor(th, kk, -c, th, ALU.mult, ALU.add)
                    dve.drain()
                pi = float(np.nextafter(np.float32(np.pi), np.float32(0)))
                step_s(sn, th, pi, -pi, ALU.min, ALU.max)
                dve.tensor_scalar(hs, sn, 0.5, None, ALU.mult).then_inc(S("theta_ready"), 1)
                dve.wait_ge(S("sin_ready"), 1)
                step(cs, hs, hs, ALU.mult)
                step_s(cs, cs, -2.0, 1.0, ALU.mult, ALU.add)
                step(ar, mag, cs, ALU.mult)
                step(ai, mag, sn, ALU.mult)
                step(den, lr, lr, ALU.mult)
                step(t1, li, li, ALU.mult)
                step(den, den, t1, ALU.add)
                dve.reciprocal(den, den)
                step_s(ar, ar, -1.0, None, ALU.add)
                step(kr, ar, lr, ALU.mult)
                step(t1, ai, li, ALU.mult)
                step(kr, kr, t1, ALU.add)
                step(kr, kr, den, ALU.mult)
                step(ki, ai, lr, ALU.mult)
                step(t1, ar, li, ALU.mult)
                step(ki, ki, t1, ALU.subtract)
                step(ki, ki, den, ALU.mult)
                dve.wait_ge(S("s5_in"), 9 * 16)
                for i in range(2):
                    step(bbar[:, i], bmat[:, i], bc(kr, SH), ALU.mult)
                    step(btmp, bmat[:, 1 - i], bc(ki, SH), ALU.mult)
                    step(bbar[:, i], bbar[:, i], btmp, ALU.add if i else ALU.subtract)
                    last = dve.tensor_tensor(
                        bpad[:, i].rearrange("p c s -> p (c s)").rearrange("p (j g h) -> p j g h", g=2, h=SH),
                        bbar[:, i, :, None, :].broadcast_to([P, NPAIR, 2, SH]),
                        c_("half")[:, None, :, None].broadcast_to([P, NPAIR, 2, SH]), ALU.mult)
                last.then_inc(S("bpad_ready"), 1)
                dve.tensor_copy(rot[:, 0, :, 0], cs)
                step_s(rot[:, 1, :, 0], sn, 1.0, None, ALU.mult)
                n = 1
                while n < SL:
                    er, ei = rot[:, 0, :, 0:n], rot[:, 1, :, 0:n]
                    fr, fi = (rot[:, i, :, n - 1:n].broadcast_to([P, NPAIR, n]) for i in range(2))
                    step(rot[:, 0, :, n:2 * n], er, fr, ALU.mult)
                    step(dbl[:, :, 0:n], ei, fi, ALU.mult)
                    step(rot[:, 0, :, n:2 * n], rot[:, 0, :, n:2 * n], dbl[:, :, 0:n], ALU.subtract)
                    step(rot[:, 1, :, n:2 * n], er, fi, ALU.mult)
                    step(dbl[:, :, 0:n], ei, fr, ALU.mult)
                    step(rot[:, 1, :, n:2 * n], rot[:, 1, :, n:2 * n], dbl[:, :, 0:n], ALU.add)
                    n *= 2
                for g in range(4):
                    j = job_of["s_bT"] + g
                    wait_full(dve, j)
                    out_of(dve.tensor_copy(bT[:, g // 2, 4 * (g % 2):4 * (g % 2) + 4],
                                           bank(j).rearrange("p (c s) -> p c s", s=P)), j)
                parity = c_("parity")[:, None, :].broadcast_to([P, 4, P])
                for g in range(4):
                    j = job_of["s_cT"] + g
                    wait_full(dve, j)
                    out_of(dve.scalar_tensor_tensor(cmT[:, g // 2, 4 * (g % 2):4 * (g % 2) + 4],
                                                    bank(j).rearrange("p (c s) -> p c s", s=P), -1.0 if g // 2 else 1.0,
                                                    parity, ALU.mult, ALU.mult), j)

                def pair(c, i):
                    p = 4 * c + i
                    j = job_of["s_pair"] + i
                    dve.drain()
                    dve.wait_ge(bank_full[j % NB], c + (j // NB + 1))
                    cos2, sin2 = (rot[:, k, bass.ds(p, 1), :].broadcast_to([P, 2, SL]) for k in range(2))
                    b = [bank(j)[:, k * T:(k + 1) * T].rearrange("p (b t) -> p b t", b=2) for k in range(2)]
                    z = [zri[:, k].rearrange("p (b t) -> p b t", b=2) for k in range(2)]
                    zt = [ztmp[:, k].rearrange("p (b t) -> p b t", b=2) for k in range(2)]
                    dve.tensor_tensor(z[0], b[0], cos2, ALU.mult)
                    dve.tensor_tensor(zt[0], b[1], sin2, ALU.mult)
                    dve.tensor_tensor(z[1], b[1], cos2, ALU.mult)
                    out_of(dve.tensor_tensor(zt[1], b[0], sin2, ALU.mult), j)
                    dve.drain()
                    dve.tensor_tensor(z[0], z[0], zt[0], ALU.add)
                    dve.tensor_tensor(z[1], z[1], zt[1], ALU.subtract)
                    dve.drain()
                    mag_t = sv[:, 3, bass.ds(p, 1)].broadcast_to([P, SL])
                    cos1, sin1 = (rot[:, k, bass.ds(p, 1), :].rearrange("p o t -> p (o t)") for k in range(2))
                    for blk in range(2):
                        at = slice(blk * SL, (blk + 1) * SL)
                        x = [xri[:, i % 2, k] for k in range(2)]
                        for k in range(2):
                            start = x[k][:, SL - 1:SL] if blk else 0.0
                            dve.tensor_tensor_scan(zri[:, k, at], mag_t, zri[:, k, at], start, ALU.mult, ALU.add)
                        dve.drain()
                        if blk == 0 and not (isinstance(c, int) and i < 2):
                            dve.wait_ge(S("s5_x_used"), p - 1)
                        dve.tensor_tensor(x[0][:, at], zri[:, 0, at], cos1, ALU.mult)
                        dve.tensor_tensor(x[1][:, at], zri[:, 1, at], cos1, ALU.mult)
                        dve.tensor_tensor(ztmp[:, 0, at], zri[:, 1, at], sin1, ALU.mult)
                        dve.tensor_tensor(ztmp[:, 1, at], zri[:, 0, at], sin1, ALU.mult)
                        dve.drain()
                        dve.tensor_tensor(x[0][:, at], x[0][:, at], ztmp[:, 0, at], ALU.subtract)
                        last = dve.tensor_tensor(x[1][:, at], x[1][:, at], ztmp[:, 1, at], ALU.add)
                        if blk == 0:
                            dve.drain()
                    last.then_inc(S("s5_x_ready"), 1)

                def y_out(c, back):
                    c = c + back
                    dve.wait_ge(S("s5_x_used"), 4 * c + 4)
                    dve.scalar_tensor_tensor(gT[:, bass.ds(c, 1), :], act_in[:, bass.ds(c, 1), :],
                                             par[:, bass.ds(prow_at["s5_d"] + c, 1)],
                                             psum[:, bass.ds(NB + c % 2, 1), 0:T], ALU.mult, ALU.add
                                             ).then_inc(S("s5_y_out"), 1)

                for i in range(4):
                    pair(0, i)
                with dve.Fori(1, DC) as c:
                    for i in range(4):
                        pair(c, i)
                        if i == 0:
                            y_out(c, -1)
                y_out(DC, -1)
                for i in range(4):
                    j = job_of["glu"] + 2 * i
                    wait_out(dve, j + 1)
                    wait_full(dve, j)
                    for n in range(2):
                        last = dve.scalar_tensor_tensor(res[:, 2 * i + n], bank(j)[:, n * T:(n + 1) * T],
                                                        col("s5_b_glu", 2 * i + n), sil[:, i % 2, n], ALU.add, ALU.mult)
                    out_of(last, j)
                    dve.drain()
                    for n in range(2):
                        dve.tensor_scalar(res[:, 2 * i + n], res[:, 2 * i + n], mod1[:, 1, 16 + 2 * i + n, 0:1], None,
                                          ALU.mult)
                dve.drain()
                dve.scalar_tensor_tensor(res[:], xT[:], ALPHA, res[:], ALU.mult, ALU.add).then_inc(S("ln_sum_ready"), 1)
                layer_norm(2, 1, "mix")

            def stage_moe():
                modulate(1, 24, "moe_in_ready")
                j = job_of["router"]
                wait_full(dve, j)
                logit, ex, m1, rank, tot, wt = (lg[:, i] for i in (0, 1, 2, 3, 4, 6))
                out_of(dve.tensor_copy(logit, bank(j)[:, 0:2 * NE].rearrange("p (a e) -> p a e", a=2)), j)
                dve.drain()
                dve.tensor_reduce(m1[:, :, 0:1], logit, AX.X, ALU.max)
                dve.drain()
                dve.tensor_tensor(ex, logit, m1[:, :, 0:1].broadcast_to([P, 2, NE]), ALU.subtract
                                  ).then_inc(S("logits_ready"), 1)
                lj = logit[:, :, None, :].broadcast_to([P, 2, NE, NE])
                le = logit[:, :, :, None].broadcast_to([P, 2, NE, NE])
                before = c_("before").rearrange("p (e j) -> p e j", e=NE)[:, None].broadcast_to([P, 2, NE, NE])
                dve.tensor_tensor(cmp_[:, 0], lj, le, ALU.is_gt)
                dve.tensor_tensor(cmp_[:, 1], lj, le, ALU.is_equal)
                dve.drain()
                dve.tensor_tensor(cmp_[:, 1], cmp_[:, 1], before, ALU.mult)
                dve.drain()
                dve.tensor_tensor(cmp_[:, 0], cmp_[:, 0], cmp_[:, 1], ALU.add)
                dve.drain()
                dve.tensor_reduce(rank[:, :, :, None], cmp_[:, 0], AX.X, ALU.add)
                dve.drain()
                dve.tensor_scalar(rank, rank, 1.5, None, ALU.is_lt)
                dve.wait_ge(S("exp_logits_ready"), 1)
                dve.drain()
                dve.tensor_tensor(ex, ex, rank, ALU.mult)
                dve.drain()
                dve.tensor_reduce(tot[:, :, 0:1], ex, AX.X, ALU.add)
                dve.drain()
                dve.reciprocal(tot[:, :, 0:1], tot[:, :, 0:1])
                dve.drain()
                dve.tensor_tensor(wt, ex, tot[:, :, 0:1].broadcast_to([P, 2, NE]), ALU.mult
                                  ).then_inc(S("top2_ready"), 1)
                j = job_of["gateT"]
                wait_full(dve, j)
                out_of(dve.tensor_copy(gate8[0:NE], bank(j)[0:NE, 0:T]), j)
                for g in range(4):
                    j = job_of["gates"] + g
                    wait_full(dve, j)
                    out_of(dve.tensor_copy(gate_bc[:, 2 * g:2 * g + 2], bank(j).rearrange("p (e t) -> p e t", e=2)), j)
                dve.drain()
                hidden_steps("moe", FSTEPS * NE, lambda it, i: gate_bc[
                    :, bass.ds(val(i, it, 2) // FSTEPS, 1), :].broadcast_to([P, 2, T]))
                ffn_residual(1)
                layer_norm(3, 1, "ffn")

            def rms2(i, m, norm, shift, dst, signal):
                gain = col(norm, 0, DC)[:, :, None].broadcast_to([P, DC, 2])
                dve.tensor_tensor(norm_gain[:], mod1[:, m, shift + DC:shift + 2 * DC], gain, ALU.mult)
                j, n = job_of[f"rms{i}"], T * len(dst)
                wait_full(dve, j)
                out_of(dve.tensor_scalar(rstd2[:, 0:n], bank(j)[:, 0:n], 1.0 / D, RMS_EPS, ALU.mult, ALU.add), j)
                dve.wait_ge(S("rms_std_ready"), i + 1)
                dve.reciprocal(rstd2[:, 0:n], rstd2[:, 0:n])
                dve.drain()
                for k in range(len(dst)):
                    dve.tensor_tensor(dst[k], halves[k][:], rstd2[:, None, k * T:(k + 1) * T].broadcast_to([P, DC, T]),
                                      ALU.mult)
                dve.drain()
                for k in range(len(dst)):
                    for c in range(DC):
                        last = dve.tensor_scalar(dst[k][:, c], dst[k][:, c], norm_gain[:, c, k:k + 1],
                                                 mod[:, m, shift + c, k:k + 1], ALU.mult, ALU.add)
                last.then_inc(S(signal), 1)

            def stage_mla():
                dve.drain().then_inc(S("moe_done"), 1)
                for g in range(4):
                    j = job_of["ctxT"] + g
                    wait_full(dve, j)
                    out_of(dve.tensor_copy(ctxT[:, 2 * g:2 * g + 2], bank(j).rearrange("p (a t) -> p a t", a=2)), j)
                dve.drain().then_inc(S("x2_ready"), 1)
                ada(2, 2)
                rms2(0, 2, "norm1_w_20", 0, [a2[:, :, 0:T], a2[:, :, T:T2]], "a2_ready")
                for kind, m, c in MLA_SEQ:
                    if kind != "S":
                        continue
                    name, h, n, rows, dst, weight, slots = item_of(m)
                    j = mla_job[kind, m, c]
                    st = nstat[0:rows, m % 2]
                    wait_full(dve, j)
                    out_of(dve.tensor_scalar(st, bank(j)[0:rows], 1.0 / (rows * n), RMS_EPS, ALU.mult, ALU.add), j)
                    dve.wait_ge(S("nstd_ready"), m + 1)
                    dve.reciprocal(st, st)
                    dve.drain()
                    for k in range(n):
                        d = dst[0:rows, k if n > 1 else h]
                        last = dve.scalar_tensor_tensor(d, d, col(weight, k)[0:rows], st, ALU.mult, ALU.mult)
                    last.then_inc(S("item_normed"), 1)
                cos, sin = c_("rope_cos")[0:ROPE], c_("rope_sin")[0:ROPE]
                for i in range(AH + 1):
                    j = job_of["rope"] + i
                    t = kr[0:ROPE, 0, 0:T] if i == 0 else qr[0:ROPE, i - 1, 0:T]
                    a, b = (rope_tmp[0:ROPE, i % 2, k * T:(k + 1) * T] for k in range(2))
                    wait_full(dve, j)
                    dve.tensor_tensor(a, t, cos, ALU.mult)
                    out_of(dve.tensor_tensor(b, bank(j)[0:ROPE, 0:T], sin, ALU.mult), j)
                    dve.drain()
                    dve.tensor_tensor(t, a, b, ALU.add).then_inc(S("rope_ready"), 1)
                dve.drain()
                for kind, h, k in ATTN_SEQ:
                    if kind != "S":
                        continue
                    j = attn_job[kind, h, k]
                    g = 1 if k < 2 else 2
                    mx = smax[:, h % 2, 2 * k:2 * k + g]
                    sm = smax[:, h % 2, 8 + 2 * k:8 + 2 * k + g]
                    wait_full(dve, j)
                    dve.tensor_reduce(mx, bank(j).rearrange("p (g s) -> p g s", g=g), AX.X, ALU.max)
                    dve.drain()
                    dve.tensor_scalar(mx, mx, -ATT_SCALE, None, ALU.mult).then_inc(S("max_ready"), 1)
                    wait_out(dve, j)
                    pr = prob[:, h % 2, k].rearrange("p (g s) -> p g s", g=g)
                    dve.tensor_reduce(sm, pr, AX.X, ALU.add)
                    dve.drain()
                    dve.reciprocal(sm, sm)
                    dve.drain()
                    for a in range(g):
                        last = dve.tensor_scalar(pr[:, a], pr[:, a], sm[:, a:a + 1], None, ALU.mult)
                    last.then_inc(S("prob_ready"), 1)
                residual2(job_of["mla_o"], 2, 16)

            def residual2(j0, m, gate):
                for c in range(DC):
                    j = j0 + c
                    wait_full(dve, j)
                    for k in range(2):
                        last = dve.scalar_tensor_tensor(halves[k][:, c], bank(j)[:, k * T:(k + 1) * T],
                                                        mod[:, m, gate + c, k:k + 1], halves[k][:, c], ALU.mult, ALU.add)
                    out_of(last, j)
                dve.drain().then_inc(S("x2_ready"), 1)

            def stage_ffn2():
                rms2(1, 2, "norm2_w_20", 24, [a2[:, :, 0:T], a2[:, :, T:T2]], "a2_ready")
                j0 = job_of["ffn2"]

                def body(it, i):
                    for n in range(2):
                        j = j0 + 4 * i + 2 + n
                        wait_out(dve, j - 2, it, 12)
                        wait_full(dve, j, it, 12)
                        at = val(2 * i + n, it, 6)
                        out_of(dve.tensor_tensor(hid2[:, bass.ds(at, 1), :], sil2[:, n:n + 1], bank(j)[:, None, :],
                                                 ALU.mult), j)
                repeat(dve, FSTEPS, 3, body)
                for half in range(2):
                    dve.wait_ge(S("ffn2_sum"), half + 1)
                    for n in range(4):
                        c = 4 * half + n
                        for k in range(2):
                            dve.scalar_tensor_tensor(halves[k][:, c], psum[:, NB + n, k * T:(k + 1) * T],
                                                     mod[:, 2, 40 + c, k:k + 1], halves[k][:, c], ALU.mult, ALU.add)
                    dve.drain().then_inc(S("ffn2_out"), 1)
                dve.nop().then_inc(S("x2_ready"), 1)

            def stage_hg():
                ada(3, 2)
                rms2(2, 3, "norm1_w_21", 0, [a2[:, :, 0:T], a2[:, :, T:T2]], "a2_ready")
                dve.tensor_tensor(lbs[:, 0], col("lb", 16, 16), col("lb", 0, 16), ALU.subtract
                                  ).then_inc(S("lb_logits_ready"), 1)
                dve.wait_ge(S("lb_ready"), 1)
                dve.tensor_scalar(lbs[:, 1], lbs[:, 0], -1.0, 1.0, ALU.mult, ALU.add)
                dve.drain()
                for d in range(2):
                    for h in range(AH):
                        i = d * AH + h
                        wait_out(dve, job_of["hg_z"] + i)
                        lb, lb1 = lbs[:, 0, i:i + 1], lbs[:, 1, i:i + 1]
                        dve.tensor_scalar(lf[:, d, h], lf[:, d, h], lb1, lb, ALU.mult, ALU.add)
                        dve.tensor_scalar(kf[:, d, h], kf[:, d, h], lb1, None, ALU.mult)
                    dve.drain()
                    dve.tensor_scalar(lf[:, d], lf[:, d], 2.0 ** -64, None, ALU.max).then_inc(S("forget_ready"), 1)
                wait_full(dve, job_of["hg_g"] + 3)
                for d in range(2):
                    dve.wait_ge(S("log_forget_ready"), d + 1)
                    tmp = ework[:, d]
                    for h in range(AH):
                        src = lf[:, d, h, T:T2] if d else lf[:, d, h, T2 - 1:T - 1:-1]
                        dst = tmp[:, h] if d else tmp[:, h, ::-1]
                        dve.tensor_tensor_scan(dst, c_one(T), src, 0.0, ALU.mult, ALU.add)
                    dve.drain()
                    dve.tensor_tensor(lf[:, d, :, T:T2], tmp, lf[:, d, :, T:T2], ALU.subtract).then_inc(S("ctx_decay_ready"), 1)
                for d in range(2):
                    for h in range(AH):
                        x = lf[:, d, h, T - 1::-1] if d else lf[:, d, h, 0:T]
                        last = dve.tensor_tensor_scan(x, c_one(T), x, 0.0, ALU.mult, ALU.add)
                dve.drain().then_inc(S("lat_sums_ready"), 1)
                for d in range(2):
                    dve.wait_ge(S("ctx_decay_exp"), d + 1)
                    dve.tensor_tensor(kf[:, d, :, T:T2], kf[:, d, :, T:T2], lf[:, d, :, T:T2], ALU.mult
                                      ).then_inc(S("ctx_keys_ready"), 1)
                for i in range(8):
                    j = job_of["hg_wk"] + i
                    wait_full(dve, j)
                    out_of(dve.tensor_copy(wkT[:, 4 * i:4 * i + 4], bank(j).rearrange("p (i s) -> p i s", s=P)), j)
                for i in range(4):
                    j = job_of["hg_state"] + i
                    wait_full(dve, j)
                    m = 4 * i
                    out_of(dve.tensor_copy(state[:, m // AH, m % AH:m % AH + 4, T:T + P],
                                           bank(j).rearrange("p (i s) -> p i s", s=P)), j)
                dve.wait_ge(S("q_decay_exp"), 1)
                for d in range(2):
                    last = dve.tensor_tensor(ework[:, d], ework[:, d], qh[:], ALU.mult)
                last.then_inc(S("q_decayed"), 1)

                def att_out(n):
                    lev, j = n // 4, job_of["hg_level"] + n
                    if n >= 2:
                        dve.wait_ge(S("att_used"), n - 1)
                    wait_full(dve, j)
                    src = bank(j).rearrange("p (i t) -> p i t", t=P)
                    if lev == 0:
                        ins = dve.tensor_copy(atts[:, n % 2], src)
                    else:
                        mask = c_("levels")[:, (lev - 1) * P:lev * P]
                        ins = dve.tensor_tensor(atts[:, n % 2], src, mask[:, None, :].broadcast_to([P, 4, P]), ALU.mult)
                    out_of(ins, j)

                for lev, b in enumerate([P] + LEVELS):
                    e = eworks[lev % 2]
                    if lev == 0:
                        dve.wait_ge(S("q_decayed_used"), 1)
                    if lev >= 2:
                        wait_full(dve, job_of["hg_level"] + 4 * (lev - 2) + 3)
                    nb = T // (2 * b)

                    def blocks(x):
                        return x.rearrange("p h (n t) -> p h n t", t=2 * b)

                    def lo(x):
                        return blocks(x)[:, :, :, 0:b]

                    def hi(x):
                        return blocks(x)[:, :, :, b:2 * b]

                    f, g = lf[:, 0, :, 0:T], lf[:, 1, :, 0:T]
                    f_ref = blocks(f)[:, :, :, b - 1:b].broadcast_to([P, AH, nb, b])
                    g_ref = blocks(g)[:, :, :, b:b + 1].broadcast_to([P, AH, nb, b])
                    dve.tensor_tensor(hi(e[:, 0]), hi(f), f_ref, ALU.subtract)
                    dve.tensor_tensor(lo(e[:, 0]), lo(g), g_ref, ALU.subtract)
                    dve.tensor_tensor(lo(e[:, 1]), f_ref, lo(f), ALU.subtract)
                    dve.tensor_tensor(hi(e[:, 1]), g_ref, hi(g), ALU.subtract)
                    dve.drain().then_inc(S("level_exponents"), 1)
                    if lev >= 1:
                        for i in range(4):
                            att_out(4 * (lev - 1) + i)
                    dve.wait_ge(S("level_exp"), lev + 1)
                    dve.tensor_tensor(e[:, 0], e[:, 0], qh[:], ALU.mult)
                    dve.tensor_tensor(lo(e[:, 1]), lo(e[:, 1]), lo(kf[:, 0, :, 0:T]), ALU.mult)
                    dve.tensor_tensor(hi(e[:, 1]), hi(e[:, 1]), hi(kf[:, 1, :, 0:T]), ALU.mult)
                    dve.drain().then_inc(S("level_ready"), 1)
                lev = len(LEVELS) + 1
                wait_full(dve, job_of["hg_level"] + 4 * (lev - 2) + 3)
                dve.tensor_tensor(eworks[lev % 2][:, 1], kf[:, 0, :, 0:T], kf[:, 1, :, 0:T], ALU.add
                                  ).then_inc(S("level_ready"), 1)
                for n in range(4 * (lev - 1), 4 * (lev + 1)):
                    att_out(n)
                for i in range(4):
                    j = job_of["hg_norm"] + i
                    wait_full(dve, j)
                    out_of(dve.tensor_scalar(hstat[:, 2 * i:2 * i + 2], bank(j).rearrange("p (h t) -> p h t", h=2),
                                             1.0 / P, RMS_EPS, ALU.mult, ALU.add), j)
                for i in range(4):
                    dve.wait_ge(S("o_std_ready"), i + 1)
                    hs = hstat[:, 2 * i:2 * i + 2]
                    o = ework[:, 1, 2 * i:2 * i + 2]
                    dve.reciprocal(hs, hs)
                    dve.drain()
                    dve.scalar_tensor_tensor(o, psum[:, NB + i].rearrange("p (h t) -> p h t", h=2), col("hg_o_norm_w_2"),
                                             hs, ALU.mult, ALU.mult)
                    dve.drain()
                    last = dve.tensor_tensor(o, o, gsil[:, 2 * i:2 * i + 2], ALU.mult)
                last.then_inc(S("hg_o_ready"), 1)
                for i in range(4):
                    j = job_of["hg_o"] + i
                    wait_full(dve, j)
                    for n in range(2):
                        c = 2 * i + n
                        last = dve.scalar_tensor_tensor(xT[:, c], bank(j)[:, n * T:(n + 1) * T], mod[:, 3, 16 + c, 0:1],
                                                        xT[:, c], ALU.mult, ALU.add)
                    out_of(last, j)
                dve.drain().then_inc(S("x2_ready"), 1)

            def stage_ffn3():
                rms2(3, 3, "norm2_w_21", 24, [act_in[:]], "ffn3_in_ready")
                hidden_steps("ffn3", FSTEPS)
                for c in range(DC):
                    last = dve.scalar_tensor_tensor(xT[:, c], psum[:, NB + c // 2, (c % 2) * T:(c % 2 + 1) * T],
                                                    mod[:, 3, 40 + c, 0:1], xT[:, c], ALU.mult, ALU.add)
                last.then_inc(S("x_final"), 1)

            def stage_out():
                for g in range(4):
                    j = job_of["outT"] + g
                    wait_full(dve, j)
                    out_of(dve.tensor_copy(out_tok[:, g // 2, (g % 2) * 512:(g % 2 + 1) * 512], bank(j)), j)
                dve.drain().then_inc(S("out_tok_ready"), 1)

            stage_prep()
            stage_ada0()
            stage_mlstm()
            stage_ffn0()
            stage_s5()
            stage_moe()
            stage_mla()
            stage_ffn2()
            stage_hg()
            stage_ffn3()
            stage_out()


def kernel(**inputs):
    import concourse.bacc as bacc
    from concourse.bass_utils import run_bass_kernel_spmd

    nc = bacc.Bacc("TRN2", target_bir_lowering=False, num_devices=1)
    arrays, w = {}, {}
    for name, a in inputs.items():
        if name.startswith("df_"):
            continue
        a = np.ascontiguousarray(a)
        arrays[f"in_{name}"] = a
        w[name] = nc.dram_tensor(f"in_{name}", a.shape, mybir.dt.from_np(a.dtype), kind="ExternalInput").ap()
    table, _ = shape_constants()
    arrays["shape_constants"] = table
    const = nc.dram_tensor("shape_constants", table.shape, F32, kind="ExternalInput").ap()
    out = nc.dram_tensor("out", (1, T, D), F32, kind="ExternalOutput").ap()
    build_program(nc, w, const, out)
    r = run_bass_kernel_spmd(nc, [arrays], core_ids=[0])
    return r.results[0]["out"]
```

```python
from contextlib import ExitStack

import numpy as np

import concourse.bass as bass
from concourse import mybir

P = 128
F32 = mybir.dt.float32
ALU = mybir.AluOpType
ACT = mybir.ActivationFunctionType
AX = mybir.AxisListType

D = 1024
T = 256
DC = D // P
LN_EPS = 1e-5
RMS_EPS = 1e-6
ALPHA = 4 ** 0.25

DI = 2 * D
IC = DI // P
NH = 4
DH = DI // NH
HC = DH // P
CONV = 4

FF = 2816
FC = FF // P
FSTEPS = FC // 2
NE = 8
SLOTS = P
PAIR_STEPS = 2 * FSTEPS

SG, SP_, SH = 64, 64, 16
SL = 128
NPAIR = SG // 2

AH = 8
NOPE, ROPE = 128, 64
QR, KVR = 384, 256
ATT_SCALE = (NOPE + ROPE) ** -0.5

RING = 6
SLOT = 2048
NB = 4
BANK = 512

LEVELS = [64, 32, 16, 8, 4, 2, 1]

ADA_STAGES = {"a": (0, 6), "b": (6, 18), "c": (24, 24)}



def shape_constants():
    p = np.arange(P)
    parts = {}

    def put(name, a):
        full = np.zeros((P, a.shape[1]), np.float32)
        full[: a.shape[0]] = a
        parts[name] = full

    put("ident", np.eye(P))
    put("ones", np.ones((P, P)))
    put("block4", (p[:, None] // 4 == np.arange(32)[None]).astype(np.float32))
    s = p[:, None, None] + P * np.arange(2)[None, :, None]
    put("causal", np.where(s <= np.arange(T)[None, None], 0.0, -1e30).reshape(P, 2 * T))
    put("partial", (p[:, None] % 32 == np.arange(2)[None]).astype(np.float32))
    put("half", (p[:, None] // 64 == np.arange(2)[None]).astype(np.float32))
    put("parity", ((p[None] // SH) % 2 == p[:, None] // 64).astype(np.float32))
    put("before", np.tile((np.arange(NE)[None] < np.arange(NE)[:, None]).reshape(1, -1), (P, 1)))
    rows = T // 64
    row = np.repeat(np.arange(rows, dtype=np.float32), 64)
    col = np.tile(np.arange(64, dtype=np.float32), rows)
    inv = np.power(np.float32(10000.0), -np.arange(0, 32, 2, dtype=np.float32) / np.float32(32)).astype(np.float32)
    ar, ac = row[:, None] * inv, col[:, None] * inv
    ang = np.concatenate([ar, ar, ac, ac], axis=-1).astype(np.float32)
    put("rope_cos", np.cos(ang).T)
    put("rope_sin", np.sin(ang).T)
    rot = np.zeros((ROPE, ROPE), np.float32)
    for i in range(16):
        rot[i, 16 + i] = -1
        rot[16 + i, i] = 1
        rot[32 + i, 48 + i] = -1
        rot[48 + i, 32 + i] = 1
    put("rotT", rot.T)
    masks = []
    for b in LEVELS:
        same = p[:, None] // (2 * b) == p[None] // (2 * b)
        masks.append(same & (p[:, None] // b != p[None] // b))
    masks.append(np.eye(P, dtype=bool))
    put("levels", np.concatenate(masks, 1).astype(np.float32))
    put("earlier", (p[:, None] < p[None]).astype(np.float32))
    put("slots", np.tile(p[None], (P, 1)))
    where, at = {}, 0
    for name, a in parts.items():
        where[name] = (at, at + a.shape[1])
        at += a.shape[1]
    return np.concatenate(list(parts.values()), 1).astype(np.float32), where


def reserve(counts):
    first, n = {}, 0
    for name, k in counts:
        first[name] = n
        n += k
    first["end"] = n
    return first


def pair_tiles():
    order = [("gate", 0), ("up", 0)]
    for u in range(PAIR_STEPS):
        if u + 1 < PAIR_STEPS:
            order += [("gate", u + 1), ("up", u + 1)]
        order.append(("down", u))
    return [(t, kind, u) for t, (kind, u) in enumerate(order)]


PAIR_TILES = pair_tiles()

MLA_ITEMS = [("cq", 0, 3), ("ckv", 0, 2), ("kr", 0, 1)]
for _h in range(AH):
    MLA_ITEMS += [("qn", _h, 1), ("qr", _h, 1)]
MLA_ITEMS += [("kn", _h, 1) for _h in range(AH)]


def mla_sequence():
    seq, waiting = [], []
    for m, (kind, h, n) in enumerate(MLA_ITEMS):
        seq += [("P", m, c) for c in range(n)]
        if waiting:
            seq.append(("S", waiting.pop(), 0))
        waiting.append(m)
        if kind == "kr":
            seq.append(("S", waiting.pop(), 0))
        if kind == "kn" and h % 4 == 3:
            seq += [("V", h // 4, a) for a in range(4)]
    seq.append(("S", waiting.pop(), 0))
    return seq


MLA_SEQ = mla_sequence()


def attention_sequence():
    seq = [("S", 0, k) for k in range(3)]
    for h in range(AH + 1):
        if h + 1 < AH:
            seq += [("S", h + 1, k) for k in range(3)]
        if h < AH:
            seq += [("T", h, k) for k in range(3)]
        if h >= 1:
            seq.append(("O", h - 1, 0))
    return seq


ATTN_SEQ = attention_sequence()

TILES = [("ada_a", 12), ("m_in", 16), ("ada_b", 36), ("m_out", 8), ("ffn0", 3 * FSTEPS), ("ada_c", 48), ("glu", 8),
         ("moe", 3 * FSTEPS * NE), ("mla_in", 3), ("mla_uq", 3), ("mla_ukv", 2), ("mla_o", 4),
         ("ffn2", 34), ("hg_z", 8), ("hg_q", 4), ("hg_i", 4), ("hg_g", 4), ("hg_o", 4),
         ("ffn3", 3 * FSTEPS)]
JOBS = [("params", 5), ("xT", 4), ("m_in", 16), ("m_qk", 16), ("m_vT", 8), ("m_gates", 1),
        ("m_fsel", 1), ("m_cT", 1), ("m_rows", NH), ("m_v", 8), ("m_head", 4 * NH), ("m_norm", 2 * NH),
        ("m_out", 4), ("ln0", 2), ("ffn0", 2 * FSTEPS), ("ln1", 2), ("s_bT", 4), ("s_cT", 4),
        ("s_pair", NPAIR), ("glu", 8), ("ln2", 2), ("router", 1), ("u_tok", 4), ("gateT", 1),
        ("places", 1), ("gates", 4), ("scatterT", 4), ("gather", 16),
        ("moe", 2 * FSTEPS * NE), ("ln3", 2), ("ctxT", 4), ("rms0", 1),
        ("mla_seq", len(MLA_SEQ)), ("rope", AH + 1), ("attn", len(ATTN_SEQ)), ("mla_o", 8), ("rms1", 1),
        ("ffn2", 4 * FSTEPS), ("rms2", 1), ("hg_z", 16), ("hg_q", 4), ("hg_i", 8), ("hg_g", 4),
        ("hg_wk", 8), ("hg_state", 4), ("hg_level", 4 * (len(LEVELS) + 2)), ("hg_norm", 4), ("hg_o", 4), ("rms3", 1),
        ("ffn3", 2 * FSTEPS), ("outT", 4)]


def build_program(nc, w, const, out):
    _, cols = shape_constants()
    tile_of, job_of = reserve(TILES), reserve(JOBS)

    with ExitStack() as ctx:
        signals = {}

        def S(name):
            if name not in signals:
                signals[name] = ctx.enter_context(nc.semaphore(name))
            return signals[name]

        def sb(name, shape, scope=ctx):
            return scope.enter_context(nc.sbuf_tensor(name, shape, F32))

        loaded = [S(f"slot_loaded{i}") for i in range(RING)]
        tile_begun = S("tile_begun")
        bank_full = [S(f"bank_full{i}") for i in range(NB)]
        bank_out = [S(f"bank_out{i}") for i in range(NB)]

        psum = ctx.enter_context(nc.psum_tensor("psum", [P, 8, BANK], F32))
        ring = sb("ring", [P, RING, SLOT])
        cst = sb("cst", [P, const.shape[1] - 2 * P])
        prow = sb("prow", [P, 5, P])
        par = sb("par", [P, 5 * P])
        xT = sb("xT", [P, DC, T])
        mod = sb("mod", [P, 4, 48, 2])
        mod1 = sb("mod1", [P, 4, 48, 2])
        csil = sb("csil", [P, DC, 3])
        small = sb("small", [P, 64])
        stat = sb("stat", [P, 2, T])
        zeros = sb("zeros", [P, P])
        router_w = sb("router_w", [P, DC, NE])
        one = sb("one", [P, 3])
        ln_eps, rms_eps = one[:, 1:2], one[:, 2:3]

        def c_(name):
            a, b = cols[name]
            return cst[:, a:b]

        ident, ones = c_("ident"), c_("ones")

        def c_one(n):
            return ones[:, 0:1].broadcast_to([P, n])

        def val(base, it, inc):
            return base if it is None else it * inc + base

        def wait_tile(pe, t, it=None, per=0):
            pe.wait_ge(loaded[t % RING], val(16 * (t // RING + 1), it, 16 * (per // RING)))

        def wait_free(pe, j, it=None, per=0):
            if it is not None or j // NB > 0:
                pe.wait_ge(bank_out[j % NB], val(j // NB, it, per // NB))

        def wait_full(eng, j, it=None, per=0):
            eng.wait_ge(bank_full[j % NB], val(j // NB + 1, it, per // NB))

        def full(ins, j):
            ins.then_inc(bank_full[j % NB], 1)

        def out_of(ins, j):
            ins.then_inc(bank_out[j % NB], 1)

        def wait_out(eng, j, it=None, per=0):
            eng.wait_ge(bank_out[j % NB], val(j // NB + 1, it, per // NB))

        def bank(j):
            return psum[:, j % NB, :]

        def repeat(eng, n, g, body):
            whole = n // g
            if whole >= 2:
                with eng.Fori(0, whole) as it:
                    for j in range(g):
                        body(it, j)
                rest = whole * g
            else:
                rest = 0
            for j in range(rest, n):
                body(None, j)

        def after_two(eng, n, g, body):
            whole = (n - 2) // g
            with eng.Fori(0, whole) as it:
                for j in range(g):
                    body(it, 2 + j)
            for j in range(2 + whole * g, n):
                body(None, j)

        def step_of(it, j, g):
            return j if it is None else it * g + j

        prow_at, prow_dmas, n_rows = {}, [], 0

        def rows_of(name, ap, width=P):
            nonlocal n_rows
            k = ap.shape[0]
            prow_at[name] = n_rows
            done = 0
            while done < k:
                r = n_rows % P
                m = min(k - done, P - r)
                prow_dmas.append((prow[r:r + m, n_rows // P, 0:width], ap[done:done + m, :]))
                done += m
                n_rows += m

        def r128(ap):
            return ap.rearrange("(a b) -> a b", b=P)

        rows_of("c", w["c"].rearrange("o (a b) -> (o a) b", b=P))
        rows_of("c_2", w["c_2"].rearrange("o (a b) -> (o a) b", b=P))
        rows_of("c_ctx_2", r128(w["c_ctx_2"]))
        for l in range(2):
            rows_of(f"ada_b{l}", r128(w["ada_b"][l]))
            rows_of(f"ada_b{l + 2}", r128(w["ada_b_2"][l]))
            for name in ("ln_mix_g", "ln_mix_b", "ln_ffn_g", "ln_ffn_b", "norm1_w_2", "norm2_w_2"):
                rows_of(f"{name}{l}", r128(w[name][l]))
        rows_of("conv_w", w["mlstm_conv_w"].rearrange("o k (a b) -> (o k a) b", b=P))
        for name in ("mlstm_conv_b", "mlstm_norm_w", "mlstm_skip", "s5_d", "s5_b_glu",
                     "mla_q_norm_w_2", "mla_kv_norm_w_2", "mla_qn_w_2", "mla_kn_w_2", "hg_o_norm_w_2"):
            rows_of(name, r128(w[name][0]))
        rows_of("lam_re", w["s5_lambda_re"].rearrange("o (a b) p -> (o a) (b p)", b=2))
        rows_of("lam_im", w["s5_lambda_im"].rearrange("o (a b) p -> (o a) (b p)", b=2))
        rows_of("lb", w["hg_lb_logits_2"].rearrange("l d (a b) -> (l d a) b", b=P))
        rows_of("mla_qr_w_2", w["mla_qr_w_2"], ROPE)
        rows_of("mla_kr_w_2", w["mla_kr_w_2"], ROPE)
        rows_of("b_gates", w["mlstm_b_gates"], 8)
        assert n_rows <= 5 * P, n_rows

        def col(name, k=0, n=1):
            a = prow_at[name] + k
            return par[:, a:a + n]

        act_in = sb("act_in", [P, DC, T])
        first = ctx.enter_context(ExitStack())
        xm = sb("xm", [P, IC, T + 4], first)
        zs = sb("zs", [P, IC, T], first)
        work = ExitStack()
        xc = sb("xc", [P, IC, T], work)
        qk = sb("qk", [P, IC, 2, T], work)
        vbuf = sb("vbuf", [P, 2, DI], work)
        bd = sb("bd", [P, 3, IC, P], work)
        qkv_small = sb("qkv_small", [P, 3, IC, 4], work)
        wgates = sb("wgates", [P, 3 * IC, 2 * NH], work)
        work.close()
        order_ = sb("order", [P, 2, P], first)
        earlier, slots = order_[:, 0], order_[:, 1]
        mod_rows = stat.rearrange("p a t -> p (a t)")
        vT = vbuf.rearrange("p a b -> p (a b)").rearrange("p (c t) -> p c t", t=T)
        xtok = zs.rearrange("p c t -> p (c t)")[:, 0:2 * D].rearrange("p (a d) -> p a d", a=2)
        hT = qk[:, :, 0, :]
        gate_rows = act_in
        nm = bd[:, 0].rearrange("p c o -> p (c o)").rearrange("p (h k t) -> p h k t", h=NH, k=2)
        decay = bd[:, 1, 0:4].rearrange("p c o -> p (c o)").rearrange("p (s t) -> p s t", s=2)
        scor = bd[:, 1, 4:12].rearrange("p c o -> p (c o)").rearrange("p (k s t) -> p k s t", k=2, s=2)
        recip_ = bd[:, 1, 12:16].rearrange("p c o -> p (c o)").rearrange("p (k t) -> p k t", k=2)
        cT = small[:, 0:8].rearrange("p (s h) -> p s h", s=2)
        res = xm.rearrange("p c t -> p (c t)")[:, 0:DC * T].rearrange("p (c t) -> p c t", t=T)
        sqr = xm.rearrange("p c t -> p (c t)")[:, DC * T:2 * DC * T].rearrange("p (c t) -> p c t", t=T)

        hid = zs[:, 0:4].rearrange("p (b a) t -> p b a t", a=2)
        sil = zs[:, 4:8].rearrange("p (b a) t -> p b a t", a=2)
        ffn_bufs = {"ffn0": (hid, sil), "moe": (hid, sil)}

        work = ExitStack()
        bmat = sb("bmat", [P, 2, NPAIR, SH], work)
        bbar = sb("bbar", [P, 2, NPAIR, SH], work)
        bpad = sb("bpad", [P, 2, DC, P], work)
        bT = sb("bT", [P, 2, DC, P], work)
        ctok = sb("ctok", [P, 2, DC, 2, SP_], work)
        cmT = sb("cmT", [P, 2, DC, P], work)
        rot = sb("rot", [P, 2, NPAIR, SL], work)
        sv = sb("sv", [P, 20, NPAIR], work)
        pairbuf = sb("pairbuf", [P, 12, T], work)
        work.close()
        dbl = pairbuf[:, 0:8].rearrange("p a t -> p (a t)").rearrange("p (j n) -> p j n", n=SL // 2)
        btmp = pairbuf[:, 8:10].rearrange("p a t -> p (a t)").rearrange("p (j n) -> p j n", n=SH)
        zris, ztmp = (pairbuf[:, 0:2], pairbuf[:, 8:10]), pairbuf[:, 6:8]
        xri, xtmp = pairbuf[:, 2:6].rearrange("p (k a) t -> p k a t", k=2), pairbuf[:, 10:12]
        carry = small[:, 16:22].rearrange("p (k n) -> p k n", n=2)
        gT = zs[:, 8:16]

        work = ExitStack()
        gate_bc = sb("gate_bc", [P, NE, T], work)
        gate8 = sb("gate8", [P, T], work)
        lg = sb("lg", [P, 8, 2, NE], work)
        cmp_ = sb("cmp_", [P, 2, 2, NE, NE], work)
        place = sb("place", [P, 2, NE], work)
        crowd = sb("crowd", [P, NE], work)
        gather = sb("gather", [P, 2, NE, SLOTS], work)
        scatterT = sb("scatterT", [P, NE, T], work)
        xe = sb("xe", [P, DC, NE * SLOTS], work)
        ye = sb("ye", [P, D], work)
        crowded = work.enter_context(nc.sbuf_tensor("crowded", [P, 1], mybir.dt.int32))
        work.close()
        u_tok = zs[:, 8:16].rearrange("p c t -> p (c t)").rearrange("p (a d) -> p a d", a=2)
        wgather = sqr.rearrange("p c t -> p (c t)").rearrange("p (a e s) -> p a e s", a=2, e=NE)

        first.close()
        second = ctx.enter_context(ExitStack())
        T2 = 2 * T
        ctxT = sb("ctxT", [P, DC, T], second)
        a2 = sb("a2", [P, DC, T2], second)
        norm_gain = sb("norm_gain", [P, DC, 2], second)
        rstd2 = sb("rstd2", [P, T2], second)
        halves = (xT, ctxT)

        work = ExitStack()
        qn = sb("qn", [P, AH, T2], work)
        qr = sb("qr", [P, AH, T2], work)
        kn = sb("kn", [P, AH, T2], work)
        vtok = sb("vtok", [P, 4, D], work)
        cq = sb("cq", [P, 3, T2], work)
        ckv = sb("ckv", [P, 2, T2], work)
        kr = sb("kr", [P, 1, T2], work)
        nstat = sb("nstat", [P, 2, T2], work)
        prob = sb("prob", [P, 2, 3, T2], work)
        smax = sb("smax", [P, 2, 16], work)
        work.close()
        nsq = prob[:, 0]
        rms_sq = qn
        probTs = [x.rearrange("p a t -> p (a t)")[:, 0:6 * T].rearrange("p (s t) -> p s t", t=T) for x in (cq, act_in)]
        oT = a2
        ctx_tok = qn.rearrange("p h t -> p (h t)")[:, 0:2 * D].rearrange("p (a d) -> p a d", a=2)
        rope_tmp = prob[:, 1]
        mla_buf = {"cq": cq, "ckv": ckv, "kr": kr, "qn": qn, "qr": qr, "kn": kn}
        mla_job = {key: job_of["mla_seq"] + n for n, key in enumerate(MLA_SEQ)}
        attn_job = {key: job_of["attn"] + n for n, key in enumerate(ATTN_SEQ)}

        def item_of(m):
            kind, h, n = MLA_ITEMS[m]
            rows = ROPE if kind in ("qr", "kr") else P
            weight = {"cq": "mla_q_norm_w_2", "ckv": "mla_kv_norm_w_2", "kr": "mla_kr_w_2", "qn": "mla_qn_w_2",
                      "qr": "mla_qr_w_2", "kn": "mla_kn_w_2"}[kind]
            slots = {"cq": (0, 1, 2), "ckv": (0, 1), "kr": (2,)}.get(kind, (m % 3,))
            return kind, h, n, rows, mla_buf[kind], weight, slots

        work = ExitStack()
        hid2 = sb("hid2", [P, FC, T2], work)
        sil2 = sb("sil2", [P, 2, T2], work)
        work.close()
        rms_sq2 = hid2[:, 0:DC]

        work = ExitStack()
        lf = sb("lf", [P, 2, AH, T2], work)
        kf = sb("kf", [P, 2, AH, T2], work)
        itok = sb("itok", [P, 4, D], work)
        ework2 = sb("ework2", [P, 2, AH, T], work)
        lbs = sb("lbs", [P, 3, 16], work)
        work.close()
        ework = a2.rearrange("p c t -> p (c t)").rearrange("p (k h t) -> p k h t", k=2, h=AH)
        eworks = (ework, ework2)
        wkT = ework2.rearrange("p k h t -> p (k h t)").rearrange("p (i s) -> p i s", s=P)
        qh = act_in
        gsil = ctxT
        atts = [lf[:, b // 2, 4 * (b % 2):4 * (b % 2) + 4, T:T + P] for b in range(4)]
        hstat = itok[:, 0:2].rearrange("p a d -> p (a d)").rearrange("p (h t) -> p h t", h=AH)
        state = kf
        rms_sq3 = kf[:, 0].rearrange("p h t -> p (h t)")[:, 0:DC * T].rearrange("p (c t) -> p c t", t=T)
        hid3 = gsil[:, 0:4].rearrange("p (b a) t -> p b a t", a=2)
        sil3 = gsil[:, 4:8].rearrange("p (b a) t -> p b a t", a=2)
        ffn_bufs["ffn3"] = (hid3, sil3)

        def lo_half(x, b):
            return x.rearrange("p h (n t) -> p h n t", t=2 * b)[:, :, :, 0:b]

        def hi_half(x, b):
            return x.rearrange("p h (n t) -> p h n t", t=2 * b)[:, :, :, b:2 * b]

        out_tok = ework2.rearrange("p k h t -> p (k h t)")[:, 0:2 * D].rearrange("p (a d) -> p a d", a=2)

        block = ctx.enter_context(nc.Block())

        @block.sync
        def _(sp):
            def load(t, width, shape, src, it=None, per=0):
                if it is not None or t >= RING:
                    sp.wait_ge(tile_begun, val(t - RING + 2, it, per))
                dst = ring[:, t % RING, 0:width]
                for pattern, dims in shape:
                    dst = dst.rearrange(pattern, **dims)
                sp.dma_start(dst, src).then_inc(loaded[t % RING], 16)

            def load_cols(t, mat, n0, n, k0=0, kc=DC, it=None, per=0):
                src = mat[k0 * P:(k0 + kc) * P].rearrange("(c p) n -> p c n", p=P)[:, :, bass.ds(n0, n)]
                load(t, kc * n, [("p (c n) -> p c n", dict(c=kc))], src, it, per)

            def load_rows(t, mat, k0, it=None, per=0):
                src = mat[bass.ds(k0, 2 * P)].rearrange("(c p) n -> p c n", p=P)
                load(t, 2 * D, [("p (c n) -> p c n", dict(c=2))], src, it, per)

            def ada(t0, mat, n0, tiles):
                def body(it, j):
                    load_cols(t0 + j, mat, step_of(it, j, 6) * 256 + n0, 256, it=it, per=6)
                for j in range(6):
                    body(None, j)
                with sp.Fori(1, tiles // 6) as it:
                    for j in range(6):
                        body(it, j)

            def ffn(t0, gate, up, down, steps=FSTEPS):
                def pair(t, s, it):
                    e = s // FSTEPS if steps > FSTEPS else 0
                    for i, mat in enumerate((gate, up)):
                        rows = mat[bass.ds(e * D, D)] if steps > FSTEPS else mat
                        load_cols(t + i, rows, (s % FSTEPS) * 256, 256, it=it, per=6)

                pair(t0, 0, None)

                def body(it, j):
                    s = step_of(it, j, 2)
                    t = t0 + 2 + 3 * j
                    pair(t, s + 1, it)
                    load_rows(t + 2, down, s * 256, it=it, per=6)
                repeat(sp, steps - 1, 2, body)
                load_rows(t0 + 3 * steps - 1, down, (steps - 1) * 256)

            def stage_prep():
                sp.dma_start(cst[:], const[:, 0:cst.shape[1]]).then_inc(S("params_in"), 16)
                sp.wait_ge(S("prow_zero"), 1)
                for dst, src in prow_dmas:
                    sp.dma_start(dst, src).then_inc(S("params_in"), 16)
                sp.dma_start(xtok[:], w["x"][0].rearrange("(a p) d -> p a d", p=P)).then_inc(S("x_in"), 16)
                for i, name in enumerate(("mlstm_wq", "mlstm_wk", "mlstm_wv")):
                    src = w[name][0].rearrange("(c n) i o -> (n i) c o", n=32)
                    sp.dma_start(qkv_small[:, i], src).then_inc(S("mlstm_small_in"), 16)
                sp.dma_start(wgates[:], w["mlstm_w_gates"][0].rearrange("(c p) g -> p c g", p=P)
                             ).then_inc(S("mlstm_small_in"), 16)

            def stage_ada0():
                ada(tile_of["ada_a"], w["ada_w"][0], 0, 12)

            def stage_mlstm():
                t0 = tile_of["m_in"]
                for j in range(16):
                    load_cols(t0 + j, w["mlstm_w_in"][0], 256 * j, 256)
                ada(tile_of["ada_b"], w["ada_w"][0], 12 * 256, 12)
                ada(tile_of["ada_b"] + 12, w["ada_w"][1], 0, 24)
                t0 = tile_of["m_out"]
                for j in range(8):
                    load_cols(t0 + j, w["mlstm_w_out"][0], 256 * (j // 2), 256, k0=8 * (j % 2))

            def stage_ffn0():
                w13 = w["ffn_w13"][0]
                ffn(tile_of["ffn0"], w13[:, 0:FF], w13[:, FF:2 * FF], w["ffn_w2"][0])

            def stage_s5():
                sp.dma_start(order_[:], const[:, cst.shape[1]:].rearrange("p (i s) -> p i s", i=2)
                             ).then_inc(S("order_in"), 16)
                for l in range(2):
                    ada(tile_of["ada_c"] + 24 * l, w["ada_w_2"][l], 0, 24)
                t0, glu = tile_of["glu"], w["s5_w_glu"][0]
                for j in range(4):
                    load_cols(t0 + 2 * j, glu, 256 * j, 256)
                    load_cols(t0 + 2 * j + 1, glu, D + 256 * j, 256)

            def stage_moe():
                w13, down = w["moe_w13"][0], w["moe_w2"][0]

                def step(pe_order, it):
                    for t, kind, u in pe_order:
                        expert = it * 2 + u // FSTEPS
                        if kind == "down":
                            mat = down[bass.ds(expert, 1)].rearrange("e k n -> (e k) n")
                            load_rows(tile_of["moe"] + t, mat, (u % FSTEPS) * 256, it=it, per=3 * PAIR_STEPS)
                        else:
                            mat = w13[bass.ds(expert, 1)].rearrange("e k n -> (e k) n")
                            load_cols(tile_of["moe"] + t, mat, (u % FSTEPS) * 256 + (FF if kind == "up" else 0), 256,
                                      it=it, per=3 * PAIR_STEPS)
                with sp.Fori(0, NE // 2) as it:
                    step(PAIR_TILES, it)

            def stage_mla():
                sp.wait_ge(S("moe_done"), 1)
                sp.dma_start(ctx_tok, w["ctx_2"][0].rearrange("(a p) d -> p a d", p=P)).then_inc(S("ctx_in"), 16)
                mat, t = w["mla_w_in_2"][0], tile_of["mla_in"]
                load_cols(t, mat, 0, 256)
                load_cols(t + 1, mat, 256, 256)
                load_cols(t + 2, mat, 512, 192)
                mat, t = w["mla_w_uq_2"][0], tile_of["mla_uq"]
                for i in range(3):
                    load_cols(t + i, mat, 576 * i, 576 if i < 2 else 384, kc=QR // P)
                mat, t = w["mla_w_ukv_2"][0], tile_of["mla_ukv"]
                for i in range(2):
                    load_cols(t + i, mat, 1024 * i, 1024, kc=KVR // P)
                for i in range(4):
                    load_cols(tile_of["mla_o"] + i, w["mla_w_o_2"][0], 256 * i, 256)

            def stage_ffn2():
                t0 = tile_of["ffn2"]

                def body(it, j):
                    s = step_of(it, j, 3)
                    load_cols(t0 + 2 * j, w["ffn_w1_2"][0], s * 256, 256, it=it, per=6)
                    load_cols(t0 + 2 * j + 1, w["ffn_w3_2"][0], s * 256, 256, it=it, per=6)
                repeat(sp, FSTEPS, 3, body)
                for i in range(12):
                    k0 = 4 * (i % 6)
                    load_cols(t0 + 22 + i, w["ffn_w2_2"][0], 512 * (i // 6), 512, k0=k0, kc=min(4, FC - k0))

            def stage_hg():
                mat = w["hg_w_in_2"][0]
                for i in range(8):
                    load_cols(tile_of["hg_z"] + i, mat, D + 256 * i, 256)
                for i in range(4):
                    load_cols(tile_of["hg_q"] + i, mat, 256 * i, 256)
                for i in range(4):
                    load_cols(tile_of["hg_i"] + i, mat, 3 * D + 256 * i, 256)
                for i in range(4):
                    load_cols(tile_of["hg_g"] + i, mat, 4 * D + 256 * i, 256)
                for i in range(4):
                    load_cols(tile_of["hg_o"] + i, w["hg_w_o_2"][0], 256 * i, 256)

            def stage_ffn3():
                ffn(tile_of["ffn3"], w["ffn_w1_2"][1], w["ffn_w3_2"][1], w["ffn_w2_2"][1])

            def stage_out():
                sp.wait_ge(S("out_tok_ready"), 1)
                sp.dma_start(out[0].rearrange("(a p) d -> p a d", p=P), out_tok).then_inc(S("out_written"), 16)
                sp.wait_ge(S("out_written"), 16)

            stage_prep()
            stage_ada0()
            stage_mlstm()
            stage_ffn0()
            stage_s5()
            stage_moe()
            stage_mla()
            stage_ffn2()
            stage_hg()
            stage_ffn3()
            stage_out()

        @block.tensor
        def _(pe):
            def mm_pair(t, j, src, kc=DC, start=True, stop_=True, it=None, per_t=0, per_j=0, width=256):
                wait_tile(pe, t, it, per_t)
                wait_free(pe, j, it, per_j)
                tile = ring[:, t % RING, :]
                for n in range(2):
                    for k in range(kc):
                        last = pe.matmul(bank(j)[:, n * T:(n + 1) * T],
                                         tile[:, k * width + n * P:k * width + (n + 1) * P], src(k),
                                         start=start and k == 0, stop=stop_ and k == kc - 1)
                        if n == 0 and k == 0:
                            last.then_inc(tile_begun, 1)
                full(last, j)

            def stats(j, src, n, width=T, rows=P):
                wait_free(pe, j)
                for k in range(n):
                    last = pe.matmul(bank(j)[0:rows, 0:width], ones[0:rows, 0:rows], src(k), start=k == 0, stop=k == n - 1)
                full(last, j)

            def turn(j, srcs, rows=P):
                wait_free(pe, j)
                for i, src in enumerate(srcs):
                    n = src.shape[0]
                    m = src.free_size()
                    last = pe.transpose(bank(j)[0:m, i * P:i * P + n], src, ident[0:n, 0:n])
                full(last, j)

            def ada_columns(stage, s, n):
                pe.wait_ge(S("mod_rows_out"), ADA_STAGES[stage][0] + s + 1)
                swapped = (tile_of[f"ada_{stage}"] + 2 * s) % RING == RING - 1
                for m in range(4):
                    at = (4 * s + (m + 2 * swapped) % 4) * n + (24 if stage == "b" else 0)
                    last = pe.matmul(psum[:, 7, at:at + n], mod_rows[:, m * P:(m + 1) * P], c_("partial")[:, 0:n],
                                     start=True, stop=True)
                return last

            def ada_step(stage, s, who, n):
                if s == 0:
                    pe.wait_ge(S("csil_ready"), 1)
                    if stage != "b":
                        pe.matmul(psum[:, 6, :], zeros[:], cst[:, 0:BANK], start=True, stop=True)
                else:
                    ada_columns(stage, s - 1, n)
                t = tile_of[f"ada_{stage}"] + 2 * s
                wait_tile(pe, t)
                wait_tile(pe, t + 1)
                slots = ring[:, 0:RING:RING - 1] if t % RING == RING - 1 else ring[:, t % RING:t % RING + 2]
                for k in range(DC):
                    g = 32 * (k % 4)
                    last = pe.matmul(psum[g:g + n, 6, :], csil[:, k, who:who + n],
                                     slots[:, :, k * 256:(k + 1) * 256],
                                     start=k < 4, stop=k >= 4, skip_group_check=True)
                    if k in (0, DC - 1):
                        last.then_inc(tile_begun, 1)

            def ada_end(stage, n):
                ada_columns(stage, ADA_STAGES[stage][1] - 1, n).then_inc(S("mods_full"), 1)

            def layer_norm(i):
                pe.wait_ge(S("ln_sum_ready"), i + 1)
                stats(job_of[f"ln{i}"], lambda k: res[:, k], DC)
                pe.wait_ge(S("ln_sq_ready"), i + 1)
                stats(job_of[f"ln{i}"] + 1, lambda k: sqr[:, k], DC)

            def ffn(name, steps, ready):
                hid = ffn_bufs[name][0]
                t0, j0 = tile_of[name], job_of[name]
                ready()
                for b in range(4):
                    pe.matmul(psum[:, NB + b, :], zeros[:], cst[:, 0:BANK],
                              start=True, stop=False, skip_group_check=True)
                mm_pair(t0, j0, lambda k: act_in[:, k])
                mm_pair(t0 + 1, j0 + 1, lambda k: act_in[:, k])

                def down(t, i, it, last_step=False):
                    wait_tile(pe, t, it, 6)
                    wait_out(pe, j0 + 2 * i + 1, it, 4)
                    for n in range(DC):
                        for k in range(2):
                            last = pe.matmul(psum[:, NB + n // 2, (n % 2) * T:(n % 2 + 1) * T],
                                             ring[:, t % RING, k * D + n * P:k * D + (n + 1) * P],
                                             hid[:, i % 2, k], start=False, stop=last_step and k == 1,
                                             skip_group_check=True)
                            if n == 0 and k == 0:
                                last.then_inc(tile_begun, 1)
                    last.then_inc(S(f"{name}_down"), 1)

                def body(it, i):
                    t, j = t0 + 2 + 3 * i, j0 + 2 + 2 * i
                    mm_pair(t, j, lambda k: act_in[:, k], it=it, per_t=6, per_j=4)
                    mm_pair(t + 1, j + 1, lambda k: act_in[:, k], it=it, per_t=6, per_j=4)
                    down(t + 2, i, it)
                repeat(pe, steps - 1, 2, body)
                down(t0 + 3 * steps - 1, steps - 1, None, True)

            def stage_prep():
                pe.wait_ge(S("params_in"), 16 * (1 + len(prow_dmas)))
                for g in range(5):
                    turn(job_of["params"] + g, [prow[:, g, :]])
                pe.wait_ge(S("x_in"), 16)
                for g in range(4):
                    turn(job_of["xT"] + g, [xtok[:, a, (2 * g + d) * P:(2 * g + d + 1) * P]
                                            for d in range(2) for a in range(2)])

            def stage_ada0():
                for i in range(6):
                    ada_step("a", i, 0, 1)
                ada_end("a", 1)

            def stage_mlstm():
                pe.wait_ge(S("mlstm_in_ready"), 1)
                for j in range(16):
                    mm_pair(tile_of["m_in"] + j, job_of["m_in"] + j, lambda k: act_in[:, k])
                pe.wait_ge(S("block_diag_ready"), 3)
                for c in range(IC):
                    j = job_of["m_qk"] + c
                    pe.wait_ge(S("conv_ready"), c + 1)
                    wait_free(pe, j)
                    for i in range(2):
                        last = pe.matmul(bank(j)[:, i * T:(i + 1) * T], bd[:, i, c], xc[:, c], start=True, stop=True)
                    full(last, j)
                    if c % 2:
                        ada_step("b", c // 2, 0, 1)
                for g in range(8):
                    j = job_of["m_vT"] + g
                    wait_free(pe, j)
                    for i in range(2):
                        last = pe.matmul(bank(j)[:, i * T:(i + 1) * T], bd[:, 2, 2 * g + i], xm[:, 2 * g + i, 4:4 + T],
                                         start=True, stop=True)
                    full(last, j)
                j = job_of["m_gates"]
                wait_free(pe, j)
                wait_out(pe, job_of["m_qk"] + IC - 1)
                wait_out(pe, job_of["m_vT"] + 7)
                for i in range(3):
                    for c in range(IC):
                        src = vT[:, c] if i == 2 else qk[:, c, i]
                        last = pe.matmul(bank(j)[0:8, 0:T], wgates[:, i * IC + c], src,
                                         start=i == 0 and c == 0, stop=i == 2 and c == IC - 1)
                full(last, j)
                j = job_of["m_fsel"]
                wait_free(pe, j)
                wait_out(pe, job_of["m_gates"])
                full(pe.matmul(bank(j)[0:NH, 0:T], ident[0:8, NH:2 * NH], gate_rows[0:8, 0], start=True, stop=True), j)
                for i in range(2):
                    ada_step("b", 8 + i, 0, 1)
                j = job_of["m_cT"]
                wait_free(pe, j)
                pe.wait_ge(S("gate_rows_ready"), 1)
                for a in range(2):
                    last = pe.matmul(bank(j)[:, a * NH:(a + 1) * NH], gate_rows[0:NH, 4, a * P:(a + 1) * P],
                                     ident[0:NH, 0:NH], start=True, stop=True)
                full(last, j)
                for h in range(NH):
                    j = job_of["m_rows"] + h
                    wait_free(pe, j)
                    full(pe.matmul(bank(j), ident[0:NH, h:h + 1].broadcast_to([NH, P]),
                                   gate_rows[0:NH, 5:7].rearrange("p a t -> p (a t)"), start=True, stop=True), j)
                for g in range(8):
                    a, c0 = g // 4, 4 * (g % 4)
                    j = job_of["m_v"] + g
                    wait_free(pe, j)
                    for c in range(4):
                        last = pe.matmul(bank(j)[:, c * P:(c + 1) * P], xm[:, c0 + c, 4 + a * P:4 + (a + 1) * P],
                                         bd[:, 2, c0 + c], start=True, stop=True)
                    full(last, j)
                for h in range(NH):
                    j = job_of["m_head"] + 4 * h
                    wait_free(pe, j)
                    for s in range(2):
                        for c in range(HC):
                            last = pe.matmul(bank(j)[:, s * T:(s + 1) * T], qk[:, h * HC + c, 1, s * P:(s + 1) * P],
                                             qk[:, h * HC + c, 0], start=c == 0, stop=c == HC - 1)
                    full(last, j)
                    ada_step("b", 10 + 2 * h, 0, 1)
                    wait_out(pe, j)
                    stats(j + 1, lambda s: scor[:, h % 2, s], 2)
                    wait_out(pe, job_of["m_v"] + 7)
                    for g in range(2):
                        wait_free(pe, j + 2 + g)
                        for e in range(2):
                            for s in range(2):
                                at = h * DH + (2 * g + e) * P
                                last = pe.matmul(bank(j + 2 + g)[:, e * T:(e + 1) * T], vbuf[:, s, at:at + P],
                                                 scor[:, h % 2, s], start=s == 0, stop=s == 1)
                        full(last, j + 2 + g)
                    ada_step("b", 11 + 2 * h, 0, 1)
                ada_end("b", 1)
                for h in range(NH):
                    j = job_of["m_norm"] + 2 * h
                    wait_out(pe, job_of["m_head"] + 4 * h + 3)
                    stats(j, lambda k: hT[:, h * HC + k], HC)
                    pe.wait_ge(S("h_sq_ready"), h + 1)
                    stats(j + 1, lambda k: vT[:, (h % 2) * HC + k], HC)
                pe.wait_ge(S("h_out_ready"), 1)
                for g in range(4):
                    t, j = tile_of["m_out"] + 2 * g, job_of["m_out"] + g
                    wait_tile(pe, t)
                    wait_tile(pe, t + 1)
                    wait_free(pe, j)
                    for n in range(2):
                        for k in range(IC):
                            last = pe.matmul(bank(j)[:, n * T:(n + 1) * T],
                                             ring[:, (t + k // 8) % RING, (k % 8) * 256 + n * P:(k % 8) * 256 + (n + 1) * P],
                                             hT[:, k], start=k == 0, stop=k == IC - 1)
                            if (n, k) in ((0, 0), (1, 8)):
                                last.then_inc(tile_begun, 1)
                    full(last, j)
                layer_norm(0)

            def stage_ffn0():
                ffn("ffn0", FSTEPS, lambda: pe.wait_ge(S("ffn0_in_ready"), 1))
                layer_norm(1)

            def stage_s5():
                pe.wait_ge(S("bpad_ready"), 1)
                for g in range(4):
                    turn(job_of["s_bT"] + g, [bpad[:, g // 2, 4 * (g % 2) + i] for i in range(4)])
                pe.wait_ge(S("s5_in"), 7 * 16)
                for g in range(4):
                    turn(job_of["s_cT"] + g, [ctok[:, g // 2, 4 * (g % 2) + i].rearrange("p d s -> p (d s)")
                                              for i in range(4)])
                pe.wait_ge(S("s5_u_ready"), 1)
                wait_out(pe, job_of["s_cT"] + 3)

                def drive(p):
                    c, r = p // 4, 32 * (p % 4)
                    j = job_of["s_pair"] + p
                    wait_free(pe, j)
                    for i in range(2):
                        last = pe.matmul(bank(j)[:, i * T:(i + 1) * T], bT[r:r + 32, i, c], act_in[r:r + 32, c],
                                         start=True, stop=True)
                    full(last, j)

                drive(0)
                drive(1)
                for p in range(NPAIR):
                    if p + 2 < NPAIR:
                        drive(p + 2)
                    c, r = p // 4, 32 * (p % 4)
                    pe.wait_ge(S("s5_x_ready"), p + 1)
                    if p % 4 == 0 and c >= 2:
                        pe.wait_ge(S("s5_y_out"), c - 1)
                    for i in range(2):
                        last = pe.matmul(psum[r:r + 32, NB + c % 2, 0:T], cmT[:, i, c, r:r + 32], xri[:, p % 2, i],
                                         start=i == 0, stop=i == 1)
                    last.then_inc(S("s5_x_used"), 1)
                    if p % 4:
                        ada_step("c", 3 * (p // 4) + p % 4 - 1, 1, 2)
                ada_end("c", 2)
                pe.wait_ge(S("gelu_ready"), DC)
                for j in range(8):
                    mm_pair(tile_of["glu"] + j, job_of["glu"] + j, lambda k: gT[:, k])
                layer_norm(2)

            def stage_moe():
                pe.wait_ge(S("moe_in_ready"), 1)
                j = job_of["router"]
                wait_free(pe, j)
                for a in range(2):
                    for k in range(DC):
                        last = pe.matmul(bank(j)[:, a * NE:(a + 1) * NE], act_in[:, k, a * P:(a + 1) * P], router_w[:, k],
                                         start=k == 0, stop=k == DC - 1)
                full(last, j)
                for g in range(4):
                    a, c0 = g // 2, 4 * (g % 2)
                    turn(job_of["u_tok"] + g, [act_in[:, c0 + i, a * P:(a + 1) * P] for i in range(4)])
                pe.wait_ge(S("top2_ready"), 1)
                turn(job_of["gateT"], [lg[:, 6, 0], lg[:, 6, 1]])
                j = job_of["places"]
                pe.wait_ge(S("order_in"), 16)
                wait_free(pe, j)
                chosen = lg[:, 3]
                pe.matmul(bank(j)[:, 0:NE], earlier, chosen[:, 0], start=True, stop=True)
                for a, lhs in ((0, ones), (1, earlier)):
                    pe.matmul(bank(j)[:, NE:2 * NE], lhs, chosen[:, a], start=a == 0, stop=a == 1)
                for a in range(2):
                    last = pe.matmul(bank(j)[:, 2 * NE:3 * NE], ones, chosen[:, a], start=a == 0, stop=a == 1)
                full(last, j)
                wait_out(pe, job_of["gateT"])
                for g in range(4):
                    j = job_of["gates"] + g
                    wait_free(pe, j)
                    for i in range(2):
                        last = pe.matmul(bank(j)[:, i * T:(i + 1) * T],
                                         ident[0:NE, 2 * g + i:2 * g + i + 1].broadcast_to([NE, P]), gate8[0:NE],
                                         start=True, stop=True)
                    full(last, j)
                pe.wait_ge(S("slots_ready"), 1)
                for g in range(4):
                    turn(job_of["scatterT"] + g, [wgather[:, a, 2 * g + i] for i in range(2) for a in range(2)])
                wait_out(pe, job_of["u_tok"] + 3)
                for g in range(16):
                    j, c, e4 = job_of["gather"] + g, g // 2, 4 * (g % 2)
                    wait_free(pe, j)
                    for a in range(2):
                        last = pe.matmul(bank(j), u_tok[:, a, c * P:(c + 1) * P],
                                         gather[:, a, e4:e4 + 4].rearrange("p e s -> p (e s)"), start=a == 0, stop=a == 1)
                    full(last, j)
                wait_out(pe, job_of["gather"] + 15)
                wait_out(pe, job_of["gather"] + 14)

                def experts(gathered):
                    t0, j0 = tile_of["moe"], job_of["moe"]
                    per_t, per_j = 3 * PAIR_STEPS, 2 * PAIR_STEPS
                    n_cols = SLOTS if gathered else T
                    for i in range(2):
                        pe.drain().then_inc(S("hidden_free"), 1)
                    if not gathered:
                        for b in range(4):
                            pe.matmul(psum[:, NB + b, :], zeros[:], cst[:, 0:BANK],
                                      start=True, stop=False, skip_group_check=True)

                    def gate_or_up(t, j, u, it):
                        wait_tile(pe, t, it, per_t)
                        wait_free(pe, j, it, per_j)
                        for n in range(2):
                            for k in range(DC):
                                src = (xe[:, k, bass.ds((it * 2 + u // FSTEPS) * SLOTS, SLOTS)] if gathered
                                       else act_in[:, k])
                                last = pe.matmul(bank(j)[:, n * n_cols:(n + 1) * n_cols],
                                                 ring[:, t % RING, k * 256 + n * P:k * 256 + (n + 1) * P], src,
                                                 start=k == 0, stop=k == DC - 1)
                                if n == 0 and k == 0:
                                    last.then_inc(tile_begun, 1)
                        full(last, j)

                    def down(t, u, it):
                        wait_tile(pe, t, it, per_t)
                        wait_out(pe, j0 + 2 * u + 1, it, per_j)
                        tile = ring[:, t % RING]
                        for k in range(2):
                            if gathered:
                                for n in range(2):
                                    last = pe.matmul(psum[:, NB + n, :], hid[:, u % 2, k, 0:SLOTS],
                                                     tile[:, k * D + n * BANK:k * D + (n + 1) * BANK],
                                                     start=u % FSTEPS == 0 and k == 0,
                                                     stop=u % FSTEPS == FSTEPS - 1 and k == 1, skip_group_check=True)
                                    if n == 0 and k == 0:
                                        last.then_inc(tile_begun, 1)
                            else:
                                for n in range(DC):
                                    last = pe.matmul(psum[:, NB + n // 2, (n % 2) * T:(n % 2 + 1) * T],
                                                     tile[:, k * D + n * P:k * D + (n + 1) * P], hid[:, u % 2, k],
                                                     start=False, stop=False, skip_group_check=True)
                                    if n == 0 and k == 0:
                                        last.then_inc(tile_begun, 1)
                        last.then_inc(S("hidden_free"), 1)

                    def scatter(e, it):
                        pe.wait_ge(S("ye_ready"), val(e + 1, it, 2))
                        for g in range(4):
                            pe.wait_ge(S("scatter_free"), val(4 * e + g + 1, it, 8))
                            for n in range(2):
                                last = pe.matmul(psum[:, NB + 2 + g % 2, n * T:(n + 1) * T],
                                                 ye[:, (2 * g + n) * P:(2 * g + n + 1) * P],
                                                 scatterT[:, bass.ds(it * 2 + e, 1), :].rearrange("p o t -> p (o t)"),
                                                 start=True, stop=True)
                            last.then_inc(S("scatter_full"), 1)

                    with pe.Fori(0, NE // 2) as it:
                        for t, kind, u in PAIR_TILES:
                            if kind == "down":
                                if gathered and u == FSTEPS:
                                    scatter(0, it)
                                down(t0 + t, u, it)
                            else:
                                gate_or_up(t0 + t, j0 + 2 * u + (kind == "up"), u, it)
                        if gathered:
                            scatter(1, it)

                is_crowded = pe.value_load(crowded[0:1, 0:1], min_val=0, max_val=1)
                with pe.If(is_crowded != 0):
                    experts(False)
                with pe.Else():
                    experts(True)
                layer_norm(3)

            def mm_wide(j, t, col0, rows, src, kc, width, first):
                wait_free(pe, j)
                for k in range(kc):
                    at = k * width + col0
                    last = pe.matmul(bank(j)[0:rows], ring[:, t % RING, at:at + rows], src(k), start=k == 0, stop=k == kc - 1)
                    if first and k == 0:
                        last.then_inc(tile_begun, 1)
                full(last, j)

            def rms2(i, srcs):
                pe.wait_ge(S("rms_sq_ready"), i + 1)
                j = job_of[f"rms{i}"]
                wait_free(pe, j)
                for n, src in enumerate(srcs):
                    for k in range(DC):
                        last = pe.matmul(bank(j)[:, n * T:(n + 1) * T], ones, src(k), start=k == 0, stop=k == DC - 1)
                full(last, j)

            def stage_mla():
                pe.wait_ge(S("ctx_in"), 16)
                for g in range(4):
                    turn(job_of["ctxT"] + g, [ctx_tok[:, a, (2 * g + d) * P:(2 * g + d + 1) * P]
                                              for d in range(2) for a in range(2)])
                rms2(0, [lambda k: rms_sq[:, k, 0:T], lambda k: rms_sq[:, k, T:T2]])
                pe.wait_ge(S("a2_ready"), 1)
                for key in MLA_SEQ:
                    kind, m, c = key
                    j = mla_job[key]
                    if kind == "V":
                        t = tile_of["mla_ukv"] + m
                        wait_free(pe, j)
                        for k in range(2):
                            cols4 = ring[:, t % RING, k * 1024:(k + 1) * 1024].rearrange("p (h n) -> p h n", n=256)[:, :, P:]
                            last = pe.matmul(bank(j).rearrange("p (h n) -> p h n", n=P), ckv[:, k, c * P:(c + 1) * P],
                                             cols4, start=k == 0, stop=k == 1)
                        full(last, j)
                        continue
                    name, h, n, rows, dst, weight, slots = item_of(m)
                    if kind == "S":
                        pe.wait_ge(S("nsq_ready"), m + 1)
                        stats(j, lambda k: nsq[0:rows, slots[k]], n, T2, rows)
                        continue
                    if name in ("cq", "ckv", "kr"):
                        n0 = c + {"cq": 0, "ckv": 3, "kr": 5}[name]
                        t = tile_of["mla_in"] + n0 // 2
                        if n0 % 2 == 0:
                            wait_tile(pe, t)
                        mm_wide(j, t, P * (n0 % 2), rows, lambda k: a2[:, k], DC, 192 if n0 >= 4 else 256, n0 % 2 == 0)
                    elif name in ("qn", "qr"):
                        if h == 0:
                            pe.wait_ge(S("item_normed"), 1)
                        t, first_ = tile_of["mla_uq"] + h // 3, name == "qn" and h % 3 == 0
                        if first_:
                            wait_tile(pe, t)
                        mm_wide(j, t, 192 * (h % 3) + (P if name == "qr" else 0), rows, lambda k: cq[:, k], 3,
                                384 if h >= 6 else 576, first_)
                    else:
                        if h == 0:
                            pe.wait_ge(S("item_normed"), 2)
                        t = tile_of["mla_ukv"] + h // 4
                        if h % 4 == 0:
                            wait_tile(pe, t)
                        mm_wide(j, t, 256 * (h % 4), rows, lambda k: ckv[:, k], 2, 1024, h % 4 == 0)
                pe.wait_ge(S("item_normed"), len(MLA_ITEMS))
                for i in range(AH + 1):
                    j = job_of["rope"] + i
                    wait_free(pe, j)
                    src = kr[0:ROPE, 0, 0:T] if i == 0 else qr[0:ROPE, i - 1, 0:T]
                    full(pe.matmul(bank(j)[0:ROPE, 0:T], c_("rotT")[0:ROPE], src, start=True, stop=True), j)
                pe.wait_ge(S("rope_ready"), AH + 1)
                for kind, h, k in ATTN_SEQ:
                    j = attn_job[kind, h, k]
                    if kind == "S":
                        wait_free(pe, j)
                        spans = [(k * P, 0, T2, 0)] if k < 2 else [(T + a * P, T, T, a * T) for a in range(2)]
                        for q0, k0, n, at in spans:
                            pe.matmul(bank(j)[:, at:at + n], qn[:, h, q0:q0 + P], kn[:, h, k0:k0 + n], start=True, stop=False)
                            last = pe.matmul(bank(j)[:, at:at + n], qr[0:ROPE, h, q0:q0 + P], kr[0:ROPE, 0, k0:k0 + n],
                                             start=False, stop=True)
                        full(last, j)
                    elif kind == "T":
                        pe.wait_ge(S("prob_ready"), 3 * h + k + 1)
                        turn(j, [prob[:, h % 2, k, s * P:(s + 1) * P] for s in range(4)])
                    else:
                        wait_out(pe, attn_job["T", h, 2])
                        wait_free(pe, j)
                        for s in range(4):
                            pe.matmul(bank(j)[:, 0:T], vtok[:, s, h * P:(h + 1) * P], probTs[h % 2][:, s],
                                      start=s == 0, stop=s == 3)
                        for s in range(2):
                            last = pe.matmul(bank(j)[:, T:T2], vtok[:, 2 + s, h * P:(h + 1) * P], probTs[h % 2][:, 4 + s],
                                             start=s == 0, stop=s == 1)
                        full(last, j)
                wait_out(pe, attn_job["O", AH - 1, 0])
                for i in range(8):
                    t = tile_of["mla_o"] + i // 2
                    if i % 2 == 0:
                        wait_tile(pe, t)
                    mm_wide(job_of["mla_o"] + i, t, P * (i % 2), P, lambda k: oT[:, k], DC, 256, i % 2 == 0)

            def stage_ffn2():
                rms2(1, [lambda k: rms_sq2[:, k, 0:T], lambda k: rms_sq2[:, k, T:T2]])
                pe.wait_ge(S("a2_ready"), 2)
                t0, j0 = tile_of["ffn2"], job_of["ffn2"]

                def body(it, i):
                    for half in range(2):
                        t = t0 + 2 * i + half
                        wait_tile(pe, t, it, 6)
                        for n in range(2):
                            j = j0 + 4 * i + 2 * half + n
                            wait_free(pe, j, it, 12)
                            for k in range(DC):
                                last = pe.matmul(bank(j), ring[:, t % RING, k * 256 + n * P:k * 256 + (n + 1) * P],
                                                 a2[:, k], start=k == 0, stop=k == DC - 1)
                                if n == 0 and k == 0:
                                    last.then_inc(tile_begun, 1)
                            full(last, j)
                repeat(pe, FSTEPS, 3, body)
                for i in range(12):
                    t, k0 = t0 + 22 + i, 4 * (i % 6)
                    wait_tile(pe, t)
                    if i == 0:
                        wait_out(pe, j0 + 4 * FSTEPS - 1)
                    if i == 6:
                        pe.wait_ge(S("ffn2_out"), 1)
                    kc = min(4, FC - k0)
                    for k in range(kc):
                        for n in range(4):
                            last = pe.matmul(psum[:, NB + n], ring[:, t % RING, k * 512 + n * P:k * 512 + (n + 1) * P],
                                             hid2[:, k0 + k], start=k0 + k == 0, stop=k0 + k == FC - 1)
                            if n == 0 and k == 0:
                                last.then_inc(tile_begun, 1)
                    if i % 6 == 5:
                        last.then_inc(S("ffn2_sum"), 1)

            def stage_hg():
                rms2(2, [lambda k: rms_sq[:, k, 0:T], lambda k: rms_sq[:, k, T:T2]])
                pe.wait_ge(S("a2_ready"), 3)
                for i in range(16):
                    t = tile_of["hg_z"] + i // 2
                    if i % 2 == 0:
                        wait_tile(pe, t)
                    mm_wide(job_of["hg_z"] + i, t, P * (i % 2), P, lambda k: a2[:, k], DC, 256, i % 2 == 0)
                for i in range(4):
                    mm_pair(tile_of["hg_q"] + i, job_of["hg_q"] + i, lambda k: a2[:, k, 0:T])
                for i in range(8):
                    t, j = tile_of["hg_i"] + i // 2, job_of["hg_i"] + i
                    if i % 2 == 0:
                        wait_tile(pe, t)
                    wait_free(pe, j)
                    for a in range(2):
                        tok = (2 * (i % 2) + a) * P
                        for k in range(DC):
                            last = pe.matmul(bank(j)[:, a * T:(a + 1) * T], a2[:, k, tok:tok + P],
                                             ring[:, t % RING, k * 256:(k + 1) * 256], start=k == 0, stop=k == DC - 1)
                            if i % 2 == 0 and a == 0 and k == 0:
                                last.then_inc(tile_begun, 1)
                    full(last, j)
                for i in range(4):
                    mm_pair(tile_of["hg_g"] + i, job_of["hg_g"] + i, lambda k: a2[:, k, 0:T])
                for i in range(8):
                    if i % 4 == 0:
                        pe.wait_ge(S("ctx_keys_ready"), i // 4 + 1)
                    turn(job_of["hg_wk"] + i, [kf[:, i // 4, 2 * (i % 4) + h, T + a * P:T + (a + 1) * P]
                                               for h in range(2) for a in range(2)])
                wait_out(pe, job_of["hg_wk"] + 7)
                for i in range(4):
                    j = job_of["hg_state"] + i
                    wait_free(pe, j)
                    for n in range(4):
                        m = 4 * i + n
                        for a in range(2):
                            last = pe.matmul(bank(j)[:, n * P:(n + 1) * P], wkT[:, 2 * m + a],
                                             itok[:, 2 + a, (m % AH) * P:(m % AH + 1) * P], start=a == 0, stop=a == 1)
                    full(last, j)
                for b in range(4):
                    pe.matmul(psum[:, NB + b, :], zeros[:], cst[:, 0:BANK], start=True, stop=False, skip_group_check=True)
                pe.wait_ge(S("q_decayed"), 1)
                wait_out(pe, job_of["hg_state"] + 3)

                def o_at(h, a=0, n=T):
                    return psum[:, NB + h // 2, (h % 2) * T + a:(h % 2) * T + a + n]

                for h in range(AH):
                    for d in range(2):
                        last = pe.matmul(o_at(h), state[:, d, h, T:T + P], ework[:, d, h], start=False, stop=False,
                                         skip_group_check=True)
                last.then_inc(S("q_decayed_used"), 1)

                def read_out(n):
                    lev, g = n // 4, n % 4
                    j = job_of["hg_level"] + n
                    wait_out(pe, j)
                    for i in range(4):
                        h, a = 2 * g + i // 2, i % 2
                        s = 1 - a if lev == 0 else a
                        last = pe.matmul(o_at(h, a * P, P), itok[:, s, h * P:(h + 1) * P], atts[n % 4][:, i],
                                         start=False, stop=lev == n_lev - 1, skip_group_check=True)
                    last.then_inc(S("att_used"), 1)

                n_lev = len(LEVELS) + 2
                for lev in range(n_lev):
                    pe.wait_ge(S("level_ready"), lev + 1)
                    for g in range(4):
                        n = 4 * lev + g
                        j = job_of["hg_level"] + n
                        wait_free(pe, j)
                        for i in range(4):
                            h, a = 2 * g + i // 2, i % 2
                            s = 1 - a if lev == 0 else a
                            eq = qh if lev == n_lev - 1 else eworks[lev % 2][:, 0]
                            ek = eworks[lev % 2][:, 1]
                            last = pe.matmul(bank(j)[:, i * P:(i + 1) * P], ek[:, h, s * P:(s + 1) * P],
                                             eq[:, h, a * P:(a + 1) * P], start=True, stop=True)
                        full(last, j)
                    if lev >= 1:
                        for g in range(4):
                            read_out(4 * (lev - 1) + g)
                for g in range(4):
                    read_out(4 * (n_lev - 1) + g)
                for i in range(4):
                    j = job_of["hg_norm"] + i
                    pe.wait_ge(S("o_sq_ready"), i + 1)
                    wait_free(pe, j)
                    for h in range(2):
                        last = pe.matmul(bank(j)[:, h * T:(h + 1) * T], ones, ework[:, 0, 2 * i + h], start=True, stop=True)
                    full(last, j)
                pe.wait_ge(S("hg_o_ready"), 1)
                for i in range(4):
                    mm_pair(tile_of["hg_o"] + i, job_of["hg_o"] + i, lambda k: ework[:, 1, k])

            def stage_ffn3():
                rms2(3, [lambda k: rms_sq3[:, k]])
                ffn("ffn3", FSTEPS, lambda: pe.wait_ge(S("ffn3_in_ready"), 1))

            def stage_out():
                pe.wait_ge(S("x_final"), 1)
                for g in range(4):
                    a = g // 2
                    turn(job_of["outT"] + g, [xT[:, 4 * (g % 2) + c, a * P:(a + 1) * P] for c in range(4)])

            stage_prep()
            stage_ada0()
            stage_mlstm()
            stage_ffn0()
            stage_s5()
            stage_moe()
            stage_mla()
            stage_ffn2()
            stage_hg()
            stage_ffn3()
            stage_out()

        @block.scalar
        def _(act):
            def root(j, dst, src, n, eps):
                wait_full(act, j)
                out_of(act.activation(dst, src, ACT.Sqrt, bias=eps[0:dst.shape[0]], scale=1.0 / n), j)

            def layer_norm(i):
                wait_out(act, job_of[f"ln{i}"])
                act.activation(sqr[:], res[:], ACT.Square).then_inc(S("ln_sq_ready"), 1)
                j = job_of[f"ln{i}"] + 1
                root(j, stat[:, 0], bank(j)[:, 0:T], D, ln_eps)

            def mod_rows_out(stage, s):
                act.wait_ge(tile_begun, tile_of[f"ada_{stage}"] + 2 * s + 2)
                act.activation(mod_rows, psum[:, 6, :], ACT.Copy).then_inc(S("mod_rows_out"), 1)

            def silu_steps(name, steps, between=None):
                sil = ffn_bufs[name][1]

                def body(it, i):
                    j = job_of[name] + 2 * i
                    wait_full(act, j, it, 4)
                    if it is not None or i >= 2:
                        wait_out(act, j - 3, it, 4)
                    out_of(act.activation(sil[:, i % 2].rearrange("p a t -> p (a t)"), bank(j), ACT.Silu), j)
                body(None, 0)
                body(None, 1)
                if between is not None:
                    between()
                after_two(act, steps, 2, body)

            def stage_prep():
                wait_out(act, job_of["params"] + 4)
                for i, name in enumerate(("c", "c_2", "c_ctx_2")):
                    last = act.activation(csil[:, :, i], col(name, 0, DC), ACT.Silu)
                last.then_inc(S("csil_ready"), 1)

            def stage_ada0():
                for i in range(6):
                    mod_rows_out("a", i)

            def stage_mlstm():
                for i in range(16):
                    j = job_of["m_in"] + i
                    wait_full(act, j)
                    src = bank(j).rearrange("p (a t) -> p a t", a=2)
                    if i < 8:
                        out_of(act.activation(xm[:, 2 * i:2 * i + 2, 4:4 + T], src, ACT.Copy), j)
                    else:
                        out_of(act.activation(zs[:, 2 * i - 16:2 * i - 14], src, ACT.Silu), j)
                for c in range(IC):
                    act.wait_ge(S("conv_sum_ready"), c + 1)
                    act.activation(xc[:, c], xc[:, c], ACT.Silu, bias=col("mlstm_conv_b", c)).then_inc(S("conv_ready"), 1)
                    if c >= 2:
                        j = job_of["m_qk"] + c - 2
                        wait_full(act, j)
                        out_of(act.activation(qk[:, c - 2], bank(j).rearrange("p (a t) -> p a t", a=2), ACT.Copy), j)
                    if c % 2 and c >= 3:
                        mod_rows_out("b", c // 2 - 1)
                for c in range(IC - 2, IC):
                    j = job_of["m_qk"] + c
                    wait_full(act, j)
                    out_of(act.activation(qk[:, c], bank(j).rearrange("p (a t) -> p a t", a=2), ACT.Copy), j)
                mod_rows_out("b", 7)
                for g in range(8):
                    j = job_of["m_vT"] + g
                    wait_full(act, j)
                    out_of(act.activation(vT[:, 2 * g:2 * g + 2], bank(j).rearrange("p (a t) -> p a t", a=2), ACT.Copy), j)
                wait_out(act, job_of["m_fsel"])
                act.activation(gate_rows[0:NH, 2], gate_rows[0:NH, 2], ACT.Exp)
                act.drain()
                act.wait_ge(S("eps_ready"), 1)
                act.activation(gate_rows[0:NH, 2], gate_rows[0:NH, 2], ACT.Ln, bias=one[0:NH, 0:1]).then_inc(S("ln_f_ready"), 1)
                for i in range(2):
                    mod_rows_out("b", 8 + i)
                act.wait_ge(S("m_sum_ready"), 1)
                act.activation(gate_rows[0:NH, 6], gate_rows[0:NH, 6], ACT.Exp, scale=-1.0).then_inc(S("gate_rows_ready"), 1)
                for h in range(NH):
                    for s in range(2):
                        act.wait_ge(S("decay_sum_ready"), 2 * h + s + 1)
                        act.activation(decay[:, s], decay[:, s], ACT.Exp, bias=cT[:, s, h:h + 1]).then_inc(S("decay_ready"), 1)
                    for i in range(2):
                        mod_rows_out("b", 10 + 2 * h + i)
                for h in range(NH):
                    wait_out(act, job_of["m_norm"] + 2 * h)
                    act.activation(vT[:, (h % 2) * HC:(h % 2 + 1) * HC], hT[:, h * HC:(h + 1) * HC], ACT.Square
                                   ).then_inc(S("h_sq_ready"), 1)
                    j = job_of["m_norm"] + 2 * h + 1
                    root(j, stat[:, h % 2], bank(j)[:, 0:T], DH, ln_eps)
                layer_norm(0)

            def s5_exponentials():
                act.wait_ge(S("s5_in"), 9 * 16)
                act.activation(sv[:, 0], sv[:, 0], ACT.Exp).then_inc(S("dt_ready"), 1)
                act.wait_ge(S("theta_ready"), 1)
                act.activation(sv[:, 3], sv[:, 3], ACT.Exp)
                for i in (5, 6):
                    last = act.activation(sv[:, i], sv[:, i], ACT.Sin)
                last.then_inc(S("sin_ready"), 1)

            def stage_ffn0():
                act.wait_ge(S("ffn0_in_ready"), 1)
                act.dma_start(router_w[:], w["moe_router"][0].rearrange("(c p) e -> p c e", p=P)).then_inc(S("s5_in"), 16)
                for i, name in enumerate(("s5_b_re", "s5_b_im")):
                    act.dma_start(bmat[:, i], w[name][0].rearrange("(j g) p h -> (g p) j h", g=2)).then_inc(S("s5_in"), 16)
                for i, name in enumerate(("s5_c_re", "s5_c_im")):
                    for d in range(2):
                        act.dma_start(ctok[:, i, :, d], w[name][0].rearrange("(c g) h p -> (g h) c p", g=8)
                                     ).then_inc(S("s5_in"), 16)
                log_dt = w["s5_log_dt"].rearrange("o (j g) -> g (o j)", g=2)
                for g in range(2):
                    act.dma_start(sv[g * SP_:(g + 1) * SP_, 0], log_dt[g:g + 1].broadcast_to([SP_, NPAIR]),
                                 allow_slow_non_contiguous=True
                                 ).then_inc(S("s5_in"), 16)
                silu_steps("ffn0", FSTEPS, s5_exponentials)
                layer_norm(1)

            def stage_s5():
                for c in range(DC):
                    for i in range(3):
                        mod_rows_out("c", 3 * c + i)
                    act.wait_ge(S("s5_y_out"), c + 1)
                    act.activation(gT[:, c], gT[:, c], ACT.Gelu_apprx_tanh).then_inc(S("gelu_ready"), 1)
                for i in range(4):
                    j = job_of["glu"] + 2 * i + 1
                    wait_full(act, j)
                    if i >= 2:
                        wait_out(act, job_of["glu"] + 2 * (i - 2))
                    for n in range(2):
                        last = act.activation(sil[:, i % 2, n], bank(j)[:, n * T:(n + 1) * T], ACT.Sigmoid,
                                              bias=col("s5_b_glu", DC + 2 * i + n))
                    out_of(last, j)
                layer_norm(2)

            def stage_moe():
                act.wait_ge(S("logits_ready"), 1)
                act.activation(lg[:, 1], lg[:, 1], ACT.Exp).then_inc(S("exp_logits_ready"), 1)
                for g in range(4):
                    j = job_of["u_tok"] + g
                    wait_full(act, j)
                    out_of(act.activation(u_tok[:, g // 2, (g % 2) * BANK:(g % 2 + 1) * BANK], bank(j), ACT.Copy), j)
                act.wait_ge(S("slots_ready"), 1)
                for g in range(4):
                    j = job_of["scatterT"] + g
                    wait_full(act, j)
                    out_of(act.activation(scatterT[:, 2 * g:2 * g + 2], bank(j).rearrange("p (e t) -> p e t", e=2),
                                          ACT.Copy), j)
                for g in range(16):
                    j = job_of["gather"] + g
                    wait_full(act, j)
                    out_of(act.activation(xe[:, g // 2, (g % 2) * BANK:(g % 2 + 1) * BANK], bank(j), ACT.Copy), j)

                def experts(gathered):
                    n_cols = SLOTS if gathered else T

                    def outputs(e, it):
                        act.wait_ge(S("hidden_free"), val(2 + FSTEPS * (e + 1), it, PAIR_STEPS))
                        act.activation(ye[:, 0:BANK], psum[:, NB, :], ACT.Copy)
                        act.activation(ye[:, BANK:D], psum[:, NB + 1, :], ACT.Copy).then_inc(S("ye_ready"), 1)

                    with act.Fori(0, NE // 2) as it:
                        for u in range(PAIR_STEPS):
                            j = job_of["moe"] + 2 * u
                            wait_full(act, j, it, 2 * PAIR_STEPS)
                            wait_out(act, j - 3, it, 2 * PAIR_STEPS)
                            out_of(act.activation(sil[:, u % 2, :, 0:n_cols],
                                                  bank(j)[:, 0:2 * n_cols].rearrange("p (a t) -> p a t", a=2),
                                                  ACT.Silu), j)
                            if gathered and u in (FSTEPS, PAIR_STEPS - 1):
                                outputs(u // FSTEPS if u > FSTEPS else 0, it)

                is_crowded = act.value_load(crowded[0:1, 0:1], min_val=0, max_val=1)
                with act.If(is_crowded != 0):
                    experts(False)
                with act.Else():
                    experts(True)
                layer_norm(3)

            def rms2(i, dst):
                act.wait_ge(S("x2_ready"), i + 1)
                for n in range(len(dst)):
                    last = act.activation(dst[n], halves[n][:], ACT.Square)
                last.then_inc(S("rms_sq_ready"), 1)
                j, n = job_of[f"rms{i}"], T * len(dst)
                root(j, rstd2[:, 0:n], bank(j)[:, 0:n], D, rms_eps)

            def stage_mla():
                rms2(0, [rms_sq[:, :, 0:T], rms_sq[:, :, T:T2]])

                def item_root(m):
                    n, rows = item_of(m)[2:4]
                    j = mla_job["S", m, 0]
                    if m >= 2:
                        act.wait_ge(S("item_normed"), m - 1)
                    root(j, nstat[0:rows, m % 2], bank(j)[0:rows], rows * n, rms_eps)

                last_use = {}
                for kind, m, c in MLA_SEQ:
                    j = mla_job[kind, m, c]
                    if kind == "V":
                        wait_full(act, j)
                        out_of(act.activation(vtok[:, c, 512 * m:512 * m + 512], bank(j), ACT.Copy), j)
                    elif kind == "P":
                        name, h, n, rows, dst, weight, slots = item_of(m)
                        wait_full(act, j)
                        if slots[c] in last_use:
                            wait_full(act, mla_job["S", last_use[slots[c]], 0])
                        last_use[slots[c]] = m
                        at = c if n > 1 else h
                        act.activation(dst[0:rows, at], bank(j)[0:rows], ACT.Copy)
                        out_of(act.activation(nsq[0:rows, slots[c]], bank(j)[0:rows], ACT.Square), j)
                        if c == n - 1:
                            act.drain().then_inc(S("nsq_ready"), 1)
                    else:
                        item_root(m)
                for kind, h, k in ATTN_SEQ:
                    j = attn_job[kind, h, k]
                    wait_full(act, j)
                    if kind == "S":
                        act.wait_ge(S("max_ready"), 3 * h + k + 1)
                        for a in range(1 if k < 2 else 2):
                            n = T2 if k < 2 else T
                            last = act.activation(prob[:, h % 2, k, a * n:(a + 1) * n], bank(j)[:, a * n:(a + 1) * n],
                                                  ACT.Exp, bias=smax[:, h % 2, 2 * k + a:2 * k + a + 1], scale=ATT_SCALE)
                        out_of(last, j)
                    elif kind == "T":
                        src = bank(j).rearrange("p (s t) -> p s t", t=P)
                        if k < 2:
                            out_of(act.activation(probTs[h % 2][:, 0:4, k * P:(k + 1) * P], src, ACT.Copy), j)
                        else:
                            out_of(act.activation(probTs[h % 2][:, 4:6].rearrange("p s (a t) -> p a s t", a=2),
                                                  bank(j).rearrange("p (a s t) -> p a s t", a=2, s=2), ACT.Copy), j)
                    else:
                        out_of(act.activation(oT[:, h], bank(j), ACT.Copy), j)

            def stage_ffn2():
                rms2(1, [rms_sq2[:, :, 0:T], rms_sq2[:, :, T:T2]])
                j0 = job_of["ffn2"]

                def body(it, i):
                    for n in range(2):
                        j = j0 + 4 * i + n
                        wait_full(act, j, it, 12)
                        if it is not None or i >= 1:
                            wait_out(act, j - 2, it, 12)
                        out_of(act.activation(sil2[:, n], bank(j), ACT.Silu), j)
                for i in range(3):
                    body(None, i)
                whole = (FSTEPS - 3) // 3
                with act.Fori(0, whole) as it:
                    for i in range(3):
                        body(it, 3 + i)
                for i in range(3 + 3 * whole, FSTEPS):
                    body(None, i)

            def stage_hg():
                rms2(2, [rms_sq[:, :, 0:T], rms_sq[:, :, T:T2]])
                act.wait_ge(S("lb_logits_ready"), 1)
                act.activation(lbs[:, 0], lbs[:, 0], ACT.Sigmoid).then_inc(S("lb_ready"), 1)
                def log_forget(d):
                    act.wait_ge(S("forget_ready"), d + 1)
                    act.activation(lf[:, d], lf[:, d], ACT.Ln).then_inc(S("log_forget_ready"), 1)

                for i in range(16):
                    j = job_of["hg_z"] + i
                    d, h = i // AH, i % AH
                    wait_full(act, j)
                    act.activation(lf[:, d, h], bank(j), ACT.Sigmoid)
                    out_of(act.activation(kf[:, d, h], bank(j), ACT.Sigmoid, scale=-1.0), j)
                    if i == AH + 3:
                        log_forget(0)
                for i in range(4):
                    j = job_of["hg_q"] + i
                    wait_full(act, j)
                    out_of(act.activation(qh[:, 2 * i:2 * i + 2], bank(j).rearrange("p (a t) -> p a t", a=2), ACT.Copy), j)
                log_forget(1)
                for i in range(8):
                    j = job_of["hg_i"] + i
                    wait_full(act, j)
                    a = 2 * (i % 2)
                    out_of(act.activation(itok[:, a:a + 2, 256 * (i // 2):256 * (i // 2 + 1)],
                                          bank(j).rearrange("p (a t) -> p a t", a=2), ACT.Copy), j)
                for d in range(2):
                    act.wait_ge(S("ctx_decay_ready"), d + 1)
                    act.activation(lf[:, d, :, T:T2], lf[:, d, :, T:T2], ACT.Exp).then_inc(S("ctx_decay_exp"), 1)
                for i in range(4):
                    j = job_of["hg_g"] + i
                    wait_full(act, j)
                    out_of(act.activation(gsil[:, 2 * i:2 * i + 2], bank(j).rearrange("p (a t) -> p a t", a=2), ACT.Silu), j)
                act.wait_ge(S("lat_sums_ready"), 1)
                act.activation(ework[:], lf[:, :, :, 0:T], ACT.Exp).then_inc(S("q_decay_exp"), 1)
                for lev in range(len(LEVELS) + 1):
                    act.wait_ge(S("level_exponents"), lev + 1)
                    e = eworks[lev % 2]
                    act.activation(e[:], e[:], ACT.Exp).then_inc(S("level_exp"), 1)
                for i in range(4):
                    act.wait_ge(S("att_used"), 4 * (len(LEVELS) + 2))
                    act.activation(ework[:, 0, 2 * i:2 * i + 2], psum[:, NB + i].rearrange("p (h t) -> p h t", h=2), ACT.Square
                                   ).then_inc(S("o_sq_ready"), 1)
                for i in range(4):
                    j = job_of["hg_norm"] + i
                    root(j, hstat[:, 2 * i:2 * i + 2].rearrange("p h t -> p (h t)"), bank(j), P, rms_eps)

            def stage_ffn3():
                rms2(3, [rms_sq3])
                silu_steps("ffn3", FSTEPS)

            stage_prep()
            stage_ada0()
            stage_mlstm()
            stage_ffn0()
            stage_s5()
            stage_moe()
            stage_mla()
            stage_ffn2()
            stage_hg()
            stage_ffn3()

        @block.vector
        def _(dve):
            def modulate(m, shift, signal):
                for c in range(DC):
                    last = dve.tensor_scalar(act_in[:, c], xT[:, c], mod1[:, m, shift + DC + c, 0:1],
                                             mod[:, m, shift + c, 0:1], ALU.mult, ALU.add)
                last.then_inc(S(signal), 1)

            def ada(count, l, c0, c1, at, n):
                dve.wait_ge(S("mods_full"), count)
                bias = col(f"ada_b{l}", c0, c1 - c0)[:, :, None].broadcast_to([P, c1 - c0, n])
                src = psum[:, 7, at:at + (c1 - c0) * n].rearrange("p (c n) -> p c n", n=n)
                dve.tensor_tensor(mod[:, l, c0:c1, 0:n], src, bias, ALU.add)
                dve.drain()
                dve.tensor_scalar(mod1[:, l, c0:c1, 0:n], mod[:, l, c0:c1, 0:n], 1.0, None, ALU.add)
                dve.drain()

            def layer_norm(i, l, which):
                j = job_of[f"ln{i}"]
                wait_full(dve, j)
                mean = bank(j)[:, None, 0:T].broadcast_to([P, DC, T])
                out_of(dve.scalar_tensor_tensor(res[:], mean, -1.0 / D, res[:], ALU.mult, ALU.add), j)
                wait_out(dve, j + 1)
                dve.reciprocal(stat[:, 0], stat[:, 0])
                dve.drain()
                dve.tensor_tensor(res[:], res[:], stat[:, 0:1].broadcast_to([P, DC, T]), ALU.mult)
                dve.drain()
                for c in range(DC):
                    dve.tensor_scalar(xT[:, c], res[:, c], col(f"ln_{which}_g{l}", c), col(f"ln_{which}_b{l}", c),
                                      ALU.mult, ALU.add)
                dve.drain()

            def residual(c, src, gate):
                dve.tensor_scalar(res[:, c], src, gate, None, ALU.mult)

            def hidden_steps(name, steps, between=None):
                hid, sil = ffn_bufs[name]

                def body(it, i):
                    j = job_of[name] + 2 * i + 1
                    wait_out(dve, j - 1, it, 4)
                    wait_full(dve, j, it, 4)
                    if it is not None or i >= 2:
                        dve.wait_ge(S(f"{name}_down"), val(i - 1, it, 2))
                    up = bank(j).rearrange("p (a t) -> p a t", a=2)
                    out_of(dve.tensor_tensor(hid[:, i % 2], sil[:, i % 2], up, ALU.mult), j)
                body(None, 0)
                body(None, 1)
                if between is not None:
                    between()
                after_two(dve, steps, 2, body)
                dve.wait_ge(S(f"{name}_down"), steps)

            def ffn_residual(m):
                for c in range(DC):
                    dve.tensor_scalar(res[:, c], psum[:, NB + c // 2, (c % 2) * T:(c % 2 + 1) * T],
                                      mod1[:, m, 40 + c, 0:1], None, ALU.mult)
                dve.drain()
                dve.scalar_tensor_tensor(res[:], xT[:], ALPHA, res[:], ALU.mult, ALU.add).then_inc(S("ln_sum_ready"), 1)

            def stage_prep():
                dve.memset(prow[:], 0.0).then_inc(S("prow_zero"), 1)
                dve.memset(xm[:, :, 0:4], 0.0)
                dve.memset(zeros[:], 0.0)
                for i, x in enumerate((1.0, LN_EPS, RMS_EPS)):
                    last = dve.memset(one[:, i:i + 1], x)
                last.then_inc(S("eps_ready"), 1)
                for g in range(5):
                    j = job_of["params"] + g
                    wait_full(dve, j)
                    out_of(dve.tensor_copy(par[:, g * P:(g + 1) * P], bank(j)[:, 0:P]), j)
                for g in range(4):
                    j = job_of["xT"] + g
                    wait_full(dve, j)
                    out_of(dve.tensor_copy(xT[:, 2 * g:2 * g + 2], bank(j).rearrange("p (a t) -> p a t", a=2)), j)
                dve.wait_ge(S("mlstm_small_in"), 64)
                mask = c_("block4")[:, :, None].broadcast_to([P, 32, 4])
                for i in range(3):
                    for c in range(IC):
                        last = dve.tensor_tensor(bd[:, i, c].rearrange("p (n o) -> p n o", o=4),
                                                 qkv_small[:, i, c:c + 1].broadcast_to([P, 32, 4]), mask, ALU.mult)
                    last.then_inc(S("block_diag_ready"), 1)

            def stage_ada0():
                ada(1, 0, 0, 24, 0, 1)

            def stage_mlstm():
                modulate(0, 0, "mlstm_in_ready")
                for c in range(IC):
                    wait_out(dve, job_of["m_in"] + c // 2)
                    dve.tensor_scalar(xc[:, c], xm[:, c, 1:1 + T], col("conv_w", c), None, ALU.mult)
                    for k in range(1, CONV):
                        dve.drain()
                        last = dve.scalar_tensor_tensor(xc[:, c], xm[:, c, 1 + k:1 + k + T], col("conv_w", k * IC + c),
                                                        xc[:, c], ALU.mult, ALU.add)
                    last.then_inc(S("conv_sum_ready"), 1)
                j = job_of["m_gates"]
                wait_full(dve, j)
                g = gate_rows
                out_of(dve.tensor_scalar(g[0:8, 0], bank(j)[0:8, 0:T], col("b_gates")[0:8], None, ALU.add), j)
                j = job_of["m_fsel"]
                wait_full(dve, j)
                f = bank(j)[0:NH, 0:T]
                dve.tensor_scalar(g[0:NH, 1], f, 0.0, None, ALU.min)
                dve.drain()
                out_of(dve.scalar_tensor_tensor(g[0:NH, 2], g[0:NH, 1], 2.0, f, ALU.mult, ALU.subtract), j)
                dve.memset(g[0:NH, 7], 1.0)
                dve.wait_ge(S("ln_f_ready"), 1)
                dve.tensor_tensor(g[0:NH, 1], g[0:NH, 1], g[0:NH, 2], ALU.subtract)
                dve.drain()
                dve.tensor_tensor_scan(g[0:NH, 3], g[0:NH, 7], g[0:NH, 1], 0.0, ALU.mult, ALU.add)
                dve.drain()
                dve.tensor_tensor(g[0:NH, 4], g[0:NH, 0], g[0:NH, 3], ALU.subtract)
                dve.drain()
                dve.tensor_tensor_scan(g[0:NH, 5], g[0:NH, 4], g[0:NH, 4], 0.0, ALU.max, ALU.max)
                dve.drain()
                dve.tensor_tensor(g[0:NH, 6], g[0:NH, 3], g[0:NH, 5], ALU.add)
                dve.tensor_scalar(g[0:NH, 5], g[0:NH, 5], -1.0, None, ALU.mult).then_inc(S("m_sum_ready"), 1)
                j = job_of["m_cT"]
                wait_full(dve, j)
                out_of(dve.tensor_copy(cT, bank(j)[:, 0:2 * NH].rearrange("p (s h) -> p s h", s=2)), j)
                wait_out(dve, job_of["m_qk"] + IC - 1)
                for h in range(NH):
                    j = job_of["m_rows"] + h
                    wait_full(dve, j)
                    out_of(dve.tensor_copy(nm[:, h], bank(j).rearrange("p (k t) -> p k t", k=2)), j)
                for g in range(8):
                    a, c0 = g // 4, 4 * (g % 4)
                    j = job_of["m_v"] + g
                    wait_full(dve, j)
                    out_of(dve.tensor_copy(vbuf[:, a, c0 * P:(c0 + 4) * P], bank(j)), j)
                causal = c_("causal").rearrange("p (s t) -> p s t", s=2)
                for h in range(NH):
                    for s in range(2):
                        dve.tensor_tensor(decay[:, s], nm[:, h, 0], causal[:, s], ALU.add).then_inc(S("decay_sum_ready"), 1)
                    j = job_of["m_head"] + 4 * h
                    dve.wait_ge(S("decay_ready"), 2 * h + 2)
                    wait_full(dve, j)
                    out_of(dve.scalar_tensor_tensor(scor[:, h % 2], bank(j).rearrange("p (s t) -> p s t", s=2), DH ** -0.5,
                                                  decay[:], ALU.mult, ALU.mult), j)
                    wait_full(dve, j + 1)
                    dve.tensor_tensor(recip_[:, 0], bank(j + 1)[:, 0:T], nm[:, h, 1], ALU.max)
                    dve.drain()
                    out_of(dve.scalar_tensor_tensor(recip_[:, 0], bank(j + 1)[:, 0:T], -1.0, recip_[:, 0],
                                                    ALU.mult, ALU.max), j + 1)
                    dve.drain()
                    dve.reciprocal(recip_[:, 1], recip_[:, 0])
                    dve.drain()
                    for g in range(2):
                        wait_full(dve, j + 2 + g)
                        out_of(dve.tensor_tensor(hT[:, h * HC + 2 * g:h * HC + 2 * g + 2],
                                               bank(j + 2 + g).rearrange("p (a t) -> p a t", a=2),
                                               recip_[:, 1:2].broadcast_to([P, 2, T]), ALU.mult), j + 2 + g)
                ada(2, 0, 24, 48, 24, 1)
                ada(2, 1, 0, 48, 48, 1)
                for h in range(NH):
                    j = job_of["m_norm"] + 2 * h
                    wait_full(dve, j)
                    hh = hT[:, h * HC:(h + 1) * HC]
                    out_of(dve.scalar_tensor_tensor(hh, bank(j)[:, None, 0:T].broadcast_to([P, HC, T]), -1.0 / DH, hh,
                                                  ALU.mult, ALU.add), j)
                    wait_out(dve, j + 1)
                    dve.reciprocal(stat[:, h % 2], stat[:, h % 2])
                    dve.drain()
                    dve.tensor_tensor(hh, hh, stat[:, h % 2:h % 2 + 1].broadcast_to([P, HC, T]), ALU.mult)
                    dve.drain()
                    for c in range(h * HC, (h + 1) * HC):
                        dve.tensor_scalar(xc[:, c], xc[:, c], col("mlstm_skip", c), None, ALU.mult)
                    dve.drain()
                    for c in range(h * HC, (h + 1) * HC):
                        dve.scalar_tensor_tensor(hT[:, c], hT[:, c], col("mlstm_norm_w", c), xc[:, c], ALU.mult, ALU.add)
                    dve.drain()
                    last = dve.tensor_tensor(hh, hh, zs[:, h * HC:(h + 1) * HC], ALU.mult)
                last.then_inc(S("h_out_ready"), 1)
                for g in range(4):
                    j = job_of["m_out"] + g
                    wait_full(dve, j)
                    for n in range(2):
                        last = dve.tensor_scalar(res[:, 2 * g + n], bank(j)[:, n * T:(n + 1) * T],
                                                 mod1[:, 0, 16 + 2 * g + n, 0:1], None, ALU.mult)
                    out_of(last, j)
                dve.drain()
                dve.scalar_tensor_tensor(res[:], xT[:], ALPHA, res[:], ALU.mult, ALU.add).then_inc(S("ln_sum_ready"), 1)
                layer_norm(0, 0, "mix")

            def s5_parameters():
                dt, th, lam, mag, kk, sn, hs, den, ar, ai, kr, ki, cs, t1 = (sv[:, i] for i in range(14))
                lr, li = col("lam_re", 0, NPAIR), col("lam_im", 0, NPAIR)

                def step(*a):
                    dve.tensor_tensor(*a)
                    dve.drain()

                def step_s(*a):
                    dve.tensor_scalar(*a)
                    dve.drain()

                dve.wait_ge(S("dt_ready"), 1)
                step(mag, lr, dt, ALU.mult)
                step(th, li, dt, ALU.mult)
                magic = 1.5 * 2 ** 23
                step_s(kk, th, 1 / (2 * np.pi), magic, ALU.mult, ALU.add)
                step_s(kk, kk, magic, None, ALU.subtract)
                c1 = 6.28125
                c2 = float(np.float32(round((2 * np.pi - c1) * 2 ** 21) / 2 ** 21))
                c3 = 2 * np.pi - c1 - c2
                for c in (c1, c2, c3):
                    dve.scalar_tensor_tensor(th, kk, -c, th, ALU.mult, ALU.add)
                    dve.drain()
                pi = float(np.nextafter(np.float32(np.pi), np.float32(0)))
                step_s(sn, th, pi, -pi, ALU.min, ALU.max)
                dve.tensor_scalar(hs, sn, 0.5, None, ALU.mult).then_inc(S("theta_ready"), 1)
                dve.wait_ge(S("sin_ready"), 1)
                step(cs, hs, hs, ALU.mult)
                step_s(cs, cs, -2.0, 1.0, ALU.mult, ALU.add)
                step(ar, mag, cs, ALU.mult)
                step(ai, mag, sn, ALU.mult)
                step(den, lr, lr, ALU.mult)
                step(t1, li, li, ALU.mult)
                step(den, den, t1, ALU.add)
                dve.reciprocal(den, den)
                step_s(ar, ar, -1.0, None, ALU.add)
                step(kr, ar, lr, ALU.mult)
                step(t1, ai, li, ALU.mult)
                step(kr, kr, t1, ALU.add)
                step(kr, kr, den, ALU.mult)
                step(ki, ai, lr, ALU.mult)
                step(t1, ar, li, ALU.mult)
                step(ki, ki, t1, ALU.subtract)
                step(ki, ki, den, ALU.mult)
                dve.nop().then_inc(S("s5_params_ready"), 1)

            def stage_ffn0():
                modulate(0, 24, "ffn0_in_ready")
                hidden_steps("ffn0", FSTEPS, s5_parameters)
                ffn_residual(0)
                layer_norm(1, 0, "ffn")

            def stage_s5():
                modulate(1, 0, "s5_u_ready")
                for g in range(4):
                    j = job_of["s_bT"] + g
                    wait_full(dve, j)
                    out_of(dve.tensor_copy(bT[:, g // 2, 4 * (g % 2):4 * (g % 2) + 4],
                                           bank(j).rearrange("p (c s) -> p c s", s=P)), j)
                parity = c_("parity")[:, None, :].broadcast_to([P, 4, P])
                for g in range(4):
                    j = job_of["s_cT"] + g
                    wait_full(dve, j)
                    out_of(dve.scalar_tensor_tensor(cmT[:, g // 2, 4 * (g % 2):4 * (g % 2) + 4],
                                                    bank(j).rearrange("p (c s) -> p c s", s=P), -1.0 if g // 2 else 1.0,
                                                    parity, ALU.mult, ALU.mult), j)

                def pair(c, i):
                    p = 4 * c + i
                    j = job_of["s_pair"] + i
                    dve.drain()
                    dve.wait_ge(bank_full[j % NB], c + (j // NB + 1))
                    cos2, sin2 = (rot[:, k, bass.ds(p, 1), :].broadcast_to([P, 2, SL]) for k in range(2))
                    b = [bank(j)[:, k * T:(k + 1) * T].rearrange("p (b t) -> p b t", b=2) for k in range(2)]
                    zri = zris[i % 2]
                    z = [zri[:, k].rearrange("p (b t) -> p b t", b=2) for k in range(2)]
                    zt = [ztmp[:, k].rearrange("p (b t) -> p b t", b=2) for k in range(2)]
                    if not (isinstance(c, int) and i < 2):
                        dve.wait_ge(S("s5_x_ready"), p - 1)
                    dve.tensor_tensor(z[0], b[0], cos2, ALU.mult)
                    dve.tensor_tensor(zt[0], b[1], sin2, ALU.mult)
                    dve.tensor_tensor(z[1], b[1], cos2, ALU.mult)
                    out_of(dve.tensor_tensor(zt[1], b[0], sin2, ALU.mult), j)
                    dve.drain()
                    dve.tensor_tensor(z[0], z[0], zt[0], ALU.add)
                    dve.tensor_tensor(z[1], z[1], zt[1], ALU.subtract)
                    dve.drain()
                    mag_t = sv[:, 3, bass.ds(p, 1)].broadcast_to([P, SL])
                    ends = zri[:, :, SL - 1]
                    rot_end = [rot[:, k, bass.ds(p, 1), SL - 1].broadcast_to([P, 2]) for k in range(2)]
                    for blk in range(2):
                        at = slice(blk * SL, (blk + 1) * SL)
                        for k in range(2):
                            last = dve.tensor_tensor_scan(zri[:, k, at], mag_t, zri[:, k, at],
                                                          carry[:, 2, k:k + 1] if blk else 0.0, ALU.mult, ALU.add)
                        if blk == 0:
                            dve.drain()
                            dve.tensor_tensor(carry[:, 0], ends, rot_end[0], ALU.mult)
                            dve.tensor_tensor(carry[:, 1], ends, rot_end[1], ALU.mult)
                            dve.drain()
                            dve.tensor_tensor(carry[:, 2, 0:1], carry[:, 0, 0:1], carry[:, 1, 1:2], ALU.subtract)
                            dve.tensor_tensor(carry[:, 2, 1:2], carry[:, 0, 1:2], carry[:, 1, 0:1], ALU.add)
                            dve.drain()
                    last.then_inc(S("s5_z_ready"), 1)

                def y_out(c, back):
                    c = c + back
                    dve.wait_ge(S("s5_x_used"), 4 * c + 4)
                    dve.scalar_tensor_tensor(gT[:, bass.ds(c, 1), :], act_in[:, bass.ds(c, 1), :],
                                             par[:, bass.ds(prow_at["s5_d"] + c, 1)],
                                             psum[:, bass.ds(NB + c % 2, 1), 0:T], ALU.mult, ALU.add
                                             ).then_inc(S("s5_y_out"), 1)

                dve.wait_ge(S("rot_ready"), 1)
                for i in range(4):
                    pair(0, i)
                with dve.Fori(1, DC) as c:
                    for i in range(4):
                        pair(c, i)
                        if i == 2:
                            y_out(c, -1)
                y_out(DC, -1)
                for l in range(2):
                    ada(3, l + 2, 0, 48, 96 * l, 2)
                for i in range(4):
                    j = job_of["glu"] + 2 * i
                    wait_out(dve, j + 1)
                    wait_full(dve, j)
                    for n in range(2):
                        last = dve.scalar_tensor_tensor(res[:, 2 * i + n], bank(j)[:, n * T:(n + 1) * T],
                                                        col("s5_b_glu", 2 * i + n), sil[:, i % 2, n], ALU.add, ALU.mult)
                    out_of(last, j)
                    dve.drain()
                    for n in range(2):
                        dve.tensor_scalar(res[:, 2 * i + n], res[:, 2 * i + n], mod1[:, 1, 16 + 2 * i + n, 0:1], None,
                                          ALU.mult)
                dve.drain()
                dve.scalar_tensor_tensor(res[:], xT[:], ALPHA, res[:], ALU.mult, ALU.add).then_inc(S("ln_sum_ready"), 1)
                layer_norm(2, 1, "mix")

            def stage_moe():
                modulate(1, 24, "moe_in_ready")
                j = job_of["router"]
                wait_full(dve, j)
                logit, ex, m1, rank, tot, wt = (lg[:, i] for i in (0, 1, 2, 3, 4, 6))
                out_of(dve.tensor_copy(logit, bank(j)[:, 0:2 * NE].rearrange("p (a e) -> p a e", a=2)), j)
                dve.drain()
                dve.tensor_reduce(m1[:, :, 0:1], logit, AX.X, ALU.max)
                dve.drain()
                dve.tensor_tensor(ex, logit, m1[:, :, 0:1].broadcast_to([P, 2, NE]), ALU.subtract
                                  ).then_inc(S("logits_ready"), 1)
                lj = logit[:, :, None, :].broadcast_to([P, 2, NE, NE])
                le = logit[:, :, :, None].broadcast_to([P, 2, NE, NE])
                before = c_("before").rearrange("p (e j) -> p e j", e=NE)[:, None].broadcast_to([P, 2, NE, NE])
                dve.tensor_tensor(cmp_[:, 0], lj, le, ALU.is_gt)
                dve.tensor_tensor(cmp_[:, 1], lj, le, ALU.is_equal)
                dve.drain()
                dve.tensor_tensor(cmp_[:, 1], cmp_[:, 1], before, ALU.mult)
                dve.drain()
                dve.tensor_tensor(cmp_[:, 0], cmp_[:, 0], cmp_[:, 1], ALU.add)
                dve.drain()
                dve.tensor_reduce(rank[:, :, :, None], cmp_[:, 0], AX.X, ALU.add)
                dve.drain()
                dve.tensor_scalar(rank, rank, 1.5, None, ALU.is_lt)
                dve.wait_ge(S("exp_logits_ready"), 1)
                dve.drain()
                dve.tensor_tensor(ex, ex, rank, ALU.mult)
                dve.drain()
                dve.tensor_reduce(tot[:, :, 0:1], ex, AX.X, ALU.add)
                dve.drain()
                dve.reciprocal(tot[:, :, 0:1], tot[:, :, 0:1])
                dve.drain()
                dve.tensor_tensor(wt, ex, tot[:, :, 0:1].broadcast_to([P, 2, NE]), ALU.mult
                                  ).then_inc(S("top2_ready"), 1)
                j = job_of["places"]
                dve.wait_ge(S("order_in"), 16)
                wait_full(dve, j)
                dve.tensor_copy(place[:], bank(j)[:, 0:2 * NE].rearrange("p (a e) -> p a e", a=2))
                out_of(dve.tensor_reduce(crowd[:, 0:1], bank(j)[:, 2 * NE:3 * NE], AX.X, ALU.max), j)
                dve.drain()
                dve.tensor_scalar(crowded[:], crowd[:, 0:1], SLOTS + 0.5, None, ALU.is_gt)
                for a in range(2):
                    for e in range(NE):
                        dve.tensor_scalar(gather[:, a, e], slots, place[:, a, e:e + 1], rank[:, a, e:e + 1],
                                          ALU.is_equal, ALU.mult)
                        dve.tensor_scalar(wgather[:, a, e], slots, place[:, a, e:e + 1], wt[:, a, e:e + 1],
                                          ALU.is_equal, ALU.mult)
                dve.drain().then_inc(S("slots_ready"), 1)
                j = job_of["gateT"]
                wait_full(dve, j)
                out_of(dve.tensor_copy(gate8[0:NE], bank(j)[0:NE, 0:T]), j)
                for g in range(4):
                    j = job_of["gates"] + g
                    wait_full(dve, j)
                    out_of(dve.tensor_copy(gate_bc[:, 2 * g:2 * g + 2], bank(j).rearrange("p (e t) -> p e t", e=2)), j)
                dve.drain()

                def experts(gathered):
                    n_cols = SLOTS if gathered else T
                    if gathered:
                        dve.memset(res[:], 0.0)
                        for i in range(2):
                            dve.drain().then_inc(S("scatter_free"), 1)

                    def add(e, it):
                        dve.drain()
                        for g in range(4):
                            dve.wait_ge(S("scatter_full"), val(4 * e + g + 1, it, 8))
                            dve.tensor_tensor(res[:, 2 * g:2 * g + 2], res[:, 2 * g:2 * g + 2],
                                              psum[:, NB + 2 + g % 2].rearrange("p (a t) -> p a t", a=2), ALU.add
                                              ).then_inc(S("scatter_free"), 1)

                    with dve.Fori(0, NE // 2) as it:
                        for u in range(PAIR_STEPS):
                            j = job_of["moe"] + 2 * u + 1
                            wait_out(dve, j - 1, it, 2 * PAIR_STEPS)
                            silu = sil[:, u % 2, :, 0:n_cols]
                            if not gathered:
                                weight = gate_bc[:, bass.ds(it * 2 + u // FSTEPS, 1), :].broadcast_to([P, 2, T])
                                dve.tensor_tensor(silu, silu, weight, ALU.mult)
                                dve.drain()
                            wait_full(dve, j, it, 2 * PAIR_STEPS)
                            dve.wait_ge(S("hidden_free"), val(u + 1, it, PAIR_STEPS))
                            up = bank(j)[:, 0:2 * n_cols].rearrange("p (a t) -> p a t", a=2)
                            out_of(dve.tensor_tensor(hid[:, u % 2, :, 0:n_cols], silu, up, ALU.mult), j)
                            if gathered and u in (FSTEPS, PAIR_STEPS - 1):
                                add(u // FSTEPS if u > FSTEPS else 0, it)
                    if gathered:
                        dve.drain()
                        for c in range(DC):
                            dve.tensor_scalar(res[:, c], res[:, c], mod1[:, 1, 40 + c, 0:1], None, ALU.mult)
                        dve.drain()
                        dve.scalar_tensor_tensor(res[:], xT[:], ALPHA, res[:], ALU.mult, ALU.add
                                                 ).then_inc(S("ln_sum_ready"), 1)
                    else:
                        dve.wait_ge(S("hidden_free"), 2 + FSTEPS * NE)
                        ffn_residual(1)

                is_crowded = dve.value_load(crowded[0:1, 0:1], min_val=0, max_val=1)
                with dve.If(is_crowded != 0):
                    experts(False)
                with dve.Else():
                    experts(True)
                layer_norm(3, 1, "ffn")

            def rms2(i, m, norm, shift, dst, signal):
                gain = col(norm, 0, DC)[:, :, None].broadcast_to([P, DC, 2])
                dve.tensor_tensor(norm_gain[:], mod1[:, m, shift + DC:shift + 2 * DC], gain, ALU.mult)
                j, n = job_of[f"rms{i}"], T * len(dst)
                wait_out(dve, j)
                dve.reciprocal(rstd2[:, 0:n], rstd2[:, 0:n])
                dve.drain()
                for k in range(len(dst)):
                    dve.tensor_tensor(dst[k], halves[k][:], rstd2[:, None, k * T:(k + 1) * T].broadcast_to([P, DC, T]),
                                      ALU.mult)
                dve.drain()
                for k in range(len(dst)):
                    for c in range(DC):
                        last = dve.tensor_scalar(dst[k][:, c], dst[k][:, c], norm_gain[:, c, k:k + 1],
                                                 mod[:, m, shift + c, k:k + 1], ALU.mult, ALU.add)
                last.then_inc(S(signal), 1)

            def stage_mla():
                dve.drain().then_inc(S("moe_done"), 1)
                for g in range(4):
                    j = job_of["ctxT"] + g
                    wait_full(dve, j)
                    out_of(dve.tensor_copy(ctxT[:, 2 * g:2 * g + 2], bank(j).rearrange("p (a t) -> p a t", a=2)), j)
                dve.drain().then_inc(S("x2_ready"), 1)
                rms2(0, 2, "norm1_w_20", 0, [a2[:, :, 0:T], a2[:, :, T:T2]], "a2_ready")
                for kind, m, c in MLA_SEQ:
                    if kind != "S":
                        continue
                    name, h, n, rows, dst, weight, slots = item_of(m)
                    j = mla_job[kind, m, c]
                    st = nstat[0:rows, m % 2]
                    wait_out(dve, j)
                    dve.reciprocal(st, st).then_inc(S("nrstd_ready"), 1)
                cos, sin = c_("rope_cos")[0:ROPE], c_("rope_sin")[0:ROPE]
                dve.wait_ge(S("item_normed"), len(MLA_ITEMS))
                for i in range(AH + 1):
                    j = job_of["rope"] + i
                    t = kr[0:ROPE, 0, 0:T] if i == 0 else qr[0:ROPE, i - 1, 0:T]
                    a, b = (rope_tmp[0:ROPE, i % 2, k * T:(k + 1) * T] for k in range(2))
                    wait_full(dve, j)
                    dve.tensor_tensor(a, t, cos, ALU.mult)
                    out_of(dve.tensor_tensor(b, bank(j)[0:ROPE, 0:T], sin, ALU.mult), j)
                    dve.drain()
                    dve.tensor_tensor(t, a, b, ALU.add).then_inc(S("rope_ready"), 1)
                dve.drain()
                for kind, h, k in ATTN_SEQ:
                    if kind != "S":
                        continue
                    j = attn_job[kind, h, k]
                    g = 1 if k < 2 else 2
                    mx = smax[:, h % 2, 2 * k:2 * k + g]
                    sm = smax[:, h % 2, 8 + 2 * k:8 + 2 * k + g]
                    wait_full(dve, j)
                    dve.tensor_reduce(mx, bank(j).rearrange("p (g s) -> p g s", g=g), AX.X, ALU.max)
                    dve.drain()
                    dve.tensor_scalar(mx, mx, -ATT_SCALE, None, ALU.mult).then_inc(S("max_ready"), 1)
                    wait_out(dve, j)
                    pr = prob[:, h % 2, k].rearrange("p (g s) -> p g s", g=g)
                    dve.tensor_reduce(sm, pr, AX.X, ALU.add)
                    dve.drain()
                    dve.reciprocal(sm, sm)
                    dve.drain()
                    for a in range(g):
                        last = dve.tensor_scalar(pr[:, a], pr[:, a], sm[:, a:a + 1], None, ALU.mult)
                    last.then_inc(S("prob_ready"), 1)
                residual2(job_of["mla_o"], 2, 16)

            def residual2(j0, m, gate):
                for c in range(DC):
                    j = j0 + c
                    wait_full(dve, j)
                    for k in range(2):
                        last = dve.scalar_tensor_tensor(halves[k][:, c], bank(j)[:, k * T:(k + 1) * T],
                                                        mod[:, m, gate + c, k:k + 1], halves[k][:, c], ALU.mult, ALU.add)
                    out_of(last, j)
                dve.drain().then_inc(S("x2_ready"), 1)

            def stage_ffn2():
                rms2(1, 2, "norm2_w_20", 24, [a2[:, :, 0:T], a2[:, :, T:T2]], "a2_ready")
                j0 = job_of["ffn2"]

                def body(it, i):
                    for n in range(2):
                        j = j0 + 4 * i + 2 + n
                        wait_out(dve, j - 2, it, 12)
                        wait_full(dve, j, it, 12)
                        at = val(2 * i + n, it, 6)
                        out_of(dve.tensor_tensor(hid2[:, bass.ds(at, 1), :], sil2[:, n:n + 1], bank(j)[:, None, :],
                                                 ALU.mult), j)
                repeat(dve, FSTEPS, 3, body)
                for half in range(2):
                    dve.wait_ge(S("ffn2_sum"), half + 1)
                    for n in range(4):
                        c = 4 * half + n
                        for k in range(2):
                            dve.scalar_tensor_tensor(halves[k][:, c], psum[:, NB + n, k * T:(k + 1) * T],
                                                     mod[:, 2, 40 + c, k:k + 1], halves[k][:, c], ALU.mult, ALU.add)
                    dve.drain().then_inc(S("ffn2_out"), 1)
                dve.nop().then_inc(S("x2_ready"), 1)

            def stage_hg():
                rms2(2, 3, "norm1_w_21", 0, [a2[:, :, 0:T], a2[:, :, T:T2]], "a2_ready")
                dve.tensor_tensor(lbs[:, 0], col("lb", 16, 16), col("lb", 0, 16), ALU.subtract
                                  ).then_inc(S("lb_logits_ready"), 1)
                dve.wait_ge(S("lb_ready"), 1)
                dve.tensor_scalar(lbs[:, 1], lbs[:, 0], -1.0, 1.0, ALU.mult, ALU.add)
                dve.drain()
                for d in range(2):
                    for h in range(AH):
                        i = d * AH + h
                        wait_out(dve, job_of["hg_z"] + i)
                        lb, lb1 = lbs[:, 0, i:i + 1], lbs[:, 1, i:i + 1]
                        dve.tensor_scalar(lf[:, d, h], lf[:, d, h], lb1, lb, ALU.mult, ALU.add)
                        dve.tensor_scalar(kf[:, d, h], kf[:, d, h], lb1, None, ALU.mult)
                    dve.drain()
                    dve.tensor_scalar(lf[:, d], lf[:, d], 2.0 ** -64, None, ALU.max).then_inc(S("forget_ready"), 1)
                for d in range(2):
                    dve.wait_ge(S("log_forget_ready"), d + 1)
                    tmp = ework2[:, d]
                    for h in range(AH):
                        src = lf[:, d, h, T:T2] if d else lf[:, d, h, T2 - 1:T - 1:-1]
                        dst = tmp[:, h] if d else tmp[:, h, ::-1]
                        dve.tensor_tensor_scan(dst, c_one(T), src, 0.0, ALU.mult, ALU.add)
                    dve.drain()
                    dve.tensor_tensor(lf[:, d, :, T:T2], tmp, lf[:, d, :, T:T2], ALU.subtract).then_inc(S("ctx_decay_ready"), 1)
                for d in range(2):
                    for h in range(AH):
                        x = lf[:, d, h, T - 1::-1] if d else lf[:, d, h, 0:T]
                        last = dve.tensor_tensor_scan(x, c_one(T), x, 0.0, ALU.mult, ALU.add)
                dve.drain().then_inc(S("lat_sums_ready"), 1)
                for d in range(2):
                    dve.wait_ge(S("ctx_decay_exp"), d + 1)
                    dve.tensor_tensor(kf[:, d, :, T:T2], kf[:, d, :, T:T2], lf[:, d, :, T:T2], ALU.mult
                                      ).then_inc(S("ctx_keys_ready"), 1)
                for i in range(8):
                    j = job_of["hg_wk"] + i
                    wait_full(dve, j)
                    out_of(dve.tensor_copy(wkT[:, 4 * i:4 * i + 4], bank(j).rearrange("p (i s) -> p i s", s=P)), j)
                for i in range(4):
                    j = job_of["hg_state"] + i
                    wait_full(dve, j)
                    m = 4 * i
                    out_of(dve.tensor_copy(state[:, m // AH, m % AH:m % AH + 4, T:T + P],
                                           bank(j).rearrange("p (i s) -> p i s", s=P)), j)
                dve.wait_ge(S("q_decay_exp"), 1)
                for d in range(2):
                    last = dve.tensor_tensor(ework[:, d], ework[:, d], qh[:], ALU.mult)
                last.then_inc(S("q_decayed"), 1)

                def att_out(n):
                    lev, j = n // 4, job_of["hg_level"] + n
                    if n >= 4:
                        dve.wait_ge(S("att_used"), n - 3)
                    wait_full(dve, j)
                    src = bank(j).rearrange("p (i t) -> p i t", t=P)
                    if lev == 0:
                        ins = dve.tensor_copy(atts[n % 4], src)
                    else:
                        mask = c_("levels")[:, (lev - 1) * P:lev * P]
                        ins = dve.tensor_tensor(atts[n % 4], src, mask[:, None, :].broadcast_to([P, 4, P]), ALU.mult)
                    out_of(ins, j)

                for lev, b in enumerate([P] + LEVELS):
                    e = eworks[lev % 2]
                    dve.wait_ge(S("level_exp"), lev + 1)
                    dve.tensor_tensor(e[:, 0], e[:, 0], qh[:], ALU.mult)
                    for half, part in ((0, lo_half), (1, hi_half)):
                        dve.tensor_tensor(part(e[:, 1], b), part(e[:, 1], b), part(kf[:, half, :, 0:T], b), ALU.mult)
                    dve.drain().then_inc(S("level_ready"), 1)
                    if lev >= 1:
                        for i in range(4):
                            att_out(4 * (lev - 1) + i)
                lev = len(LEVELS) + 1
                wait_full(dve, job_of["hg_level"] + 4 * (lev - 2) + 3)
                dve.tensor_tensor(eworks[lev % 2][:, 1], kf[:, 0, :, 0:T], kf[:, 1, :, 0:T], ALU.add
                                  ).then_inc(S("level_ready"), 1)
                for n in range(4 * (lev - 1), 4 * (lev + 1)):
                    att_out(n)
                for i in range(4):
                    wait_out(dve, job_of["hg_norm"] + i)
                    hs = hstat[:, 2 * i:2 * i + 2]
                    o = ework[:, 1, 2 * i:2 * i + 2]
                    dve.reciprocal(hs, hs)
                    dve.drain()
                    dve.scalar_tensor_tensor(o, psum[:, NB + i].rearrange("p (h t) -> p h t", h=2), col("hg_o_norm_w_2"),
                                             hs, ALU.mult, ALU.mult)
                    dve.drain()
                    last = dve.tensor_tensor(o, o, gsil[:, 2 * i:2 * i + 2], ALU.mult)
                last.then_inc(S("hg_o_ready"), 1)
                for i in range(4):
                    j = job_of["hg_o"] + i
                    wait_full(dve, j)
                    for n in range(2):
                        c = 2 * i + n
                        last = dve.scalar_tensor_tensor(xT[:, c], bank(j)[:, n * T:(n + 1) * T], mod[:, 3, 16 + c, 0:1],
                                                        xT[:, c], ALU.mult, ALU.add)
                    out_of(last, j)
                dve.drain().then_inc(S("x2_ready"), 1)

            def stage_ffn3():
                rms2(3, 3, "norm2_w_21", 24, [act_in[:]], "ffn3_in_ready")
                hidden_steps("ffn3", FSTEPS)
                for c in range(DC):
                    last = dve.scalar_tensor_tensor(xT[:, c], psum[:, NB + c // 2, (c % 2) * T:(c % 2 + 1) * T],
                                                    mod[:, 3, 40 + c, 0:1], xT[:, c], ALU.mult, ALU.add)
                last.then_inc(S("x_final"), 1)

            def stage_out():
                for g in range(4):
                    j = job_of["outT"] + g
                    wait_full(dve, j)
                    out_of(dve.tensor_copy(out_tok[:, g // 2, (g % 2) * 512:(g % 2 + 1) * 512], bank(j)), j)
                dve.drain().then_inc(S("out_tok_ready"), 1)

            stage_prep()
            stage_ada0()
            stage_mlstm()
            stage_ffn0()
            stage_s5()
            stage_moe()
            stage_mla()
            stage_ffn2()
            stage_hg()
            stage_ffn3()
            stage_out()

        @block.gpsimd
        def _(pool):
            def bc(v, n):
                return v[:, :, None].broadcast_to([P, v.shape[1], n])

            def step(*a):
                pool.tensor_tensor(*a)
                pool.drain()

            sn, kr, ki, cs = (sv[:, i] for i in (5, 10, 11, 12))
            pool.wait_ge(S("s5_params_ready"), 1)
            pool.wait_ge(S("s5_in"), 9 * 16)
            for i in range(2):
                step(bbar[:, i], bmat[:, i], bc(kr, SH), ALU.mult)
                step(btmp, bmat[:, 1 - i], bc(ki, SH), ALU.mult)
                step(bbar[:, i], bbar[:, i], btmp, ALU.add if i else ALU.subtract)
                last = pool.tensor_tensor(
                    bpad[:, i].rearrange("p c s -> p (c s)").rearrange("p (j g h) -> p j g h", g=2, h=SH),
                    bbar[:, i, :, None, :].broadcast_to([P, NPAIR, 2, SH]),
                    c_("half")[:, None, :, None].broadcast_to([P, NPAIR, 2, SH]), ALU.mult)
            last.then_inc(S("bpad_ready"), 1)
            pool.tensor_copy(rot[:, 0, :, 0], cs)
            pool.tensor_copy(rot[:, 1, :, 0], sn)
            pool.drain()
            n = 1
            while n < SL:
                er, ei = rot[:, 0, :, 0:n], rot[:, 1, :, 0:n]
                fr, fi = (rot[:, i, :, n - 1:n].broadcast_to([P, NPAIR, n]) for i in range(2))
                step(rot[:, 0, :, n:2 * n], er, fr, ALU.mult)
                step(dbl[:, :, 0:n], ei, fi, ALU.mult)
                step(rot[:, 0, :, n:2 * n], rot[:, 0, :, n:2 * n], dbl[:, :, 0:n], ALU.subtract)
                step(rot[:, 1, :, n:2 * n], er, fi, ALU.mult)
                step(dbl[:, :, 0:n], ei, fr, ALU.mult)
                step(rot[:, 1, :, n:2 * n], rot[:, 1, :, n:2 * n], dbl[:, :, 0:n], ALU.add)
                n *= 2
            pool.nop().then_inc(S("rot_ready"), 1)

            def turn_back(c, i):
                p = 4 * c + i
                cos2, sin2 = (rot[:, k, bass.ds(p, 1), :].broadcast_to([P, 2, SL]) for k in range(2))
                z, x, tmp = ([a[:, k].rearrange("p (b t) -> p b t", b=2) for k in range(2)]
                             for a in (zris[i % 2], xri[:, i % 2], xtmp))
                pool.drain()
                pool.wait_ge(S("s5_z_ready"), p + 1)
                pool.tensor_tensor(tmp[0], z[1], sin2, ALU.mult)
                pool.tensor_tensor(tmp[1], z[0], sin2, ALU.mult)
                if not (isinstance(c, int) and i < 2):
                    pool.wait_ge(S("s5_x_used"), p - 1)
                pool.tensor_tensor(x[0], z[0], cos2, ALU.mult)
                pool.tensor_tensor(x[1], z[1], cos2, ALU.mult)
                pool.drain()
                pool.tensor_tensor(x[0], x[0], tmp[0], ALU.subtract)
                pool.tensor_tensor(x[1], x[1], tmp[1], ALU.add).then_inc(S("s5_x_ready"), 1)

            for i in range(4):
                turn_back(0, i)
            with pool.Fori(1, DC) as c:
                for i in range(4):
                    turn_back(c, i)

            for kind, m, c in MLA_SEQ:
                if kind == "S":
                    name, h, n, rows, dst, weight, slots = item_of(m)
                    st = nstat[0:rows, m % 2]
                    pool.wait_ge(S("nrstd_ready"), m + 1)
                    for k in range(n):
                        d = dst[0:rows, k if n > 1 else h]
                        pool.tensor_tensor(d, d, st, ALU.mult)
                    pool.drain()
                    for k in range(n):
                        d = dst[0:rows, k if n > 1 else h]
                        last = pool.tensor_scalar(d, d, col(weight, k)[0:rows], None, ALU.mult)
                    last.then_inc(S("item_normed"), 1)

            for lev, b in enumerate([P] + LEVELS):
                e = eworks[lev % 2]
                if lev == 0:
                    pool.wait_ge(S("q_decayed_used"), 1)
                if lev >= 2:
                    wait_full(pool, job_of["hg_level"] + 4 * (lev - 2) + 3)
                f, g = lf[:, 0, :, 0:T], lf[:, 1, :, 0:T]
                shape = [P, AH, T // (2 * b), b]
                f_ref = lo_half(f, b)[:, :, :, b - 1:b].broadcast_to(shape)
                g_ref = hi_half(g, b)[:, :, :, 0:1].broadcast_to(shape)
                pool.tensor_tensor(hi_half(e[:, 0], b), hi_half(f, b), f_ref, ALU.subtract)
                pool.tensor_tensor(lo_half(e[:, 0], b), lo_half(g, b), g_ref, ALU.subtract)
                pool.tensor_tensor(lo_half(e[:, 1], b), f_ref, lo_half(f, b), ALU.subtract)
                pool.tensor_tensor(hi_half(e[:, 1], b), g_ref, hi_half(g, b), ALU.subtract)
                pool.drain().then_inc(S("level_exponents"), 1)



def kernel(**inputs):
    import concourse.bacc as bacc
    from concourse.bass_utils import run_bass_kernel_spmd

    nc = bacc.Bacc("TRN2", target_bir_lowering=False, num_devices=1)
    arrays, w = {}, {}
    for name, a in inputs.items():
        if name.startswith("df_"):
            continue
        a = np.ascontiguousarray(a)
        arrays[f"in_{name}"] = a
        w[name] = nc.dram_tensor(f"in_{name}", a.shape, mybir.dt.from_np(a.dtype), kind="ExternalInput").ap()
    table, _ = shape_constants()
    arrays["shape_constants"] = table
    const = nc.dram_tensor("shape_constants", table.shape, F32, kind="ExternalInput").ap()
    out = nc.dram_tensor("out", (1, T, D), F32, kind="ExternalOutput").ap()
    build_program(nc, w, const, out)
    r = run_bass_kernel_spmd(nc, [arrays], core_ids=[0])
    return r.results[0]["out"]
```
